# Optimizing a Trainium2 kernel written in Bass

```python
import functools
import jax, jax.numpy as jnp
from jax import lax
import numpy as np

D_MODEL = 1024
BATCH = 1
SEQ = 1024
DEPTH = 1
DEC_BATCH = 8
DEC_SEQ = 4
PAST_LEN = 4096
PAGE_SIZE = 128

N_HEADS = 16
HEAD_DIM = 64
N_KV_HEADS = 4
GROUP = N_HEADS // N_KV_HEADS
WINDOW = 128
ATTN_BLOCK = 128
ROPE_THETA = 10000.0
Q_W = N_HEADS * HEAD_DIM
KV_W = N_KV_HEADS * HEAD_DIM
D_CONV = 1024
CONV_WIDTH = 3
PEER_HEADS = 8
N_KEYS = 128
N_EXPERTS = N_KEYS * N_KEYS
PEER_TOPK = 16
PEER_QDIM = 256
PEER_HALF = PEER_QDIM // 2
PEER_BLOCK = 128
IN_SIZES = (Q_W, KV_W, KV_W, D_CONV, D_CONV, D_CONV, D_MODEL, D_MODEL)
D_IN = Q_W + 2 * KV_W + 3 * D_CONV + 2 * D_MODEL
EPS = 1e-6
NEG = -1e30

kernel_name = 'hybrid_swa_shortconv_peer_adaln_step'

def rms_norm(x, g):
    xf = x.astype(jnp.float32)
    y = xf * lax.rsqrt(jnp.mean(xf * xf, axis=-1, keepdims=True) + EPS)
    return (y * g.astype(jnp.float32)).astype(x.dtype)

def rope(x, pos):
    half = HEAD_DIM // 2
    inv = jnp.power(jnp.float32(ROPE_THETA), -jnp.arange(half, dtype=jnp.float32) / half)
    ang = pos.astype(jnp.float32)[:, None] * inv[None, :]
    cos = jnp.cos(ang)[:, None, :]
    sin = jnp.sin(ang)[:, None, :]
    x1 = x[..., :half].astype(jnp.float32)
    x2 = x[..., half:].astype(jnp.float32)
    return jnp.concatenate([x1 * cos - x2 * sin, x2 * cos + x1 * sin], axis=-1).astype(x.dtype)

def in_projection(h, w_in, q_norm, k_norm, pos):
    z = h @ w_in
    parts = []
    start = 0
    for n in IN_SIZES:
        parts.append(z[..., start:start + n])
        start += n
    q, k, v, b_gate, c_gate, x_conv, g_attn, g_conv = parts
    bsz, s = h.shape[0], h.shape[1]
    q = rope(rms_norm(q.reshape(bsz, s, N_HEADS, HEAD_DIM), q_norm), pos)
    k = rope(rms_norm(k.reshape(bsz, s, N_KV_HEADS, HEAD_DIM), k_norm), pos)
    v = v.reshape(bsz, s, N_KV_HEADS, HEAD_DIM)
    u = c_gate * x_conv
    return q, k, v, u, b_gate, g_attn, g_conv

def sink_attend(q, k, v, valid, sinks):
    s = jnp.einsum('...qkgd,...skd->...kgqs', q, k).astype(jnp.float32) * (HEAD_DIM ** -0.5)
    s = jnp.where(valid, s, jnp.float32(NEG))
    sink = sinks.astype(jnp.float32).reshape(N_KV_HEADS, GROUP)[:, :, None]
    m = jnp.maximum(jnp.max(s, axis=-1), sink)
    p = jnp.exp(s - m[..., None])
    denom = jnp.sum(p, axis=-1) + jnp.exp(sink - m)
    probs = (p / denom[..., None]).astype(v.dtype)
    return jnp.einsum('...kgqs,...skd->...qkgd', probs, v)

def swa_prompt(q, k, v, sinks):
    bsz, s = q.shape[0], q.shape[1]
    nb = s // ATTN_BLOCK
    qb = q.reshape(bsz, nb, ATTN_BLOCK, N_KV_HEADS, GROUP, HEAD_DIM)
    kb = k.reshape(bsz, nb, ATTN_BLOCK, N_KV_HEADS, HEAD_DIM)
    vb = v.reshape(bsz, nb, ATTN_BLOCK, N_KV_HEADS, HEAD_DIM)

    def band(t):
        prev = jnp.concatenate([jnp.zeros_like(t[:, :1]), t[:, :-1]], axis=1)
        return jnp.concatenate([prev, t], axis=2)

    blk = jnp.arange(nb)[:, None]
    qpos = blk * ATTN_BLOCK + jnp.arange(ATTN_BLOCK)[None, :]
    kpos = (blk - 1) * ATTN_BLOCK + jnp.arange(2 * ATTN_BLOCK)[None, :]
    diff = qpos[:, :, None] - kpos[:, None, :]
    valid = (diff >= 0) & (diff <= WINDOW) & (kpos[:, None, :] >= 0)
    o = sink_attend(qb, band(kb), band(vb), valid[:, None, None], sinks)
    return o.reshape(bsz, s, Q_W)

def swa_sample(q, k, v, win_k, win_v, sinks):
    bsz, t = q.shape[0], q.shape[1]
    L = win_k.shape[1]
    ka = jnp.concatenate([win_k, k], axis=1)
    va = jnp.concatenate([win_v, v], axis=1)
    qpos = PAST_LEN + jnp.arange(t)
    kpos = PAST_LEN - L + jnp.arange(L + t)
    diff = qpos[:, None] - kpos[None, :]
    valid = (diff >= 0) & (diff <= WINDOW)
    o = sink_attend(q.reshape(bsz, t, N_KV_HEADS, GROUP, HEAD_DIM), ka, va, valid, sinks)
    return o.reshape(bsz, t, Q_W), ka[:, -L:], va[:, -L:]

def causal_conv(ext, w, t):
    y = ext[:, 0:t] * w[0]
    for j in range(1, CONV_WIDTH):
        y = y + ext[:, j:j + t] * w[j]
    return y

def peer(h, w_pq, sub_keys, u, v):
    lead = h.shape[:-1]
    tok = h.reshape(-1, D_MODEL)
    n = tok.shape[0]
    nb = -(-n // PEER_BLOCK)
    tok = jnp.pad(tok, ((0, nb * PEER_BLOCK - n), (0, 0))).reshape(nb, PEER_BLOCK, D_MODEL)

    def block(tb):
        q = (tb @ w_pq).reshape(PEER_BLOCK, PEER_HEADS, 2, PEER_HALF)
        s = jnp.einsum('thpd,hpkd->thpk', q, sub_keys)
        sv, si = lax.top_k(s, PEER_TOPK)
        cand = (sv[:, :, 0, :, None] + sv[:, :, 1, None, :]).reshape(PEER_BLOCK, PEER_HEADS, PEER_TOPK * PEER_TOPK)
        cs, ci = lax.top_k(cand, PEER_TOPK)
        i1 = jnp.take_along_axis(si[:, :, 0], ci // PEER_TOPK, axis=-1)
        i2 = jnp.take_along_axis(si[:, :, 1], ci % PEER_TOPK, axis=-1)
        e = i1 * N_KEYS + i2
        g = jax.nn.softmax(cs.astype(jnp.float32), axis=-1).astype(tb.dtype)
        ue = jnp.take(u, e, axis=0)
        a = jax.nn.gelu(jnp.einsum('td,thkd->thk', tb, ue))
        ve = jnp.take(v, e, axis=0)
        return jnp.einsum('thk,thkd->td', g * a, ve)

    out = lax.map(block, tok)
    return out.reshape(-1, D_MODEL)[:n].reshape(lead + (D_MODEL,))

def trunk_layer(x, c, pos, win_k, win_v, conv_buf, w_ada, b_ada, norm1, w_in, q_norm, k_norm,
                sinks, conv_w, w_attn_o, w_conv_o, w_out, norm2, w_peer_q, sub_keys, peer_u, peer_v):
    mod = (jax.nn.silu(c) @ w_ada + b_ada)[:, None, :]
    sh1, sc1, gt1, sh2, sc2, gt2 = jnp.split(mod, 6, axis=-1)
    t = x.shape[1]
    h = rms_norm(x, norm1) * (1 + sc1) + sh1
    q, k, v, u, b_gate, g_attn, g_conv = in_projection(h, w_in, q_norm, k_norm, pos)
    if win_k is None:
        attn = swa_prompt(q, k, v, sinks)
        new_k, new_v = k[:, -WINDOW:], v[:, -WINDOW:]
        ext = jnp.pad(u, ((0, 0), (CONV_WIDTH - 1, 0), (0, 0)))
    else:
        attn, new_k, new_v = swa_sample(q, k, v, win_k, win_v, sinks)
        ext = jnp.concatenate([conv_buf, u], axis=1)
    conv_y = causal_conv(ext, conv_w, t)
    new_conv = ext[:, -(CONV_WIDTH - 1):]
    merged = jax.nn.sigmoid(g_attn) * (attn @ w_attn_o) + jax.nn.sigmoid(g_conv) * ((b_gate * conv_y) @ w_conv_o)
    x = x + gt1 * (merged @ w_out)
    h2 = rms_norm(x, norm2) * (1 + sc2) + sh2
    x = x + gt2 * peer(h2, w_peer_q, sub_keys, peer_u, peer_v)
    return x, new_k, new_v, new_conv

def setup_inputs(seed: int = 0) -> dict:
    key = jax.random.key(seed)
    ks = jax.random.split(key, 24)
    f = jnp.float32
    nrm = lambda k, shp, s: jax.random.normal(k, shp, f) * s
    return {
        'x_prompt': nrm(ks[0], (BATCH, SEQ, D_MODEL), 1.0),
        'x_sample': nrm(ks[1], (DEC_BATCH, DEC_SEQ, D_MODEL), 1.0),
        'c_prompt': nrm(ks[2], (BATCH, D_MODEL), 1.0),
        'c_sample': nrm(ks[3], (DEC_BATCH, D_MODEL), 1.0),
        'cache_win_k': nrm(ks[4], (DEPTH, DEC_BATCH, WINDOW, N_KV_HEADS, HEAD_DIM), 1.0),
        'cache_win_v': nrm(ks[5], (DEPTH, DEC_BATCH, WINDOW, N_KV_HEADS, HEAD_DIM), 1.0),
        'state_conv': nrm(ks[6], (DEPTH, DEC_BATCH, CONV_WIDTH - 1, D_CONV), 0.5),
        'w_ada': nrm(ks[7], (DEPTH, D_MODEL, 6 * D_MODEL), 0.5 * D_MODEL ** -0.5),
        'b_ada': nrm(ks[8], (DEPTH, 6 * D_MODEL), 0.01),
        'norm1': 1.0 + nrm(ks[9], (DEPTH, D_MODEL), 0.02),
        'w_in': nrm(ks[10], (DEPTH, D_MODEL, D_IN), D_MODEL ** -0.5),
        'q_norm': 1.0 + nrm(ks[11], (DEPTH, HEAD_DIM), 0.02),
        'k_norm': 1.0 + nrm(ks[12], (DEPTH, HEAD_DIM), 0.02),
        'attn_sinks': nrm(ks[13], (DEPTH, N_HEADS), 0.5),
        'conv_w': nrm(ks[14], (DEPTH, CONV_WIDTH, D_CONV), CONV_WIDTH ** -0.5),
        'w_attn_o': nrm(ks[15], (DEPTH, Q_W, D_MODEL), Q_W ** -0.5),
        'w_conv_o': nrm(ks[16], (DEPTH, D_CONV, D_MODEL), D_CONV ** -0.5),
        'w_out': nrm(ks[17], (DEPTH, D_MODEL, D_MODEL), D_MODEL ** -0.5),
        'norm2': 1.0 + nrm(ks[18], (DEPTH, D_MODEL), 0.02),
        'w_peer_q': nrm(ks[19], (DEPTH, D_MODEL, PEER_HEADS * PEER_QDIM), D_MODEL ** -0.5),
        'peer_sub_keys': nrm(ks[20], (DEPTH, PEER_HEADS, 2, N_KEYS, PEER_HALF), PEER_HALF ** -0.5),
        'peer_u': nrm(ks[21], (DEPTH, N_EXPERTS, D_MODEL), D_MODEL ** -0.5),
        'peer_v': nrm(ks[22], (DEPTH, N_EXPERTS, D_MODEL), PEER_HEADS ** -0.5),
    }

def reference(x_prompt, x_sample, c_prompt, c_sample, cache_win_k, cache_win_v, state_conv,
              w_ada, b_ada, norm1, w_in, q_norm, k_norm, attn_sinks, conv_w, w_attn_o, w_conv_o,
              w_out, norm2, w_peer_q, peer_sub_keys, peer_u, peer_v):
    pos_p = jnp.arange(x_prompt.shape[1])
    pos_s = PAST_LEN + jnp.arange(x_sample.shape[1])
    yp, ys = x_prompt, x_sample
    kp_l, vp_l, cp_l, ks_l, vs_l, cs_l = [], [], [], [], [], []
    for l in range(DEPTH):
        lw = (w_ada[l], b_ada[l], norm1[l], w_in[l], q_norm[l], k_norm[l], attn_sinks[l], conv_w[l],
              w_attn_o[l], w_conv_o[l], w_out[l], norm2[l], w_peer_q[l], peer_sub_keys[l], peer_u[l], peer_v[l])
        yp, kp, vp, cp = trunk_layer(yp, c_prompt, pos_p, None, None, None, *lw)
        ys, kss, vss, css = trunk_layer(ys, c_sample, pos_s, cache_win_k[l], cache_win_v[l], state_conv[l], *lw)
        kp_l.append(kp); vp_l.append(vp); cp_l.append(cp)
        ks_l.append(kss); vs_l.append(vss); cs_l.append(css)
    win_k_prompt = jnp.stack(kp_l)
    win_v_prompt = jnp.stack(vp_l)
    conv_prompt = jnp.stack(cp_l)
    win_k_sample = jnp.stack(ks_l)
    win_v_sample = jnp.stack(vs_l)
    conv_sample = jnp.stack(cs_l)
    return (yp, ys, win_k_prompt, win_v_prompt, conv_prompt, win_k_sample, win_v_sample, conv_sample)


_drawn_inputs = setup_inputs


def setup_inputs(seed=0):
    import zlib

    import numpy as np

    out = dict(_drawn_inputs(seed))
    spreads = {}
    factors = {'b_ada': 3.142, 'q_norm': 8.0, 'k_norm': 3.129, 'attn_sinks': 64.0, 'norm2': 6.605}
    for name, (base, spread) in spreads.items():
        noise = np.random.default_rng([zlib.crc32(name.encode()), seed]).standard_normal(out[name].shape)
        drawn = base * np.exp(spread * noise) if base else spread * noise
        out[name] = __import__('jax').numpy.asarray(drawn.astype(out[name].dtype))
    for name, factor in factors.items():
        out[name] = (out[name] * factor).astype(out[name].dtype)
    return out
```

```python
from contextlib import ExitStack

import numpy as np

import concourse.bass as bass
from concourse import mybir

ALU = mybir.AluOpType
ACT = mybir.ActivationFunctionType
F32 = mybir.dt.float32
U32 = mybir.dt.uint32
AX = mybir.AxisListType.X

P = 128
D = 1024
DK = D // P
SEQ = 1024
DEC_B, DEC_T = 8, 4
NS = DEC_B * DEC_T
T = SEQ + NS
NT = SEQ // P
PAST = 4096
NH, NKV, HD = 16, 4, 64
GRP = NH // NKV
NQK = NH + NKV
WIN = 128
KVW = NKV * HD
QKVW = NH * HD + 2 * KVW
QKW = NQK * HD
CB = T // 3
PH, TOPK, NKEYS, PHALF = 8, 16, 128, 128
NEXP = NKEYS * NKEYS
EPS = 1e-6
SCALE = HD ** -0.5
NEG = -1e30
GELU_A, GELU_B = 0.7978845608028654, 0.044715
NMOD = 12
RING = 8
BATCH = 4
SLOTS = PH * TOPK


def hold(eng, sem, value):
    eng.wait_ge(sem, value)
    if not isinstance(value, int):
        eng.nop(nofuse=True)


class Steps:

    def __init__(self, eng, sem, base=0, own=False):
        self.eng, self.sem, self.base, self.n, self.own = eng, sem, base, 0, own

    def did(self, ins):
        self.n += 1
        return ins.then_inc(self.sem, 1)

    def wait(self):
        if self.own:
            hold(self.eng, self.sem, self.base + self.n)
        else:
            self.eng.wait_ge(self.sem, self.base + self.n)


def over(eng, first, last, body):
    if last - first == 1:
        body(first)
    else:
        with eng.Fori(first, last) as i:
            body(i)


def bc(ap, shape):
    return ap.to_broadcast(shape)


def tile_cols(i):
    return bass.ds(i * P, P) if not isinstance(i, int) else slice(i * P, i * P + P)


def tile_rows(i, rows):
    if isinstance(i, int):
        return slice(i * P, i * P + rows)
    return bass.ds(i * P, rows)


class Memory:

    def __init__(self, nc, ctx):
        self.nc, self.ctx = nc, ctx

    def sb(self, name, shape, dt=F32):
        return self.ctx.enter_context(self.nc.sbuf_tensor(name, shape, dt))

    def ps(self, name, shape):
        return self.ctx.enter_context(self.nc.psum_tensor(name, shape, F32))

    def sem(self, name):
        return self.ctx.enter_context(self.nc.semaphore(name))


def mods_stage(nc, d, w_qkv, qkv_loaded, hT, attnT):
    with ExitStack() as ctx:
        m = Memory(nc, ctx)
        NR = 1 + DEC_B
        cT = m.sb("cT", [P, DK, NR])
        cth = m.sb("cth", [P, DK, NR])
        csil = m.sb("csil", [P, DK, NR])
        early, late = hT[:].rearrange("p k n -> p (k n)"), attnT[:].rearrange("p k n -> p (k n)")
        w = [early[:, b * DK * 512:(b + 1) * DK * 512].rearrange("p (k n) -> p k n", k=DK) for b in range(2)]
        bias = m.sb("bias", [NR, NMOD * 512])
        mod = late[0:NR, 0:NMOD * 512]
        norms = late[0:NR, NMOD * 512:NMOD * 512 + 2 * D].rearrange("p (a n) -> p a n", a=2)
        acc = [m.ps(f"acc{b}", [P, 512]) for b in range(2)]
        c_loaded, rows_loaded, c_tanh, silu_ready = m.sem("c_loaded"), m.sem("rows_loaded"), m.sem("c_tanh"), m.sem("silu_ready")
        w_loaded = [m.sem(f"w_ada_loaded{b}") for b in range(2)]
        acc_ready, acc_free, mods_ready, mods_stored = m.sem("acc_ready"), m.sem("acc_free"), m.sem("mods_ready"), m.sem("mods_stored")
        silu_step = m.sem("silu_step")
        block = ctx.enter_context(nc.Block())

        @block.sync
        def _(sp):
            sp.dma_start(cT[:], d["cT"]).then_inc(c_loaded, 16)
            for n in range(2):
                sp.dma_start(w[n], d["w_ada"][n]).then_inc(w_loaded[n], 16)
            sp.dma_start(bias[:], d["b_ada"].partition_broadcast(NR)).then_inc(rows_loaded, 16)
            sp.dma_start(norms, d["norms"].partition_broadcast(NR)).then_inc(rows_loaded, 16)
            with sp.Fori(1, NMOD // 2) as i:
                for b in range(2):
                    sp.wait_ge(acc_ready, 2 * i + b - 1)
                    sp.dma_start(w[b], d["w_ada"][2 * i + b]).then_inc(w_loaded[b], 16)
            sp.dma_start(w_qkv[:], d["w_qkv"]).then_inc(qkv_loaded, 16)
            sp.wait_ge(mods_ready, 2)
            sp.dma_start(d["modrows"], mod).then_inc(mods_stored, 16)
            sp.wait_ge(mods_stored, 16)

        @block.scalar
        def _(act):
            act.wait_ge(c_loaded, 16)
            nc.scalar.activation(cth[:], cT[:], ACT.Tanh, scale=0.5).then_inc(c_tanh, 1)

        @block.vector
        def _(dve):
            dve.wait_ge(c_tanh, 1)
            nc.vector.scalar_tensor_tensor(csil[:], cth[:], 1.0, cT[:], ALU.add, ALU.mult).then_inc(silu_step, 1)
            dve.wait_ge(silu_step, 1)
            nc.vector.tensor_scalar(csil[:], csil[:], 0.5, None, ALU.mult).then_inc(silu_ready, 1)
            dve.wait_ge(rows_loaded, 32)
            with dve.Fori(0, NMOD // 2) as i:
                for b in range(2):
                    dve.wait_ge(acc_ready, 2 * i + b + 1)
                    cols = bass.ds((2 * i + b) * 512, 512)
                    nc.vector.tensor_tensor(mod[:, cols], acc[b][0:NR, :], bias[:, cols], ALU.add).then_inc(acc_free, 1)
            dve.wait_ge(acc_free, NMOD)
            for s, first in ((0, D), (1, 4 * D)):
                part = mod[:, first:first + D]
                nc.vector.scalar_tensor_tensor(part, part, 1.0, norms[:, s, :], ALU.add, ALU.mult).then_inc(mods_ready, 1)

        @block.tensor
        def _(pe):
            pe.wait_ge(silu_ready, 1)

            def chunk_pair(i):
                for b in range(2):
                    pe.wait_ge(w_loaded[b], 16 * (i + 1))
                    if not isinstance(i, int):
                        pe.wait_ge(acc_free, 2 * i + b - 1)
                    for k in range(DK):
                        mm = nc.tensor.matmul(acc[b][0:NR, :], csil[:, k, :], w[b][:, k, :], start=(k == 0), stop=(k == DK - 1))
                    mm.then_inc(acc_ready, 1)

            chunk_pair(0)
            with pe.Fori(1, NMOD // 2) as i:
                chunk_pair(i)


def qkv_attn_stage(nc, d, ident, w_qkv, qkv_loaded, hT, attnT, qk_s, v_s):
    with ExitStack() as ctx:
        m = Memory(nc, ctx)
        x = m.sb("x", [P, D])
        h = m.sb("h", [P, D])
        hTc = m.sb("hTc", [P, DK, P])
        g1 = m.sb("g1", [P, D])
        sh1 = m.sb("sh1", [P, D])
        gain = m.sb("gain", [P, QKW])
        cos = m.sb("cos", [P, HD])
        sin = m.sb("sin", [P, HD])
        mask = m.sb("mask", [P, 2, 2 * P])
        sinks = m.sb("sinks", [P, NH])
        half = m.sb("neg_half", [P, NQK])
        ss = m.sb("ss", [P, 1])
        rs = m.sb("rs", [P, 1])
        qkv = m.sb("qkv", [P, QKVW])
        sq = m.sb("sq", [P, QKW])
        rot = m.sb("rot", [P, QKW])
        qk = m.sb("qk", [P, QKW])
        ssh = m.sb("ssh", [P, NQK])
        rsh = m.sb("rsh", [P, NQK])
        qT = m.sb("qT", [HD, NH, P])
        kband = m.sb("kband", [HD, NKV, 2, P])
        vband = m.sb("vband", [P, 2, KVW])
        S = [m.sb(f"S{b}", [P, GRP, 2 * P]) for b in range(2)]
        PT = m.sb("PT", [P, GRP, 2, P])
        mx = m.sb("mx", [P, NH])
        nm = m.sb("nm", [P, NH])
        ds_ = m.sb("sink_minus_max", [P, NH])
        es = m.sb("exp_sink", [P, NH])
        rsum = m.sb("rsum", [P, NH])
        den = m.sb("den", [P, NH])
        rden = m.sb("rden", [P, NH])
        attn = m.sb("attn", [P, D])
        psT = m.ps("psT", [P, 8, P])
        psQ = [m.ps(f"psQ{b}", [P, 512]) for b in range(2)]
        psS = m.ps("psS", [P, GRP, 2 * P])
        psO = m.ps("psO", [P, NH, HD])

        s = m.sem
        rows_loaded, rope_loaded, x_loaded = s("bc_rows_loaded"), s("rope_loaded"), s("x_loaded")
        consts = s("consts_set")
        x_squared, rms_step, rms_ready, h_step, h_ready = s("x_squared"), s("rms_step"), s("rms_ready"), s("h_step"), s("h_ready")
        psT_full, psT_free = s("psT_full"), s("psT_free")
        hT_copied = s("hT_copied")
        qkv_mult, qkv_moved = s("qkv_mult"), s("qkv_moved")
        qk_squared, qk_summed, head_rms_step, head_rms = s("qk_squared"), s("qk_summed"), s("head_rms_step"), s("head_rms")
        rope_step, roped, v_placed, band_shifted = s("rope_step"), s("roped"), s("v_placed"), s("band_shifted")
        scores, scores_moved, soft_step, max_ready, exps = s("scores"), s("scores_moved"), s("soft_step"), s("max_ready"), s("exps")
        pv_done, attn_ready, den_ready = s("pv_done"), s("attn_ready"), s("den_ready")
        kv_stored = s("kv_stored")

        UT = 9

        def use_h(i):
            return 1 if isinstance(i, int) and i == 0 else 1 + UT * (i - 1) + 4

        block = ctx.enter_context(nc.Block())

        def xrows(i, rows):
            return d["x"][tile_rows(i, rows), :]

        @block.sync
        def _(sp):
            sp.dma_start(g1[:], d["modrows"][0:1, D:2 * D].partition_broadcast(P).rearrange("p a n -> p (a n)")).then_inc(rows_loaded, 16)
            sp.dma_start(sh1[:], d["modrows"][0:1, 0:D].partition_broadcast(P).rearrange("p a n -> p (a n)")).then_inc(rows_loaded, 16)
            sp.dma_start(gain[:], d["gain"].partition_broadcast(P)).then_inc(rows_loaded, 16)
            sp.dma_start(sinks[:], d["sinks"].partition_broadcast(P)).then_inc(rows_loaded, 16)
            sp.dma_start(mask[:], d["mask"]).then_inc(rows_loaded, 16)

            def load(i, rows):
                if not isinstance(i, int) or i:
                    sp.wait_ge(h_ready, i)
                sp.dma_start(x[0:rows, :], xrows(i, rows)).then_inc(x_loaded, 16)
                if not isinstance(i, int) or i:
                    sp.wait_ge(roped, i)
                sp.dma_start(cos[0:rows, :], d["cos"][tile_rows(i, rows), :]).then_inc(rope_loaded, 16)
                sp.dma_start(sin[0:rows, :], d["sin"][tile_rows(i, rows), :]).then_inc(rope_loaded, 16)

            load(0, P)
            with sp.Fori(1, NT) as i:
                load(i, P)
            sp.wait_ge(h_ready, NT)
            for dst, col in ((g1, D), (sh1, 0)):
                for b in range(DEC_B):
                    sp.dma_start(dst[b * DEC_T:(b + 1) * DEC_T, :],
                                 d["modrows"][1 + b:2 + b, col:col + D].partition_broadcast(DEC_T).rearrange("p a n -> p (a n)")
                                 ).then_inc(rows_loaded, 16)
            load(NT, NS)
            sp.wait_ge(roped, NT)
            sp.wait_ge(v_placed, NT)
            sp.dma_start(d["win_k_p"], qk[:, NH * HD:QKW]).then_inc(kv_stored, 16)
            sp.dma_start(d["win_v_p"], vband[:, 1, :]).then_inc(kv_stored, 16)
            sp.wait_ge(kv_stored, 32)

        @block.scalar
        def _(act):
            act.wait_ge(consts, 3)

            def square_x(i, rows):
                act.wait_ge(x_loaded, 16 * (i + 1))
                if not isinstance(i, int) or i:
                    act.wait_ge(psT_full, use_h(i - 1))
                nc.scalar.activation(h[0:rows, :], x[0:rows, :], ACT.Square, accum_out=ss[0:rows, :]).then_inc(x_squared, 1)

            def move_T(dst, src, use):
                act.wait_ge(psT_full, use)
                nc.scalar.activation(dst, src, ACT.Copy).then_inc(psT_free, 1)

            def move_qkv(i, c, rows):
                act.wait_ge(qkv_mult, 3 * i + c + 1)
                if c == 0 and (not isinstance(i, int) or i):
                    act.wait_ge(roped, i)
                    act.wait_ge(v_placed, i)
                nc.scalar.activation(qkv[0:rows, c * 512:(c + 1) * 512], psQ[(c) % 2][0:rows, :], ACT.Copy).then_inc(qkv_moved, 1)

            def square_qk(i, rows):
                act.wait_ge(qkv_moved, 3 * (i + 1))
                nc.scalar.activation(sq[0:rows, :], qkv[0:rows, 0:QKW], ACT.Square).then_inc(qk_squared, 1)

            def exp_group(i, g):
                act.wait_ge(max_ready, NKV * i + g + 1)
                for j in range(GRP):
                    hd = g * GRP + j
                    nc.scalar.activation(S[g % 2][:, j, :], S[g % 2][:, j, :], ACT.Exp, bias=nm[:, hd:hd + 1],
                                         accum_out=rsum[:, hd:hd + 1]).then_inc(exps, 1)
                nc.scalar.activation(es[:, g * GRP:(g + 1) * GRP], ds_[:, g * GRP:(g + 1) * GRP], ACT.Exp).then_inc(exps, 1)

            def step(i, rows):
                u = 1 + UT * i
                square_x(i + 1, rows)
                if not isinstance(i, int) or i:
                    act.wait_ge(scores, NKV * i)
                move_T(qT[:, 0:8, :], psT[0:HD, :, :], u + 1)
                move_T(qT[:, 8:16, :], psT[0:HD, :, :], u + 2)
                if not isinstance(i, int) or i:
                    act.wait_ge(band_shifted, 2 * i)
                move_T(kband[:, :, 1, :], psT[0:HD, 0:NKV, :], u + 3)
                act.wait_ge(qkv_mult, 3 * (i + 1))
                act.wait_ge(hT_copied, i + 1)
                move_T(hTc[:, :, 0:rows], psT[:, :, 0:rows], u + 4)
                for g in range(NKV):
                    exp_group(i, g)
                    if g or not isinstance(i, int) or i:
                        act.wait_ge(pv_done, NKV * i + g)
                    move_T(PT[:], psT[:, :, :].rearrange("p (j b) q -> p j b q", b=2), u + 5 + g)
                    if g < 3:
                        move_qkv(i + 1, g, rows)
                move_T(attnT[:, :, tile_cols(i)], psT[:, :, :], u + 9)
                square_qk(i + 1, rows)

            square_x(0, P)
            move_T(hTc[:, :, :], psT[:, :, :], 1)
            for c in range(3):
                move_qkv(0, c, P)
            square_qk(0, P)
            step(0, P)
            with act.Fori(1, NT - 1) as i:
                step(i, P)
            step(NT - 1, NS)

        @block.gpsimd
        def _(pool):
            nc.gpsimd.memset(half[:], -0.5).then_inc(consts, 1)
            nc.gpsimd.memset(kband[:], 0.0).then_inc(consts, 1)
            nc.gpsimd.memset(vband[:], 0.0).then_inc(consts, 1)
            hold(pool, consts, 3)

            def rms(i, rows):
                hold(pool, x_squared, i + 1)
                if not isinstance(i, int) or i:
                    hold(pool, h_ready, i)
                nc.gpsimd.tensor_scalar(rs[0:rows, :], ss[0:rows, :], 1.0 / D, EPS, ALU.mult, ALU.add).then_inc(rms_step, 1)
                hold(pool, rms_step, i + 1)
                nc.gpsimd.tensor_tensor(rs[0:rows, :], rs[0:rows, :], half[0:rows, 0:1], ALU.pow).then_inc(rms_ready, 1)

            def copy_hT(i, rows):
                hold(pool, psT_free, use_h(i))
                cols = slice(SEQ, T) if rows == NS else tile_cols(i)
                nc.gpsimd.tensor_copy(hT[:, :, cols], hTc[:, :, 0:rows]).then_inc(hT_copied, 1)

            def head_rms_of(i, rows):
                hold(pool, qk_summed, i + 1)
                if not isinstance(i, int) or i:
                    hold(pool, roped, i)
                nc.gpsimd.tensor_scalar(rsh[0:rows, :], ssh[0:rows, :], 1.0 / HD, EPS, ALU.mult, ALU.add).then_inc(head_rms_step, 1)
                hold(pool, head_rms_step, i + 1)
                nc.gpsimd.tensor_tensor(rsh[0:rows, :], rsh[0:rows, :], half[0:rows, :], ALU.pow).then_inc(head_rms, 1)

            def place_v(i):
                hold(pool, qkv_moved, 3 * (i + 1))
                nc.gpsimd.tensor_copy(vband[:, 1, :], qkv[:, QKW:QKVW]).then_inc(v_placed, 1)

            def shift_band(i):
                hold(pool, scores, NKV * (i + 1))
                nc.gpsimd.tensor_copy(kband[:, :, 0, :], kband[:, :, 1, :]).then_inc(band_shifted, 1)
                hold(pool, pv_done, NKV * (i + 1))
                nc.gpsimd.tensor_copy(vband[:, 0, :], vband[:, 1, :]).then_inc(band_shifted, 1)
                hold(pool, band_shifted, 2 * (i + 1))

            rms(0, P)
            copy_hT(0, P)
            place_v(0)
            head_rms_of(0, P)

            def step(i, rows):
                rms(i + 1, rows)
                copy_hT(i + 1, rows)
                shift_band(i)
                if rows == P:
                    place_v(i + 1)
                head_rms_of(i + 1, rows)

            step(0, P)
            with pool.Fori(1, NT - 1) as i:
                step(i, P)
            step(NT - 1, NS)
            hold(pool, qkv_moved, 3 * (NT + 1))
            nc.gpsimd.tensor_copy(v_s[:], qkv[0:NS, QKW:QKVW]).then_inc(v_placed, 1)

        @block.vector
        def _(dve):
            dve.wait_ge(rows_loaded, 80)
            dve.wait_ge(consts, 3)

            def make_h(i, rows):
                dve.wait_ge(rms_ready, i + 1)
                nc.vector.scalar_tensor_tensor(h[0:rows, :], x[0:rows, :], rs[0:rows, :], g1[0:rows, :], ALU.mult, ALU.mult).then_inc(h_step, 1)
                dve.wait_ge(h_step, i + 1)
                nc.vector.tensor_tensor(h[0:rows, :], h[0:rows, :], sh1[0:rows, :], ALU.add).then_inc(h_ready, 1)

            def rope(i, rows, out):
                st = Steps(dve, rope_step, base=5 * i)
                r = slice(0, rows)
                heads = lambda t: t[r, 0:QKW].rearrange("p (n e) -> p n e", e=HD)
                dve.wait_ge(qk_squared, i + 1)
                if not isinstance(i, int) or i:
                    dve.wait_ge(head_rms, i)
                nc.vector.tensor_reduce(ssh[r, :], heads(sq), AX, ALU.add).then_inc(qk_summed, 1)
                dve.wait_ge(head_rms, i + 1)
                dve.wait_ge(qk_summed, i + 1)
                st.did(nc.vector.tensor_tensor(heads(sq), heads(qkv), bc(rsh[r, :].unsqueeze(2), [rows, NQK, HD]), ALU.mult))
                st.wait()
                st.did(nc.vector.tensor_tensor(sq[r, :], sq[r, :], gain[r, :], ALU.mult))
                st.wait()
                dve.wait_ge(rope_loaded, 32 * (i + 1))
                tab = lambda t: bc(t.unsqueeze(1), [rows, NQK, t.shape[1]])
                H2 = HD // 2
                st.did(nc.vector.tensor_tensor(heads(rot)[:, :, 0:H2], heads(sq)[:, :, H2:HD], tab(sin[r, 0:H2]), ALU.mult))
                st.did(nc.vector.tensor_tensor(heads(rot)[:, :, H2:HD], heads(sq)[:, :, 0:H2], tab(sin[r, H2:HD]), ALU.mult))
                st.wait()
                st.did(nc.vector.tensor_tensor(heads(sq), heads(sq), tab(cos[r, :]), ALU.mult))
                st.wait()
                if not isinstance(i, int) or i:
                    dve.wait_ge(psT_full, 1 + UT * (i - 1) + 3)
                nc.vector.tensor_tensor(out[r, :], sq[r, :], rot[r, :], ALU.add).then_inc(roped, 1)

            def soft_group(i, g):
                st = Steps(dve, soft_step, base=(NKV * i + g) * 3)
                hs = slice(g * GRP, (g + 1) * GRP)
                which = 0 if isinstance(i, int) and i == 0 else 1
                dve.wait_ge(scores, NKV * i + g + 1)
                if g >= 2 or not isinstance(i, int) or i:
                    dve.wait_ge(psT_full, 1 + UT * i + 4 + (g - 1) if g >= 2 else 1 + UT * (i - 1) + 4 + 3 + g)
                nc.vector.scalar_tensor_tensor(S[g % 2][:], psS[:], SCALE, bc(mask[:, which, :].unsqueeze(1), [P, GRP, 2 * P]),
                                               ALU.mult, ALU.add).then_inc(scores_moved, 1)
                dve.wait_ge(scores_moved, NKV * i + g + 1)
                if g == 0 and (not isinstance(i, int) or i):
                    dve.wait_ge(attn_ready, i)
                st.did(nc.vector.tensor_reduce(mx[:, hs], S[g % 2][:], AX, ALU.max))
                st.wait()
                st.did(nc.vector.tensor_tensor(mx[:, hs], mx[:, hs], sinks[:, hs], ALU.max))
                st.wait()
                st.did(nc.vector.tensor_scalar(nm[:, hs], mx[:, hs], -1.0, None, ALU.mult))
                st.wait()
                nc.vector.tensor_tensor(ds_[:, hs], sinks[:, hs], mx[:, hs], ALU.subtract).then_inc(max_ready, 1)

            def normalise(i):
                dve.wait_ge(exps, NKV * (GRP + 1) * (i + 1))
                nc.vector.tensor_tensor(den[:], rsum[:], es[:], ALU.add).then_inc(den_ready, 1)
                dve.wait_ge(den_ready, 2 * i + 1)
                nc.vector.reciprocal(rden[:], den[:]).then_inc(den_ready, 1)
                dve.wait_ge(den_ready, 2 * i + 2)
                dve.wait_ge(pv_done, NKV * (i + 1))
                nc.vector.tensor_tensor(attn[:, :].rearrange("p (n e) -> p n e", e=HD), psO[:],
                                        bc(rden[:].unsqueeze(2), [P, NH, HD]), ALU.mult).then_inc(attn_ready, 1)

            make_h(0, P)
            rope(0, P, qk)

            def step(i, rows):
                if rows == NS:
                    dve.wait_ge(rows_loaded, 80 + 32 * DEC_B)
                make_h(i + 1, rows)
                for g in range(NKV):
                    soft_group(i, g)
                normalise(i)
                rope(i + 1, rows, qk if rows == P else qk_s)

            step(0, P)
            with dve.Fori(1, NT - 1) as i:
                step(i, P)
            step(NT - 1, NS)

        @block.tensor
        def _(pe):
            pe.wait_ge(d["ident_loaded"], 16)
            pe.wait_ge(qkv_loaded, 16)
            pe.wait_ge(consts, 3)

            def turn(srcs, use, width=P, rows=P):
                if not (isinstance(use, int) and use == 1):
                    hold(pe, psT_free, use - 1)
                for j, src in enumerate(srcs):
                    mm = nc.tensor.transpose(psT[0:width, j, 0:rows], src, ident[0:rows, 0:rows])
                mm.then_inc(psT_full, 1)

            def turn_h(i, rows, use):
                pe.wait_ge(h_ready, i + 1)
                turn([h[0:rows, k * P:(k + 1) * P] for k in range(DK)], use, P, rows)

            def project(i, c, rows):
                n = 3 * i + c
                pe.wait_ge(psT_free, use_h(i))
                if c == 0 and (not isinstance(i, int) or i):
                    pe.wait_ge(qkv_moved, 3 * i)
                if c == 2:
                    pe.wait_ge(qkv_moved, n - 1)
                for k in range(DK):
                    mm = nc.tensor.matmul(psQ[c % 2][0:rows, :], hTc[:, k, 0:rows], w_qkv[:, k, c * 512:(c + 1) * 512],
                                          start=(k == 0), stop=(k == DK - 1))
                mm.then_inc(qkv_mult, 1)

            def score(i, g):
                if g or not isinstance(i, int) or i:
                    pe.wait_ge(scores_moved, NKV * i + g)
                pe.wait_ge(psT_free, 1 + UT * i + 3)
                for j in range(GRP):
                    mm = nc.tensor.matmul(psS[:, j, :], qT[:, g * GRP + j, :], kband[:, g, :, :].rearrange("p b n -> p (b n)"), start=True, stop=True)
                mm.then_inc(scores, 1)

            def turn_probs(i, g):
                pe.wait_ge(exps, (GRP + 1) * (NKV * i + g + 1))
                turn([S[g % 2][:, j, b * P:(b + 1) * P] for j in range(GRP) for b in range(2)], 1 + UT * i + 5 + g)

            def weigh(i, g):
                pe.wait_ge(psT_free, 1 + UT * i + 5 + g)
                pe.wait_ge(v_placed, i + 1)
                if not isinstance(i, int) or i:
                    pe.wait_ge(attn_ready, i)
                    pe.wait_ge(band_shifted, 2 * i)
                for j in range(GRP):
                    for b in range(2):
                        mm = nc.tensor.matmul(psO[:, g * GRP + j, :], PT[:, j, b, :], vband[:, b, g * HD:(g + 1) * HD],
                                              start=(b == 0), stop=(b == 1))
                mm.then_inc(pv_done, 1)

            turn_h(0, P, 1)
            for c in range(3):
                project(0, c, P)

            def step(i, rows):
                u = 1 + UT * i
                pe.wait_ge(roped, i + 1)
                turn([qk[:, n * HD:(n + 1) * HD] for n in range(0, 8)], u + 1, HD)
                turn([qk[:, n * HD:(n + 1) * HD] for n in range(8, 16)], u + 2, HD)
                turn([qk[:, n * HD:(n + 1) * HD] for n in range(16, 20)], u + 3, HD)
                turn_h(i + 1, rows, u + 4)
                score(i, 0)
                project(i + 1, 0, rows)
                for g in range(NKV):
                    turn_probs(i, g)
                    if g < 3:
                        score(i, g + 1)
                    weigh(i, g)
                    if g < 2:
                        project(i + 1, g + 1, rows)
                pe.wait_ge(attn_ready, i + 1)
                turn([attn[:, k * P:(k + 1) * P] for k in range(DK)], u + 9)

            step(0, P)
            with pe.Fori(1, NT - 1) as i:
                step(i, P)
            step(NT - 1, NS)


def sample_stage(nc, d, ident, qk_s, v_s, attnT):
    R = GRP * DEC_T
    KN = WIN + DEC_T
    with ExitStack() as ctx:
        m = Memory(nc, ctx)
        kc = m.sb("k_cache", [P, DEC_B, KVW])
        vc = m.sb("v_cache", [P, DEC_B, KVW])
        vn = m.sb("v_new", [DEC_T, DEC_B, KVW])
        mask = m.sb("mask_s", [R, KN])
        sinks = m.sb("sinks_s", [R, NKV])
        qT = m.sb("qT_s", [HD, DEC_B, NKV, GRP, DEC_T])
        kn = m.sb("k_new_T", [HD, NKV, NS])
        kT = [m.sb(f"k_cache_T{b}", [HD, NKV, WIN]) for b in range(2)]
        S = m.sb("S_s", [R, DEC_B, NKV, KN])
        mx, ds_, es, den, rden = (m.sb(n, [R, DEC_B, NKV]) for n in ("mx_s", "ds_s", "es_s", "den_s", "rden_s"))
        PT = [m.sb(f"PT_s{b}", [P, NKV, R]) for b in range(2)]
        PN = [m.sb(f"PN_s{b}", [DEC_T, NKV, R]) for b in range(2)]
        psA = m.ps("psA", [P, NH, NS])
        psK = m.ps("psK", [P, NKV, WIN])
        psS = m.ps("psS_s", [P, NKV, 256])
        psP = m.ps("psP", [P, NKV, R])
        psN = m.ps("psN", [P, NKV, R])
        psO = m.ps("psO_s", [P, NKV, R])
        s = m.sem
        new_stored, cache_loaded, v_new_loaded = s("new_stored"), s("cache_loaded"), s("v_new_loaded")
        q_turned, q_moved, kn_turned = s("q_turned"), s("q_moved"), s("kn_turned")
        k_turned, k_moved, scores, scores_moved = s("k_turned"), s("k_moved"), s("scores_sm"), s("scores_sm_moved")
        soft, shifted, exped, probs = s("soft_s"), s("shifted_s"), s("exped_s"), s("probs_s")
        p_turned, p_moved, weighed, out_moved = s("p_turned"), s("p_moved"), s("weighed"), s("out_moved")
        block = ctx.enter_context(nc.Block())

        @block.sync
        def _(sp):
            sp.dma_start(kc[:], d["cache_k"].rearrange("b j n -> j b n")).then_inc(cache_loaded, 16)
            sp.dma_start(vc[:], d["cache_v"].rearrange("b j n -> j b n")).then_inc(cache_loaded, 16)
            sp.dma_start(mask[:], d["mask_s"]).then_inc(cache_loaded, 16)
            sp.dma_start(sinks[:], d["sinks_s"]).then_inc(cache_loaded, 16)
            for b in range(DEC_B):
                rows = slice(b * DEC_T, (b + 1) * DEC_T)
                sp.dma_start(d["win_v_s"][b, WIN - DEC_T:WIN, :], v_s[rows, :]).then_inc(new_stored, 16)
                sp.dma_start(d["win_k_s"][b, WIN - DEC_T:WIN, :], qk_s[rows, NH * HD:QKW]).then_inc(new_stored, 16)
            for out, cache in (("win_v_s", "cache_v"), ("win_k_s", "cache_k")):
                sp.dma_start(d[out][:, 0:WIN - DEC_T, :], d[cache][:, DEC_T:WIN, :]).then_inc(new_stored, 16)
            sp.wait_ge(new_stored, 16 * (2 * DEC_B + 2))
            sp.dma_start(vn[:], d["win_v_s"][:, WIN - DEC_T:WIN, :].rearrange("b t n -> t b n")).then_inc(v_new_loaded, 16)

        @block.scalar
        def _(act):
            act.wait_ge(q_turned, 1)
            for g in range(NKV):
                nc.scalar.activation(qT[:, :, g, :, :].rearrange("p b h t -> p h b t"),
                                     psA[0:HD, g * GRP:(g + 1) * GRP, :].rearrange("p h (b t) -> p h b t", t=DEC_T), ACT.Copy).then_inc(q_moved, 1)
            act.wait_ge(kn_turned, 1)
            nc.scalar.activation(kn[:], psK[0:HD, :, 0:NS], ACT.Copy).then_inc(k_moved, 1)
            for b in range(DEC_B):
                act.wait_ge(k_turned, b + 1)
                if b >= 2:
                    act.wait_ge(scores, b - 1)
                nc.scalar.activation(kT[b % 2][:], psK[0:HD, :, :], ACT.Copy).then_inc(k_moved, 1)
            act.wait_ge(shifted, 2)
            nc.scalar.activation(S[:], S[:], ACT.Exp).then_inc(exped, 1)
            nc.scalar.activation(es[:], ds_[:], ACT.Exp).then_inc(exped, 1)
            for b in range(DEC_B):
                act.wait_ge(p_turned, b + 1)
                if b >= 2:
                    act.wait_ge(weighed, b - 1)
                nc.scalar.activation(PT[b % 2][:], psP[:], ACT.Copy).then_inc(p_moved, 1)
                nc.scalar.activation(PN[b % 2][:], psN[0:DEC_T], ACT.Copy).then_inc(p_moved, 1)

        @block.vector
        def _(dve):
            dve.wait_ge(cache_loaded, 64)
            for b in range(DEC_B):
                dve.wait_ge(scores, b + 1)
                nc.vector.scalar_tensor_tensor(S[:, b], psS[0:R, :, 0:KN], SCALE, bc(mask[:].unsqueeze(1), [R, NKV, KN]), ALU.mult, ALU.add).then_inc(scores_moved, 1)
            dve.wait_ge(scores_moved, DEC_B)
            flat = lambda t: t[:].rearrange("p b g -> p (b g)")
            rows = S[:].rearrange("p b g n -> p (b g) n")
            st = Steps(dve, soft)
            st.did(nc.vector.tensor_reduce(flat(mx), rows, AX, ALU.max))
            st.wait()
            sink = bc(sinks[:].unsqueeze(1), [R, DEC_B, NKV])
            st.did(nc.vector.tensor_tensor(mx[:], mx[:], sink, ALU.max))
            st.wait()
            spread = lambda t: bc(flat(t).unsqueeze(2), [R, DEC_B * NKV, KN])
            nc.vector.tensor_tensor(rows, rows, spread(mx), ALU.subtract).then_inc(shifted, 1)
            nc.vector.tensor_tensor(ds_[:], sink, mx[:], ALU.subtract).then_inc(shifted, 1)
            dve.wait_ge(exped, 2)
            st.did(nc.vector.tensor_reduce(flat(den), rows, AX, ALU.add))
            st.wait()
            st.did(nc.vector.tensor_tensor(den[:], den[:], es[:], ALU.add))
            st.wait()
            st.did(nc.vector.reciprocal(rden[:], den[:]))
            st.wait()
            nc.vector.tensor_tensor(rows, rows, spread(rden), ALU.mult).then_inc(probs, 1)
            for b in range(DEC_B):
                dve.wait_ge(weighed, b + 1)
                for par in range(2):
                    src = psO[0:HD].rearrange("p g (k e t) -> p g k e t", e=2, t=DEC_T)[:, :, :, par, :]
                    dst = attnT[par * HD:(par + 1) * HD, :, SEQ + b * DEC_T:SEQ + (b + 1) * DEC_T].rearrange("p (g k) t -> p g k t", k=GRP // 2)
                    nc.vector.tensor_copy(dst, src).then_inc(out_moved, 1)

        @block.tensor
        def _(pe):
            for n in range(NH):
                mm = nc.tensor.transpose(psA[0:HD, n, :], qk_s[:, n * HD:(n + 1) * HD], ident[0:NS, 0:NS])
            mm.then_inc(q_turned, 1)
            for n in range(NKV):
                mm = nc.tensor.transpose(psK[0:HD, n, 0:NS], qk_s[:, (NH + n) * HD:(NH + n + 1) * HD], ident[0:NS, 0:NS])
            mm.then_inc(kn_turned, 1)
            pe.wait_ge(cache_loaded, 64)
            pe.wait_ge(q_moved, NKV)
            for b in range(DEC_B):
                pe.wait_ge(k_moved, b + 1)
                for g in range(NKV):
                    mm = nc.tensor.transpose(psK[0:HD, g, :], kc[:, b, g * HD:(g + 1) * HD], ident[:, :])
                mm.then_inc(k_turned, 1)
                pe.wait_ge(k_moved, b + 2)
                if b:
                    pe.wait_ge(scores_moved, b)
                for g in range(NKV):
                    q = qT[:, b, g].rearrange("p h t -> p (h t)")
                    nc.tensor.matmul(psS[0:R, g, 0:WIN], q, kT[b % 2][:, g, :], start=True, stop=True)
                    mm = nc.tensor.matmul(psS[0:R, g, WIN:KN], q, kn[:, g, b * DEC_T:(b + 1) * DEC_T], start=True, stop=True)
                mm.then_inc(scores, 1)
            pe.wait_ge(probs, 1)
            pe.wait_ge(v_new_loaded, 16)
            for b in range(DEC_B):
                if b:
                    pe.wait_ge(p_moved, 2 * b)
                for g in range(NKV):
                    nc.tensor.transpose(psP[:, g, :], S[:, b, g, 0:WIN], ident[0:R, 0:R])
                    mm = nc.tensor.transpose(psN[0:DEC_T, g, :], S[:, b, g, WIN:KN], ident[0:R, 0:R])
                mm.then_inc(p_turned, 1)
                pe.wait_ge(p_moved, 2 * b + 2)
                if b:
                    pe.wait_ge(out_moved, 2 * b)
                for g in range(NKV):
                    nc.tensor.matmul(psO[0:HD, g, :], vc[:, b, g * HD:(g + 1) * HD], PT[b % 2][:, g, :], start=True, stop=False)
                    mm = nc.tensor.matmul(psO[0:HD, g, :], vn[:, b, g * HD:(g + 1) * HD], PN[b % 2][:, g, :], start=False, stop=True)
                mm.then_inc(weighed, 1)


def conv_stage(nc, d, hT, yT):
    with ExitStack() as ctx:
        m = Memory(nc, ctx)
        w = [m.sb(f"w_bcx{b}", [P, 3, DK, P]) for b in range(2)]
        csb = [m.sb(f"c_gate{b}", [P, CB]) for b in range(2)]
        u = [m.sb(f"u{b}", [P, 2 + SEQ]) for b in range(2)]
        us = [m.sb(f"u_s{b}", [P, DEC_B, 2 + DEC_T]) for b in range(2)]
        y = m.sb("y", [P, SEQ])
        ys = m.sb("y_s", [P, DEC_B, DEC_T])
        cw = m.sb("conv_w", [P, DK, 3])
        state = m.sb("state", [P, DK, DEC_B, 2])
        new = m.sb("conv_new", [P, DK, 2 + 2 * DEC_B])
        psB = [m.ps(f"psB{j}", [P, 512]) for j in range(3)]
        psC = m.ps("psC", [P, 512])
        psX = [m.ps(f"psX{b}", [P, 512]) for b in range(2)]
        s = m.sem
        w_loaded = [s(f"w_bcx_loaded{b}") for b in range(2)]
        small_loaded, zeroed = s("small_loaded"), s("zeroed")
        c_mult, c_moved, x_mult, u_ready, b_mult = s("c_mult"), s("c_moved"), s("x_mult"), s("u_ready"), s("b_mult")
        conv_step, y_ready, state_placed, tail_saved, tail_stored = s("conv_step"), s("y_ready"), s("state_placed"), s("tail_saved"), s("tail_stored")
        block = ctx.enter_context(nc.Block())
        PAIRS = DK // 2
        TAIL = SEQ - 2 * CB

        @block.sync
        def _(sp):
            for b in range(2):
                sp.dma_start(w[b][:], d["w_bcx"][b]).then_inc(w_loaded[b], 16)
            for dst, name in ((cw, "conv_wT"), (state, "stateT")):
                sp.dma_start(dst[:], d[name]).then_inc(small_loaded, 16)
            with sp.Fori(1, PAIRS) as i:
                for b in range(2):
                    sp.wait_ge(b_mult, 3 * (2 * i + b - 1))
                    sp.dma_start(w[b][:], d["w_bcx"][2 * i + b]).then_inc(w_loaded[b], 16)
            sp.wait_ge(tail_saved, 2 * DK)
            sp.dma_start(d["conv_new"], new[:]).then_inc(tail_stored, 16)
            sp.wait_ge(tail_stored, 16)

        def pairs(eng, body):
            for b in range(2):
                body(b, b, 0)
            with eng.Fori(1, PAIRS) as i:
                for b in range(2):
                    body(2 * i + b, b, i)

        @block.tensor
        def _(pe):
            def chunk(c, b, i):
                pe.wait_ge(w_loaded[b], 16 * (i + 1))
                for j in range(3):
                    cols = slice(j * CB, (j + 1) * CB)
                    n = 3 * c + j
                    for part, ps, sem in ((1, psC, c_mult), (2, psX[(3 * b + j) % 2], x_mult), (0, psB[j], b_mult)):
                        if part == 1 and not (isinstance(n, int) and n == 0):
                            pe.wait_ge(c_moved, n)
                        if part == 2 and not (isinstance(n, int) and n < 2):
                            pe.wait_ge(u_ready, n - 1)
                        if part == 0 and not (isinstance(c, int) and c == 0):
                            pe.wait_ge(y_ready, 4 * c)
                        for k in range(DK):
                            mm = nc.tensor.matmul(ps[:, 0:CB], w[b][:, part, k, :], hT[:, k, cols], start=(k == 0), stop=(k == DK - 1))
                        mm.then_inc(sem, 1)
            pairs(pe, chunk)

        @block.scalar
        def _(act):
            def chunk(c, b, i):
                for j in range(3):
                    n = 3 * c + j
                    act.wait_ge(c_mult, n + 1)
                    if not (isinstance(n, int) and n < 2):
                        act.wait_ge(u_ready, n - 1)
                    nc.scalar.activation(csb[(3 * b + j) % 2][:], psC[:, 0:CB], ACT.Copy).then_inc(c_moved, 1)
            pairs(act, chunk)

        @block.gpsimd
        def _(pool):
            for b in range(2):
                nc.gpsimd.memset(u[b][:, 0:2], 0.0).then_inc(zeroed, 1)
            hold(pool, small_loaded, 32)

            def chunk(c, b, i):
                if not (isinstance(c, int) and c < 2):
                    hold(pool, y_ready, 4 * (c - 1))
                nc.gpsimd.tensor_copy(us[b][:, :, 0:2], state[:, bass.ds(c, 1) if not isinstance(c, int) else slice(c, c + 1), :, :].rearrange("p a b j -> p (a b) j")).then_inc(state_placed, 1)
                hold(pool, u_ready, 3 * (c + 1))
                one = bass.ds(c, 1) if not isinstance(c, int) else slice(c, c + 1)
                nc.gpsimd.tensor_copy(new[:, one, 0:2].rearrange("p a j -> p (a j)"), u[b][:, SEQ:SEQ + 2]).then_inc(tail_saved, 1)
                nc.gpsimd.tensor_copy(new[:, one, 2:2 + 2 * DEC_B].rearrange("p a (b j) -> p (a b) j", j=2), us[b][:, :, DEC_T:DEC_T + 2]).then_inc(tail_saved, 1)
            pairs(pool, chunk)

        @block.vector
        def _(dve):
            dve.wait_ge(small_loaded, 32)
            dve.wait_ge(zeroed, 2)

            def chunk(c, b, i):
                first = isinstance(c, int) and c == 0
                st = Steps(dve, conv_step, base=7 * c)
                if not (isinstance(c, int) and c < 2):
                    dve.wait_ge(tail_saved, 2 * (c - 1))
                for j in range(3):
                    n = 3 * c + j
                    dve.wait_ge(c_moved, n + 1)
                    dve.wait_ge(x_mult, n + 1)
                    cg, xp = csb[(3 * b + j) % 2], psX[(3 * b + j) % 2]
                    width = CB if j < 2 else TAIL
                    ins = nc.vector.tensor_tensor(u[b][:, 2 + j * CB:2 + j * CB + width], xp[:, 0:width], cg[:, 0:width], ALU.mult)
                    if j == 2:
                        st.did(ins)
                        ins = nc.vector.tensor_tensor(us[b][:, :, 2:2 + DEC_T], xp[:, TAIL:CB].rearrange("p (b t) -> p b t", t=DEC_T),
                                                      cg[:, TAIL:CB].rearrange("p (b t) -> p b t", t=DEC_T), ALU.mult)
                    ins.then_inc(u_ready, 1)
                dve.wait_ge(u_ready, 3 * (c + 1))
                st.wait()
                dve.wait_ge(state_placed, c + 1)
                if not first:
                    dve.wait_ge(y_ready, 4 * c)
                one = bass.ds(c, 1) if not isinstance(c, int) else slice(c, c + 1)
                tap = lambda j: cw[:, one, j:j + 1].rearrange("p a j -> p (a j)")
                for o, ext, width in ((y[:], lambda j: u[b][:, j:j + SEQ], 0), (ys[:], lambda j: us[b][:, :, j:j + DEC_T], 0)):
                    st.did(nc.vector.tensor_scalar(o, ext(0), tap(0), None, ALU.mult))
                    for j in (1, 2):
                        st.wait()
                        st.did(nc.vector.scalar_tensor_tensor(o, ext(j), tap(j), o, ALU.mult, ALU.add))
                st.wait()
                dve.wait_ge(b_mult, 3 * (c + 1))
                for j in range(3):
                    width = CB if j < 2 else TAIL
                    nc.vector.tensor_tensor(yT[:, one, j * CB:j * CB + width].rearrange("p a n -> p (a n)"), y[:, j * CB:j * CB + width], psB[j][:, 0:width], ALU.mult).then_inc(y_ready, 1)
                nc.vector.tensor_tensor(yT[:, one, SEQ:T].rearrange("p a n -> p (a n)"), ys[:].rearrange("p b t -> p (b t)"), psB[2][:, TAIL:CB], ALU.mult).then_inc(y_ready, 1)
            pairs(dve, chunk)


def merge_stage(nc, d, hT, attnT, yT):
    with ExitStack() as ctx:
        m = Memory(nc, ctx)
        w = [m.sb(f"w_merge{b}", [P, 4, DK, P]) for b in range(2)]
        th = [[m.sb(f"th{g}{b}", [P, CB]) for b in range(2)] for g in range(2)]
        tmp = m.sb("tmp", [P, CB])
        out = [m.sb(f"merged{b}", [P, T]) for b in range(2)]
        ps = [[m.ps(f"psm{n}{b}", [P, 512]) for b in range(2)] for n in range(4)]
        s = m.sem
        w_loaded = [s(f"w_merge_loaded{b}") for b in range(2)]
        gate_mult, proj_mult, gate_tanh, part_step, merged = s("gate_mult"), s("proj_mult"), s("gate_tanh"), s("part_step"), s("merged")
        stored = [s(f"merged_stored{b}") for b in range(2)]
        block = ctx.enter_context(nc.Block())
        PAIRS = DK // 2

        def pairs(eng, body):
            for b in range(2):
                body(b, b, 0)
            with eng.Fori(1, PAIRS) as i:
                for b in range(2):
                    body(2 * i + b, b, i)

        @block.sync
        def _(sp):
            for b in range(2):
                sp.dma_start(w[b][:], d["w_merge"][b]).then_inc(w_loaded[b], 16)

            def store(c, b):
                sp.wait_ge(merged, 3 * (c + 1))
                one = slice(c, c + 1) if isinstance(c, int) else bass.ds(c, 1)
                sp.dma_start(d["mergedT"][:, one, :].rearrange("p a n -> p (a n)"), out[b][:]).then_inc(stored[b], 16)

            with sp.Fori(0, PAIRS - 1) as i:
                for b in range(2):
                    store(2 * i + b, b)
                    sp.dma_start(w[b][:], d["w_merge"][2 * i + b + 2]).then_inc(w_loaded[b], 16)
            for b in range(2):
                store(DK - 2 + b, b)
            for b in range(2):
                sp.wait_ge(stored[b], 16 * PAIRS)

        @block.tensor
        def _(pe):
            def chunk(c, b, i):
                pe.wait_ge(w_loaded[b], 16 * (i + 1))
                for j in range(3):
                    cols = slice(j * CB, (j + 1) * CB)
                    n = 3 * c + j
                    if not (isinstance(n, int) and n < 2):
                        pe.wait_ge(merged, n - 1)
                    for part, src in ((0, hT), (2, hT), (1, attnT), (3, yT)):
                        for k in range(DK):
                            mm = nc.tensor.matmul(ps[part][(3 * b + j) % 2][:, 0:CB], w[b][:, part, k, :], src[:, k, cols], start=(k == 0), stop=(k == DK - 1))
                        mm.then_inc(gate_mult if src is hT else proj_mult, 1)
            pairs(pe, chunk)

        @block.scalar
        def _(act):
            def chunk(c, b, i):
                for j in range(3):
                    n = 3 * c + j
                    if not (isinstance(n, int) and n < 2):
                        act.wait_ge(merged, n - 1)
                    for g in range(2):
                        act.wait_ge(gate_mult, 2 * n + g + 1)
                        nc.scalar.activation(th[g][(3 * b + j) % 2][:], ps[2 * g][(3 * b + j) % 2][:, 0:CB], ACT.Tanh, scale=0.5).then_inc(gate_tanh, 1)
            pairs(act, chunk)

        @block.vector
        def _(dve):
            def chunk(c, b, i):
                for j in range(3):
                    n = 3 * c + j
                    q = (3 * b + j) % 2
                    st = Steps(dve, part_step, base=2 * n)
                    cols = slice(j * CB, (j + 1) * CB)
                    if not (isinstance(n, int) and n == 0):
                        dve.wait_ge(merged, n)
                    if not (isinstance(c, int) and c < 2):
                        dve.wait_ge(stored[b], 16 * i)
                    dve.wait_ge(gate_tanh, 2 * n + 2)
                    dve.wait_ge(proj_mult, 2 * n + 1)
                    st.did(nc.vector.scalar_tensor_tensor(tmp[:], th[0][q][:], 1.0, ps[1][q][:, 0:CB], ALU.add, ALU.mult))
                    dve.wait_ge(proj_mult, 2 * n + 2)
                    st.did(nc.vector.scalar_tensor_tensor(th[1][q][:], th[1][q][:], 1.0, ps[3][q][:, 0:CB], ALU.add, ALU.mult))
                    st.wait()
                    nc.vector.tensor_tensor(out[b][:, cols], tmp[:], th[1][q][:], ALU.add).then_inc(merged, 1)
            pairs(dve, chunk)


def residual_stage(nc, d, ident):
    with ExitStack() as ctx:
        m = Memory(nc, ctx)
        w = m.sb("w_out", [P, DK, D])
        rows_of = {n: m.sb(n, [P, D]) for n in ("gt1", "g2", "sh2")}
        mT = [m.sb(f"mT{b}", [P, DK, P]) for b in range(2)]
        x = [m.sb(f"xr{b}", [P, D]) for b in range(2)]
        x1 = [m.sb(f"x1{b}", [P, D]) for b in range(2)]
        h2 = [m.sb(f"h2{b}", [P, D]) for b in range(2)]
        h2T = [m.sb(f"h2T{b}", [P, DK, P]) for b in range(2)]
        ss = m.sb("ss2", [P, 1])
        rs = m.sb("rs2", [P, 1])
        half = m.sb("neg_half2", [P, 1])
        psY = [m.ps(f"psY{b}", [P, D]) for b in range(2)]
        psT = m.ps("psT2", [P, DK, P])
        s = m.sem
        w_loaded, rows_loaded = s("w_out_loaded"), s("rows2_loaded")
        in_loaded = [s(f"in_loaded{b}") for b in range(2)]
        half_set, y_mult, x1_step, x1_ready, x1_squared = s("half_set"), s("y_mult"), s("x1_step"), s("x1_ready"), s("x1_squared")
        rms_step, rms, h2_step, h2_ready, turned, h2T_ready = s("rms2_step"), s("rms2"), s("h2_step"), s("h2_ready"), s("turned"), s("h2T_ready")
        out_stored = [s(f"out_stored{b}") for b in range(2)]
        block = ctx.enter_context(nc.Block())

        def tiles(eng, body):
            for b in range(2):
                body(b, b, P, 0)
            with eng.Fori(1, NT // 2) as k:
                for b in range(2):
                    body(2 * k + b, b, P, k)
            body(NT, 0, NS, NT // 2)

        early = lambda i, n: isinstance(i, int) and i < n

        @block.sync
        def _(sp):
            sp.dma_start(w[:], d["w_out"]).then_inc(w_loaded, 16)
            for n, col in (("gt1", 2), ("g2", 4), ("sh2", 3)):
                sp.dma_start(rows_of[n][:], d["modrows"][0:1, col * D:(col + 1) * D].partition_broadcast(P).rearrange("p a n -> p (a n)")).then_inc(rows_loaded, 16)

            def load(i, b, rows):
                if not early(i, 2):
                    sp.wait_ge(h2T_ready, i - 1)
                cols = slice(SEQ, T) if rows == NS else tile_cols(i)
                sp.dma_start(mT[b][:, :, 0:rows], d["mergedT"][:, :, cols]).then_inc(in_loaded[b], 16)
                sp.dma_start(x[b][0:rows, :], d["x"][tile_rows(i, rows), :]).then_inc(in_loaded[b], 16)

            def store(i, b, rows):
                sp.wait_ge(h2T_ready, i + 1)
                sp.dma_start(d["x1"][tile_rows(i, rows), :], x1[b][0:rows, :]).then_inc(out_stored[b], 16)
                sp.dma_start(d["h2"][tile_rows(i, rows), :], h2[b][0:rows, :]).then_inc(out_stored[b], 16)
                one = slice(i, i + 1) if isinstance(i, int) else bass.ds(i, 1)
                dst = d["h2T"][one, :, :].rearrange("a p (k n) -> p (a k) n", n=P)
                sp.dma_start(dst[:, :, 0:rows], h2T[b][:, :, 0:rows]).then_inc(out_stored[b], 16)

            load(0, 0, P)
            load(1, 1, P)
            with sp.Fori(0, NT // 2 - 1) as k:
                for b in range(2):
                    store(2 * k + b, b, P)
                    load(2 * k + b + 2, b, P)
            store(NT - 2, 0, P)
            load(NT, 0, NS)
            store(NT - 1, 1, P)
            for n, col in (("gt1", 2), ("g2", 4), ("sh2", 3)):
                for q in range(DEC_B):
                    sp.dma_start(rows_of[n][q * DEC_T:(q + 1) * DEC_T, :],
                                 d["modrows"][1 + q:2 + q, col * D:(col + 1) * D].partition_broadcast(DEC_T).rearrange("p a n -> p (a n)")).then_inc(rows_loaded, 16)
            store(NT, 0, NS)
            sp.wait_ge(out_stored[0], 48 * (NT // 2 + 1))
            sp.wait_ge(out_stored[1], 48 * (NT // 2))

        @block.tensor
        def _(pe):
            pe.wait_ge(w_loaded, 16)
            pe.wait_ge(half_set, 1)

            def mult(i, b, rows, k):
                pe.wait_ge(in_loaded[b], 32 * (k + 1))
                if not early(i, 2):
                    pe.wait_ge(x1_ready, i - 1)
                for c in range(2):
                    for kk in range(DK):
                        mm = nc.tensor.matmul(psY[b][0:rows, c * 512:(c + 1) * 512], mT[b][:, kk, 0:rows], w[:, kk, c * 512:(c + 1) * 512],
                                              start=(kk == 0), stop=(kk == DK - 1))
                mm.then_inc(y_mult, 1)

            def turn(i, b, rows):
                pe.wait_ge(h2_ready, i + 1)
                if not early(i, 1):
                    pe.wait_ge(h2T_ready, i)
                for kk in range(DK):
                    mm = nc.tensor.transpose(psT[:, kk, 0:rows], h2[b][0:rows, kk * P:(kk + 1) * P], ident[0:rows, 0:rows])
                mm.then_inc(turned, 1)

            def pair(k, last):
                mult(2 * k + 1, 1, P, k)
                turn(2 * k, 0, P)
                mult(2 * k + 2, 0, NS if last else P, k + 1)
                turn(2 * k + 1, 1, P)

            mult(0, 0, P, 0)
            pair(0, False)
            with pe.Fori(1, NT // 2 - 1) as k:
                pair(k, False)
            pair(NT // 2 - 1, True)
            turn(NT, 0, NS)

        @block.scalar
        def _(act):
            def body(i, b, rows, k):
                act.wait_ge(x1_ready, i + 1)
                nc.scalar.activation(h2[b][0:rows, :], x1[b][0:rows, :], ACT.Square, accum_out=ss[0:rows, :]).then_inc(x1_squared, 1)
                act.wait_ge(turned, i + 1)
                nc.scalar.activation(h2T[b][:, :, 0:rows], psT[:, :, 0:rows], ACT.Copy).then_inc(h2T_ready, 1)
            tiles(act, body)

        @block.gpsimd
        def _(pool):
            nc.gpsimd.memset(half[:], -0.5).then_inc(half_set, 1)
            hold(pool, half_set, 1)

            def body(i, b, rows, k):
                hold(pool, x1_squared, i + 1)
                if not early(i, 1):
                    hold(pool, h2_ready, i)
                nc.gpsimd.tensor_scalar(rs[0:rows, :], ss[0:rows, :], 1.0 / D, EPS, ALU.mult, ALU.add).then_inc(rms_step, 1)
                hold(pool, rms_step, i + 1)
                nc.gpsimd.tensor_tensor(rs[0:rows, :], rs[0:rows, :], half[0:rows, :], ALU.pow).then_inc(rms, 1)
            tiles(pool, body)

        @block.vector
        def _(dve):
            dve.wait_ge(rows_loaded, 48)

            def body(i, b, rows, k):
                r = slice(0, rows)
                dve.wait_ge(y_mult, i + 1)
                dve.wait_ge(in_loaded[b], 32 * (k + 1))
                if rows == NS:
                    dve.wait_ge(rows_loaded, 48 * (1 + DEC_B))
                if not early(i, 2):
                    dve.wait_ge(out_stored[b], 48 * k)
                nc.vector.scalar_tensor_tensor(x1[b][r, :], psY[b][r, :], 0.5, rows_of["gt1"][r, :], ALU.mult, ALU.mult).then_inc(x1_step, 1)
                dve.wait_ge(x1_step, i + 1)
                nc.vector.tensor_tensor(x1[b][r, :], x1[b][r, :], x[b][r, :], ALU.add).then_inc(x1_ready, 1)
                dve.wait_ge(rms, i + 1)
                nc.vector.scalar_tensor_tensor(h2[b][r, :], x1[b][r, :], rs[r, :], rows_of["g2"][r, :], ALU.mult, ALU.mult).then_inc(h2_step, 1)
                dve.wait_ge(h2_step, i + 1)
                nc.vector.tensor_tensor(h2[b][r, :], h2[b][r, :], rows_of["sh2"][r, :], ALU.add).then_inc(h2_ready, 1)
            tiles(dve, body)


def peer_stage(nc, d, ident):
    with ExitStack() as ctx:
        m = Memory(nc, ctx)
        BF16 = mybir.dt.bfloat16
        w = m.sb("w_peer", [P, DK, PH * 2 * PHALF])
        keys = m.sb("sub_keys", [P, 2 * PH, NKEYS])
        ring = [m.sb(f"rows{r}", [P, 2 * D]) for r in range(RING)]
        diag = [m.sb(f"diag{r}", [P, P]) for r in range(RING)]
        idx = [m.sb(f"idx{b}", [P, TOPK], U32) for b in range(2)]
        ids = m.sb("expert_ids", [P, PH, TOPK], U32)
        gates = m.sb("half_gates", [P, PH, TOPK])
        gcur = [m.sb(f"gates_now{b}", [P, TOPK]) for b in range(2)]
        gt2, x1, y, h2n, h2c = (m.sb(n, [P, D]) for n in ("gt2", "x1_now", "y_out", "h2_next", "h2_now"))
        h2T = m.sb("h2T_now", [P, DK, P])
        q_sb = m.sb("q_sb", [P, 2 * PHALF])
        qT = m.sb("qT_p", [P, 2, P])
        sc = m.sb("key_scores", [P, 2, NKEYS])
        sc2 = m.sb("key_scores_rest", [P, 2, NKEYS])
        top = m.sb("top_scores", [P, 2, TOPK])
        topi = m.sb("top_keys", [P, 2, TOPK], U32)
        topf = m.sb("top_keys_f", [P, 2, TOPK])
        cand = m.sb("pair_scores", [P, TOPK, TOPK])
        cand2 = m.sb("pair_scores_rest", [P, TOPK * TOPK])
        cs = m.sb("best_scores", [P, TOPK])
        ci = m.sb("best_pairs", [P, TOPK], U32)
        pair = m.sb("pair_halves", [P, 2, TOPK], U32)
        iota = m.sb("iota16", [P, TOPK])
        pick = m.sb("pick", [P, 2, TOPK, TOPK])
        picked = m.sb("picked", [P, 2, TOPK])
        nmax, esum, rsum = m.sb("neg_best", [P, 1]), m.sb("exp_sum", [P, 1]), m.sb("exp_rsum", [P, 1])
        ex = m.sb("exp_best", [P, TOPK])
        a, g1, th, co = ([m.sb(f"{n}{b}", [P, BATCH]) for b in range(2)] for n in ("dots", "poly", "tanh", "coef"))
        zeros = m.sb("zeros", [P, 512], BF16)
        acc = m.ps("acc_peer", [P, D])
        psq, psT, pss = m.ps("ps_q", [P, 2 * PHALF]), m.ps("ps_qT", [P, 2, P]), m.ps("ps_scores", [P, 2, NKEYS])
        s = m.sem
        w_loaded, small_loaded, h2T_loaded, h2_loaded, x1_loaded, y_stored = s("w_peer_loaded"), s("small3_loaded"), s("h2T_loaded"), s("h2_loaded"), s("x1_loaded"), s("y_stored")
        zero_set = s("zero_set")
        q_mult, q_moved, q_turned, qT_moved, key_mult, keys_moved = s("q_mult"), s("q_moved3"), s("q_turned3"), s("qT_moved"), s("key_mult"), s("keys_moved")
        top_step, pick_step, softmax_in, exp_done, ids_ready, gates_ready = s("top_step"), s("pick_step"), s("softmax_in"), s("exp_done"), s("ids_ready"), s("gates_ready")
        staged, slot_free, dotted, gelu_step, gelu_in, tanh_done, coef_ready, diag_ready = s("staged"), s("slot_free"), s("dotted"), s("gelu_step"), s("gelu_in"), s("tanh_done"), s("coef_ready"), s("diag_ready")
        gathered = [s(f"gathered{r}") for r in range(RING)]
        h2_taken, y_step, y_ready = s("h2_taken"), s("y_step"), s("y_ready")
        block = ctx.enter_context(nc.Block())
        NB = TOPK // BATCH

        def schedule(eng, unit, begin=None, end=None):
            def tile(t, rows, next_rows):
                if begin and rows:
                    begin(t, rows)
                with eng.Fori(0, PH // 2) as hp:
                    for b in range(2):
                        unit(PH * t + 2 * hp + b, 2 * hp + b, b, rows, next_rows)
                if end and rows:
                    end(t, rows)
            tile(-1, None, P)
            with eng.Fori(0, NT - 1) as t:
                tile(t, P, P)
            tile(NT - 1, P, NS)
            tile(NT, NS, None)

        @block.sync
        def _(sp):
            sp.dma_start(h2T[:], d["h2T"][0].rearrange("p (k n) -> p k n", n=P)).then_inc(h2T_loaded, 16)
            sp.dma_start(w[:], d["w_pq"]).then_inc(w_loaded, 16)
            sp.dma_start(keys[:], d["subkT"]).then_inc(small_loaded, 16)
            sp.dma_start(iota[:], d["iota"].partition_broadcast(P)).then_inc(small_loaded, 16)
            sp.dma_start(h2n[:], d["h2"][0:P, :]).then_inc(h2_loaded, 16)
            sp.dma_start(x1[:], d["x1"][0:P, :]).then_inc(x1_loaded, 16)
            sp.dma_start(gt2[:], d["modrows"][0:1, 5 * D:6 * D].partition_broadcast(P).rearrange("p a n -> p (a n)")).then_inc(small_loaded, 16)
            sp.wait_ge(q_mult, PH)
            sp.dma_start(h2T[:], d["h2T"][1].rearrange("p (k n) -> p k n", n=P)).then_inc(h2T_loaded, 16)

            def tile(t, next_rows, rows_after):
                sp.wait_ge(h2_taken, t + 1)
                sp.dma_start(h2n[0:next_rows, :], d["h2"][tile_rows(t + 1, next_rows), :]).then_inc(h2_loaded, 16)
                if rows_after:
                    sp.wait_ge(q_mult, PH * (t + 2))
                    one = slice(t + 2, t + 3) if isinstance(t, int) else bass.ds(t + 2, 1)
                    src = d["h2T"][one, :, :].rearrange("a p (k n) -> p (a k) n", n=P)
                    sp.dma_start(h2T[:, :, 0:rows_after], src[:, :, 0:rows_after]).then_inc(h2T_loaded, 16)
                sp.wait_ge(y_ready, t + 1)
                sp.dma_start(d["y"][tile_rows(t, P), :], y[:]).then_inc(y_stored, 16)
                sp.dma_start(x1[0:next_rows, :], d["x1"][tile_rows(t + 1, next_rows), :]).then_inc(x1_loaded, 16)

            with sp.Fori(0, NT - 2) as t:
                tile(t, P, P)
            tile(NT - 2, P, NS)
            tile(NT - 1, NS, None)
            for q in range(DEC_B):
                sp.dma_start(gt2[q * DEC_T:(q + 1) * DEC_T, :],
                             d["modrows"][1 + q:2 + q, 5 * D:6 * D].partition_broadcast(DEC_T).rearrange("p a n -> p (a n)")).then_inc(small_loaded, 16)
            sp.wait_ge(y_ready, NT + 1)
            sp.dma_start(d["y"][SEQ:T, :], y[0:NS, :]).then_inc(y_stored, 16)
            sp.wait_ge(y_stored, 16 * (NT + 2))

        @block.gpsimd
        def _(pool):
            nc.gpsimd.memset(zeros[:], 0.0).then_inc(zero_set, 1)

            def unit(n, h, b, rows, next_rows):
                if rows is None:
                    return
                hold(pool, ids_ready, n + 1)
                hold(pool, dotted, TOPK * (n + 1))
                one = bass.ds(h, 1)
                nc.gpsimd.tensor_copy(idx[b][0:rows, :], ids[0:rows, one, :].rearrange("p a k -> p (a k)")).then_inc(staged, 1)
                hold(pool, staged, n + 1)
                for j in range(TOPK):
                    hold(pool, slot_free, TOPK * n + j + 1)
                    nc.gpsimd.indirect_dma_start(ring[j % RING][0:rows, :], None, d["uv"],
                                                 bass.IndirectOffsetOnAxis(ap=idx[b][0:rows, j:j + 1], axis=0)).then_inc(gathered[j % RING], 16)

            def tile(t, rows):
                with pool.Fori(0, PH // 2) as hp:
                    for b in range(2):
                        unit(PH * t + 2 * hp + b, 2 * hp + b, b, rows, None)

            with pool.Fori(0, NT) as t:
                tile(t, P)
            tile(NT, NS)

        @block.scalar
        def _(act):
            act.sem_inc(y_stored, 16)
            act.sem_inc(slot_free, RING)
            act.sem_inc(dotted, 2 * TOPK)

            def weigh(n, q, rows):
                bq = q % 2
                act.wait_ge(gelu_in, NB * n + q + 1)
                nc.scalar.activation(th[bq][0:rows, :], g1[bq][0:rows, :], ACT.Tanh, scale=GELU_A).then_inc(tanh_done, 1)
                act.wait_ge(coef_ready, NB * n + q + 1)
                for k in range(BATCH):
                    r = (q * BATCH + k) % RING
                    nc.scalar.activation(diag[r][0:rows, 0:rows], ident[0:rows, 0:rows], ACT.Copy, scale=co[bq][0:rows, k:k + 1]).then_inc(diag_ready, 1)

            def unit(n, h, b, rows, next_rows):
                m_ = n + PH

                def move(dst, src, full, sem):
                    act.wait_ge(full, m_ + 1)
                    nc.scalar.activation(dst, src, ACT.Copy).then_inc(sem, 1)
                for q in range(NB):
                    if rows:
                        weigh(n, q, rows)
                    if next_rows:
                        r = slice(0, next_rows)
                        if q == 0:
                            move(q_sb[r, :], psq[r, :], q_mult, q_moved)
                        elif q == 1:
                            move(qT[:, :, r], psT[:, :, r], q_turned, qT_moved)
                        elif q == 2:
                            move(sc[r], pss[r], key_mult, keys_moved)
                        else:
                            act.wait_ge(softmax_in, m_ + 1)
                            nc.scalar.activation(ex[r, :], cs[r, :], ACT.Exp, bias=nmax[r, :], accum_out=esum[r, :]).then_inc(exp_done, 1)
            schedule(act, unit)

        @block.tensor
        def _(pe):
            pe.wait_ge(w_loaded, 16)
            pe.wait_ge(small_loaded, 48)
            pe.wait_ge(zero_set, 1)

            def begin(t, rows):
                pe.wait_ge(y_step, t + 1)
                for c in range(2):
                    nc.tensor.matmul(acc[:, c * 512:(c + 1) * 512], zeros[:, 0:P], zeros[:], start=True, stop=False, skip_group_check=True)

            def unit(n, h, b, rows, next_rows):
                m_ = n + PH
                cols = bass.ds(h * 2 * PHALF, 2 * PHALF)
                for q in range(NB):
                    if rows:
                        for k in range(BATCH):
                            j = q * BATCH + k
                            hold(pe, diag_ready, TOPK * n + j + 1)
                            for c in range(2):
                                mm = nc.tensor.matmul(acc[0:rows, c * 512:(c + 1) * 512], diag[j % RING][0:rows, 0:rows],
                                                      ring[j % RING][0:rows, D + c * 512:D + (c + 1) * 512], start=False, stop=False, skip_group_check=True)
                            mm.then_inc(slot_free, 1)
                    if next_rows:
                        r = slice(0, next_rows)
                        if q == 0:
                            for k in range(DK):
                                mm = nc.tensor.matmul(psq[r, :], h2T[:, k, r], w[:, k, cols], start=(k == 0), stop=(k == DK - 1))
                            mm.then_inc(q_mult, 1)
                        elif q == 1:
                            hold(pe, q_moved, m_ + 1)
                            for p in range(2):
                                mm = nc.tensor.transpose(psT[:, p, r], q_sb[r, p * P:(p + 1) * P], ident[r, r])
                            mm.then_inc(q_turned, 1)
                        elif q == 2:
                            pe.wait_ge(qT_moved, m_ + 1)
                            for p in range(2):
                                one = bass.ds(2 * h + p, 1)
                                mm = nc.tensor.matmul(pss[r, p, :], qT[:, p, r], keys[:, one, :].rearrange("p a n -> p (a n)"), start=True, stop=True)
                            mm.then_inc(key_mult, 1)

            def tile(t, rows, next_rows):
                if next_rows:
                    pe.wait_ge(h2T_loaded, 16 * (t + 2))
                if rows:
                    begin(t, rows)
                with pe.Fori(0, PH // 2) as hp:
                    for b in range(2):
                        unit(PH * t + 2 * hp + b, 2 * hp + b, b, rows, next_rows)

            tile(-1, None, P)
            with pe.Fori(0, NT - 1) as t:
                tile(t, P, P)
            tile(NT - 1, P, NS)
            tile(NT, NS, None)

        @block.vector
        def _(dve):
            dve.wait_ge(small_loaded, 48)
            dve.sem_inc(y_step, 1)
            SMALL = 3
            TOP = 19

            def begin(t, rows):
                dve.wait_ge(h2_loaded, 16 * (t + 1))
                dve.wait_ge(dotted, 2 * TOPK + SLOTS * t)
                nc.vector.tensor_copy(h2c[0:rows, :], h2n[0:rows, :]).then_inc(h2_taken, 1)
                hold(dve, h2_taken, t + 1)

            def end(t, rows):
                r = slice(0, rows)
                if rows == NS:
                    dve.wait_ge(small_loaded, 48 + 16 * DEC_B)
                dve.wait_ge(slot_free, RING + SLOTS * (t + 1))
                dve.wait_ge(y_stored, 16 * (t + 1))
                dve.wait_ge(x1_loaded, 16 * (t + 1))
                nc.vector.tensor_tensor(y[r, :], acc[r, :], gt2[r, :], ALU.mult).then_inc(y_step, 1)
                dve.wait_ge(y_step, t + 2)
                nc.vector.tensor_tensor(y[r, :], y[r, :], x1[r, :], ALU.add).then_inc(y_ready, 1)

            def dots(n, b, q, rows):
                r, bq = slice(0, rows), q % 2
                st = Steps(dve, gelu_step, base=(SMALL * NB + 1) * n + 1 + SMALL * q)
                for k in range(BATCH):
                    j = q * BATCH + k
                    u = ring[j % RING][r, 0:D]
                    dve.wait_ge(gathered[j % RING], 16 * ((TOPK // RING) * n + j // RING + 1))
                    nc.vector.tensor_tensor_reduce(u, u, h2c[r, :], 1.0, 0.0, ALU.mult, ALU.add, a[bq][r, k:k + 1]).then_inc(dotted, 1)
                dve.wait_ge(dotted, 2 * TOPK + TOPK * n + (q + 1) * BATCH)
                st.did(nc.vector.tensor_tensor(g1[bq][r, :], a[bq][r, :], a[bq][r, :], ALU.mult))
                st.wait()
                st.did(nc.vector.tensor_scalar(g1[bq][r, :], g1[bq][r, :], GELU_B, 1.0, ALU.mult, ALU.add))
                st.wait()
                nc.vector.tensor_tensor(g1[bq][r, :], g1[bq][r, :], a[bq][r, :], ALU.mult).then_inc(gelu_in, 1)
                dve.wait_ge(tanh_done, NB * n + q + 1)
                st.did(nc.vector.scalar_tensor_tensor(co[bq][r, :], th[bq][r, :], 1.0, a[bq][r, :], ALU.add, ALU.mult))
                st.wait()
                nc.vector.tensor_tensor(co[bq][r, :], co[bq][r, :], gcur[b][r, q * BATCH:(q + 1) * BATCH], ALU.mult).then_inc(coef_ready, 1)

            def choose(m_, h, rows):
                r = slice(0, rows)
                one = bass.ds(h, 1)
                st = Steps(dve, top_step, base=TOP * m_, own=True)
                E8 = slice(0, 8), slice(8, 16)
                hold(dve, keys_moved, m_ + 1)
                for p in range(2):
                    st.did(nc.vector.max(top[r, p, E8[0]], sc[r, p, :]))
                st.wait()
                for p in range(2):
                    st.did(nc.vector.max_index(topi[r, p, E8[0]], top[r, p, E8[0]], sc[r, p, :]))
                    nc_ins = nc.vector.match_replace(sc2[r, p, :], top[r, p, E8[0]], sc[r, p, :], -3.0e38)
                    st.did(nc_ins)
                st.wait()
                for p in range(2):
                    st.did(nc.vector.max(top[r, p, E8[1]], sc2[r, p, :]))
                st.wait()
                for p in range(2):
                    st.did(nc.vector.max_index(topi[r, p, E8[1]], top[r, p, E8[1]], sc2[r, p, :]))
                st.did(nc.vector.tensor_tensor(cand[r], bc(top[r, 0, :].unsqueeze(2), [rows, TOPK, TOPK]),
                                               bc(top[r, 1, :].unsqueeze(1), [rows, TOPK, TOPK]), ALU.add))
                st.wait()
                flat = cand[r].rearrange("p a b -> p (a b)")
                st.did(nc.vector.tensor_copy(topf[r], topi[r]))
                st.did(nc.vector.max(cs[r, E8[0]], flat))
                st.wait()
                st.did(nc.vector.max_index(ci[r, E8[0]], cs[r, E8[0]], flat))
                st.did(nc.vector.match_replace(cand2[r, :], cs[r, E8[0]], flat, -3.0e38))
                st.wait()
                st.did(nc.vector.max(cs[r, E8[1]], cand2[r, :]))
                st.wait()
                nc.vector.tensor_scalar(nmax[r, :], cs[r, 0:1], -1.0, None, ALU.mult).then_inc(softmax_in, 1)
                st.did(nc.vector.max_index(ci[r, E8[1]], cs[r, E8[1]], cand2[r, :]))
                st.wait()
                st.did(nc.vector.tensor_scalar(pair[r, 0, :], ci[r, :], 4, None, ALU.logical_shift_right))
                st.did(nc.vector.tensor_scalar(pair[r, 1, :], ci[r, :], TOPK - 1, None, ALU.bitwise_and))
                assert st.n == TOP, st.n
                return st

            def choose_ids(m_, h, rows, staged_before):
                r = slice(0, rows)
                one = bass.ds(h, 1)
                st = Steps(dve, pick_step, base=4 * m_)
                dve.wait_ge(top_step, TOP * (m_ + 1))
                halves = pair[r].rearrange("p a k -> p (a k)")
                st.did(nc.vector.tensor_tensor(pick[r].rearrange("p a k j -> p (a k) j"), bc(halves.unsqueeze(2), [rows, 2 * TOPK, TOPK]),
                                               bc(iota[r, :].unsqueeze(1), [rows, 2 * TOPK, TOPK]), ALU.is_equal))
                st.wait()
                st.did(nc.vector.tensor_tensor(pick[r], pick[r], bc(topf[r].unsqueeze(2), [rows, 2, TOPK, TOPK]), ALU.mult))
                st.wait()
                st.did(nc.vector.tensor_reduce(picked[r].rearrange("p a k -> p (a k)"), pick[r].rearrange("p a k j -> p (a k) j"), AX, ALU.add))
                st.wait()
                if staged_before:
                    dve.wait_ge(staged, m_ - PH + 1)
                nc.vector.scalar_tensor_tensor(ids[r, one, :].rearrange("p a k -> p (a k)"), picked[r, 0, :], float(NKEYS), picked[r, 1, :],
                                               ALU.mult, ALU.add).then_inc(ids_ready, 1)
                dve.wait_ge(exp_done, m_ + 1)
                st.did(nc.vector.reciprocal(rsum[r, :], esum[r, :]))
                st.wait()
                nc.vector.tensor_scalar(gates[r, one, :].rearrange("p a k -> p (a k)"), ex[r, :], rsum[r, :], 0.5, ALU.mult, ALU.mult).then_inc(gates_ready, 1)

            def unit(n, h, b, rows, next_rows):
                m_ = n + PH
                if rows:
                    dve.wait_ge(gates_ready, n + 1)
                    g = Steps(dve, gelu_step, base=(SMALL * NB + 1) * n)
                    g.did(nc.vector.tensor_copy(gcur[b][0:rows, :], gates[0:rows, bass.ds(h, 1), :].rearrange("p a k -> p (a k)")))
                    g.wait()
                    for q in range(NB):
                        dots(n, b, q, rows)
                if next_rows:
                    choose(m_, h, next_rows)
                    choose_ids(m_, h, next_rows, rows is not None)
            schedule(dve, unit, begin, end)


def build(nc, ins, outs):
    d = dict(ins)
    d.update(outs)

    def scratch(name, shape):
        return nc.dram_tensor(name, shape, F32, kind="Internal").ap()

    d["modrows"] = scratch("modrows", (1 + DEC_B, NMOD * 512))
    d["mergedT"] = scratch("mergedT", (P, DK, T))
    d["x1"] = scratch("x1_d", (T, D))
    d["h2"] = scratch("h2_d", (T, D))
    d["h2T"] = scratch("h2T_d", (NT + 1, P, DK * P))
    with ExitStack() as whole:
        ident = whole.enter_context(nc.sbuf_tensor("ident", [P, P], F32))
        ident_loaded = whole.enter_context(nc.semaphore("ident_loaded"))
        qkv_loaded = whole.enter_context(nc.semaphore("qkv_loaded"))
        d["ident_loaded"] = ident_loaded
        with ExitStack() as c1:
            hT = c1.enter_context(nc.sbuf_tensor("hT", [P, DK, T], F32))
            attnT = c1.enter_context(nc.sbuf_tensor("attnT", [P, DK, T], F32))
            with ExitStack() as c2:
                qk_s = c2.enter_context(nc.sbuf_tensor("qk_s", [NS, QKW], F32))
                v_s = c2.enter_context(nc.sbuf_tensor("v_s", [NS, KVW], F32))
                with ExitStack() as c3:
                    w_qkv = c3.enter_context(nc.sbuf_tensor("w_qkv", [P, DK, QKVW], F32))
                    with nc.Block() as load:
                        @load.sync
                        def _(sp):
                            sp.dma_start(ident[:], d["ident"]).then_inc(ident_loaded, 16)
                    mods_stage(nc, d, w_qkv, qkv_loaded, hT, attnT)
                    qkv_attn_stage(nc, d, ident, w_qkv, qkv_loaded, hT, attnT, qk_s, v_s)
                sample_stage(nc, d, ident, qk_s, v_s, attnT)
            with ExitStack() as c4:
                yT = c4.enter_context(nc.sbuf_tensor("yT", [P, DK, T], F32))
                conv_stage(nc, d, hT, yT)
                merge_stage(nc, d, hT, attnT, yT)
        residual_stage(nc, d, ident)
        peer_stage(nc, d, ident)


def _constants():
    half = HD // 2
    inv = (10000.0 ** (-np.arange(half, dtype=np.float32) / np.float32(half)).astype(np.float64)).astype(np.float32)
    pos = np.concatenate([np.arange(SEQ), np.tile(PAST + np.arange(DEC_T), DEC_B)]).astype(np.float32)
    ang = (pos[:, None] * inv[None, :]).astype(np.float64)
    cos, sin = np.cos(ang).astype(np.float32), np.sin(ang).astype(np.float32)
    q, k = np.arange(P)[:, None], np.arange(2 * P)[None, :]
    band = (k >= q) & (k <= q + WIN)
    masks = np.stack([np.where(band & (k >= P), 0.0, NEG), np.where(band, 0.0, NEG)], axis=1).astype(np.float32)
    tok, j = np.tile(np.arange(DEC_T), GRP)[:, None], np.arange(WIN + DEC_T)[None, :]
    mask_s = np.where((j >= tok) & (j <= tok + WIN), 0.0, NEG).astype(np.float32)
    return dict(ident=np.eye(P, dtype=np.float32), cos=np.concatenate([cos, cos], 1), sin=np.concatenate([-sin, sin], 1),
                mask=masks, mask_s=mask_s, iota=np.arange(TOPK, dtype=np.float32))


def _chunks(w):
    return w.reshape(DK, P, -1).transpose(1, 0, 2)


def _by_columns(w):
    return w.reshape(DK, P, DK, P).transpose(2, 1, 0, 3)


def _layout(a):
    w_in = a["w_in"][0]
    at = np.cumsum([0, NH * HD, KVW, KVW, D, D, D, D, D])
    part = lambda n: w_in[:, at[n]:at[n + 1]]
    c_all = np.concatenate([a["c_prompt"], a["c_sample"]])
    stack = lambda *ws: np.stack([_by_columns(w) for w in ws], axis=2)
    return dict(
        x=np.concatenate([a["x_prompt"].reshape(SEQ, D), a["x_sample"].reshape(NS, D)]),
        cT=c_all.T.reshape(DK, P, -1).transpose(1, 0, 2),
        w_ada=a["w_ada"][0].reshape(DK, P, NMOD, 512).transpose(2, 1, 0, 3),
        b_ada=a["b_ada"][0],
        norms=np.stack([a["norm1"][0], a["norm2"][0]]),
        w_qkv=_chunks(w_in[:, :QKVW]),
        gain=np.concatenate([np.tile(a["q_norm"][0], NH), np.tile(a["k_norm"][0], NKV)]),
        sinks=a["attn_sinks"][0],
        sinks_s=np.repeat(a["attn_sinks"][0].reshape(NKV, GRP).T, DEC_T, axis=0),
        cache_k=a["cache_win_k"][0].reshape(DEC_B, WIN, KVW),
        cache_v=a["cache_win_v"][0].reshape(DEC_B, WIN, KVW),
        w_bcx=stack(part(3), part(4), part(5)),
        conv_wT=a["conv_w"][0].T.reshape(DK, P, 3).transpose(1, 0, 2),
        stateT=a["state_conv"][0].reshape(DEC_B, 2, DK, P).transpose(3, 2, 0, 1),
        w_merge=stack(part(6), a["w_attn_o"][0], part(7), a["w_conv_o"][0]),
        w_out=_chunks(a["w_out"][0]),
        w_pq=_chunks(a["w_peer_q"][0]),
        subkT=a["peer_sub_keys"][0].reshape(2 * PH, NKEYS, PHALF).transpose(2, 0, 1),
        uv=np.concatenate([a["peer_u"][0], a["peer_v"][0]], axis=1),
    )


_OUTS = dict(y=(T, D), win_k_p=(P, KVW), win_v_p=(P, KVW), win_k_s=(DEC_B, WIN, KVW), win_v_s=(DEC_B, WIN, KVW),
             conv_new=(P, DK, 2 + 2 * DEC_B))


def kernel(**inputs):
    import concourse.bacc as _bacc
    from concourse.bass_utils import run_bass_kernel_spmd as _run

    nc = _bacc.Bacc("TRN2", target_bir_lowering=False, num_devices=1)
    arrays = {n: np.ascontiguousarray(v) for n, v in _layout({k: np.asarray(v) for k, v in inputs.items()}).items()}
    arrays.update({n: np.ascontiguousarray(v) for n, v in _constants().items()})
    ins = {n: nc.dram_tensor(f"in_{n}", v.shape, F32, kind="ExternalInput").ap() for n, v in arrays.items()}
    outs = {n: nc.dram_tensor(f"out_{n}", shape, F32, kind="ExternalOutput").ap() for n, shape in _OUTS.items()}
    build(nc, ins, outs)
    r = _run(nc, [{f"in_{n}": v for n, v in arrays.items()}], core_ids=[0]).results[0]
    y = r["out_y"]
    new = r["out_conv_new"]
    window = (1, 1, WIN, NKV, HD)
    windows = (1, DEC_B, WIN, NKV, HD)
    conv_p = new[:, :, 0:2].transpose(2, 1, 0).reshape(1, 1, 2, D)
    conv_s = new[:, :, 2:].reshape(P, DK, DEC_B, 2).transpose(2, 3, 1, 0).reshape(1, DEC_B, 2, D)
    return (y[:SEQ].reshape(1, SEQ, D), y[SEQ:].reshape(DEC_B, DEC_T, D),
            r["out_win_k_p"].reshape(window), r["out_win_v_p"].reshape(window), np.ascontiguousarray(conv_p),
            r["out_win_k_s"].reshape(windows), r["out_win_v_s"].reshape(windows), np.ascontiguousarray(conv_s))
```

```python
from contextlib import ExitStack

import numpy as np

import concourse.bass as bass
from concourse import mybir

ALU = mybir.AluOpType
ACT = mybir.ActivationFunctionType
F32 = mybir.dt.float32
U32 = mybir.dt.uint32
AX = mybir.AxisListType.X

P = 128
D = 1024
DK = D // P
SEQ = 1024
DEC_B, DEC_T = 8, 4
NS = DEC_B * DEC_T
T = SEQ + NS
NT = SEQ // P
PAST = 4096
NH, NKV, HD = 16, 4, 64
GRP = NH // NKV
NQK = NH + NKV
WIN = 128
KVW = NKV * HD
QKVW = NH * HD + 2 * KVW
QKW = NQK * HD
CB = T // 3
PH, TOPK, NKEYS, PHALF = 8, 16, 128, 128
NEXP = NKEYS * NKEYS
EPS = 1e-6
SCALE = HD ** -0.5
NEG = -1e30
GELU_A, GELU_B = 0.7978845608028654, 0.044715
NMOD = 12
RING = 8
BATCH = 4
SLOTS = PH * TOPK


def hold(eng, sem, value):
    eng.wait_ge(sem, value)
    if not isinstance(value, int):
        eng.nop(nofuse=True)


class Steps:

    def __init__(self, eng, sem, base=0, own=False):
        self.eng, self.sem, self.base, self.n, self.own = eng, sem, base, 0, own

    def did(self, ins):
        self.n += 1
        return ins.then_inc(self.sem, 1)

    def wait(self):
        if self.own:
            hold(self.eng, self.sem, self.base + self.n)
        else:
            self.eng.wait_ge(self.sem, self.base + self.n)


def over(eng, first, last, body):
    if last - first == 1:
        body(first)
    else:
        with eng.Fori(first, last) as i:
            body(i)


def bc(ap, shape):
    return ap.to_broadcast(shape)


def tile_cols(i):
    return bass.ds(i * P, P) if not isinstance(i, int) else slice(i * P, i * P + P)


def tile_rows(i, rows):
    if isinstance(i, int):
        return slice(i * P, i * P + rows)
    return bass.ds(i * P, rows)


class Memory:

    def __init__(self, nc, ctx):
        self.nc, self.ctx = nc, ctx

    def sb(self, name, shape, dt=F32):
        return self.ctx.enter_context(self.nc.sbuf_tensor(name, shape, dt))

    def ps(self, name, shape):
        return self.ctx.enter_context(self.nc.psum_tensor(name, shape, F32))

    def sem(self, name):
        return self.ctx.enter_context(self.nc.semaphore(name))


def mods_stage(nc, d, ident, w_qkv, hT, attnT):
    with ExitStack() as ctx:
        m = Memory(nc, ctx)
        NR = 1 + DEC_B
        cT = m.sb("cT", [P, DK, NR])
        cth = m.sb("cth", [P, DK, NR])
        csil = m.sb("csil", [P, DK, NR])
        early, late = hT.rearrange("p k n -> p (k n)"), attnT.rearrange("p k n -> p (k n)")
        w = [early[:, b * DK * 512:(b + 1) * DK * 512].rearrange("p (k n) -> p k n", k=DK) for b in range(2)]
        bias = m.sb("bias", [NR, NMOD * 512])
        mod = late[0:NR, 0:NMOD * 512]
        norms = late[0:NR, NMOD * 512:NMOD * 512 + 2 * D].rearrange("p (a n) -> p a n", a=2)
        acc = [m.ps(f"acc{b}", [P, 512]) for b in range(2)]
        c_loaded, rows_loaded, c_tanh, silu_ready = m.sem("c_loaded"), m.sem("rows_loaded"), m.sem("c_tanh"), m.sem("silu_ready")
        w_loaded = [m.sem(f"w_ada_loaded{b}") for b in range(2)]
        acc_ready, acc_free, mods_ready, mods_stored = m.sem("acc_ready"), m.sem("acc_free"), m.sem("mods_ready"), m.sem("mods_stored")
        silu_step = m.sem("silu_step")
        block = ctx.enter_context(nc.Block())

        @block.sync
        def _(sp):
            sp.dma_start(cT[:], d["cT"]).then_inc(c_loaded, 16)
            for n in range(2):
                sp.dma_start(w[n], d["w_ada"][n]).then_inc(w_loaded[n], 16)
            sp.dma_start(bias[:], d["b_ada"].partition_broadcast(NR)).then_inc(rows_loaded, 16)
            sp.dma_start(norms, d["norms"].partition_broadcast(NR)).then_inc(rows_loaded, 16)
            with sp.Fori(1, NMOD // 2) as i:
                for b in range(2):
                    sp.wait_ge(acc_ready, 2 * i + b - 1)
                    sp.dma_start(w[b], d["w_ada"][2 * i + b]).then_inc(w_loaded[b], 16)
            sp.dma_start(ident[:], d["ident"]).then_inc(d["ident_loaded"], 16)
            sp.dma_start(w_qkv[:], d["w_qkv"]).then_inc(d["qkv_loaded"], 16)
            sp.wait_ge(mods_ready, 2)
            sp.dma_start(d["modrows"], mod).then_inc(mods_stored, 16)
            sp.wait_ge(mods_stored, 16)

        @block.scalar
        def _(act):
            act.wait_ge(c_loaded, 16)
            nc.scalar.activation(cth[:], cT[:], ACT.Tanh, scale=0.5).then_inc(c_tanh, 1)

        @block.vector
        def _(dve):
            dve.wait_ge(c_tanh, 1)
            nc.vector.scalar_tensor_tensor(csil[:], cth[:], 1.0, cT[:], ALU.add, ALU.mult).then_inc(silu_step, 1)
            dve.wait_ge(silu_step, 1)
            nc.vector.tensor_scalar(csil[:], csil[:], 0.5, None, ALU.mult).then_inc(silu_ready, 1)
            dve.wait_ge(rows_loaded, 32)
            with dve.Fori(0, NMOD // 2) as i:
                for b in range(2):
                    dve.wait_ge(acc_ready, 2 * i + b + 1)
                    cols = bass.ds((2 * i + b) * 512, 512)
                    nc.vector.tensor_tensor(mod[:, cols], acc[b][0:NR, :], bias[:, cols], ALU.add).then_inc(acc_free, 1)
            dve.wait_ge(acc_free, NMOD)
            for s, first in ((0, D), (1, 4 * D)):
                part = mod[:, first:first + D]
                nc.vector.scalar_tensor_tensor(part, part, 1.0, norms[:, s, :], ALU.add, ALU.mult).then_inc(mods_ready, 1)

        @block.tensor
        def _(pe):
            pe.wait_ge(silu_ready, 1)

            def chunk_pair(i):
                for b in range(2):
                    pe.wait_ge(w_loaded[b], 16 * (i + 1))
                    if not isinstance(i, int):
                        pe.wait_ge(acc_free, 2 * i + b - 1)
                    for k in range(DK):
                        mm = nc.tensor.matmul(acc[b][0:NR, :], csil[:, k, :], w[b][:, k, :], start=(k == 0), stop=(k == DK - 1))
                    mm.then_inc(acc_ready, 1)

            chunk_pair(0)
            with pe.Fori(1, NMOD // 2) as i:
                chunk_pair(i)


def qkv_attn_stage(nc, d, ident, w_qkv, qkv_loaded, hT, attnT, qk_s, v_s):
    with ExitStack() as ctx:
        m = Memory(nc, ctx)
        x = m.sb("x", [P, D])
        h = m.sb("h", [P, D])
        hTc = m.sb("hTc", [P, DK, P])
        g1 = m.sb("g1", [P, D])
        sh1 = m.sb("sh1", [P, D])
        gain = m.sb("gain", [P, QKW])
        cos = m.sb("cos", [P, HD])
        sin = m.sb("sin", [P, HD])
        mask = m.sb("mask", [P, 2, 2 * P])
        sinks = m.sb("sinks", [P, NH])
        half = m.sb("neg_half", [P, NQK])
        ss = m.sb("ss", [P, 1])
        rs = m.sb("rs", [P, 1])
        qkv = m.sb("qkv", [P, QKVW])
        sq = m.sb("sq", [P, QKW])
        rot = m.sb("rot", [P, QKW])
        qk = m.sb("qk", [P, QKW])
        ssh = m.sb("ssh", [P, NQK])
        rsh = m.sb("rsh", [P, NQK])
        qT = m.sb("qT", [HD, NH, P])
        kband = m.sb("kband", [HD, NKV, 2, P])
        vband = m.sb("vband", [P, 2, KVW])
        S = [m.sb(f"S{b}", [P, GRP, 2 * P]) for b in range(2)]
        PT = m.sb("PT", [P, GRP, 2, P])
        mx = m.sb("mx", [P, NH])
        nm = m.sb("nm", [P, NH])
        ds_ = m.sb("sink_minus_max", [P, NH])
        es = m.sb("exp_sink", [P, NH])
        rsum = m.sb("rsum", [P, NH])
        den = m.sb("den", [P, NH])
        rden = m.sb("rden", [P, NH])
        attn = m.sb("attn", [P, D])
        v_next = m.sb("v_next", [P, KVW])
        psT = m.ps("psT", [P, 8, P])
        psQ = [m.ps(f"psQ{b}", [P, 512]) for b in range(2)]
        psS = m.ps("psS", [P, GRP, 2 * P])
        psO = m.ps("psO", [P, NH, HD])

        s = m.sem
        rows_loaded, rope_loaded, x_loaded = s("bc_rows_loaded"), s("rope_loaded"), s("x_loaded")
        consts, gained = s("consts_set"), s("gained")
        x_squared, rms_step, rms_ready, h_step, h_ready = s("x_squared"), s("rms_step"), s("rms_ready"), s("h_step"), s("h_ready")
        psT_full, psT_free = s("psT_full"), s("psT_free")
        hT_copied = s("hT_copied")
        qkv_mult, qkv_moved = s("qkv_mult"), s("qkv_moved")
        qk_squared, qk_summed, head_rms_step, head_rms = s("qk_squared"), s("qk_summed"), s("head_rms_step"), s("head_rms")
        rope_step, roped, v_placed, band_shifted = s("rope_step"), s("roped"), s("v_placed"), s("band_shifted")
        scores, scores_moved, soft_step, max_ready, exps = s("scores"), s("scores_moved"), s("soft_step"), s("max_ready"), s("exps")
        pv_done, attn_ready, den_ready = s("pv_done"), s("attn_ready"), s("den_ready")
        kv_stored = s("kv_stored")

        qkv_read, v_kept = s("qkv_read"), s("v_kept")

        UT = 9
        LAST = NT - 1

        def later(i, n=1):
            return not isinstance(i, int) or i >= n

        def use_h(i):
            return i + 1 if isinstance(i, int) and i < 2 else 2 + UT * (i - 2) + 1

        def use_q(i):
            return 2 + UT * i + (0 if isinstance(i, int) and i == LAST else 1)

        def use_probs(i, g):
            return use_q(i) + 3 + g + 1

        def steps(eng, step):
            step(0, P, P, P)
            with eng.Fori(1, NT - 3) as i:
                step(i, P, P, P)
            step(NT - 3, P, P, NS)
            step(NT - 2, P, NS, None)
            step(LAST, NS, None, None)

        block = ctx.enter_context(nc.Block())

        def xrows(i, rows):
            return d["x"][tile_rows(i, rows), :]

        @block.sync
        def _(sp):
            sp.dma_start(x[:], xrows(0, P)).then_inc(x_loaded, 16)
            sp.dma_start(g1[:], d["modrows"][0:1, D:2 * D].partition_broadcast(P).rearrange("p a n -> p (a n)")).then_inc(rows_loaded, 16)
            sp.dma_start(sh1[:], d["modrows"][0:1, 0:D].partition_broadcast(P).rearrange("p a n -> p (a n)")).then_inc(rows_loaded, 16)
            sp.dma_start(gain[:], d["gain"].partition_broadcast(P)).then_inc(rows_loaded, 16)
            sp.dma_start(sinks[:], d["sinks"].partition_broadcast(P)).then_inc(rows_loaded, 16)
            sp.dma_start(mask[:], d["mask"]).then_inc(rows_loaded, 16)

            def load_tables(i, rows):
                if later(i):
                    sp.wait_ge(roped, i)
                sp.dma_start(cos[0:rows, :], d["cos"][tile_rows(i, rows), :]).then_inc(rope_loaded, 16)
                sp.dma_start(sin[0:rows, :], d["sin"][tile_rows(i, rows), :]).then_inc(rope_loaded, 16)

            def load_x(i, rows):
                sp.wait_ge(h_ready, i)
                sp.dma_start(x[0:rows, :], xrows(i, rows)).then_inc(x_loaded, 16)

            load_tables(0, P)
            load_x(1, P)
            load_x(2, P)

            def step(i, rows1, rows2, rows3):
                if rows3 == NS:
                    sp.wait_ge(h_ready, NT)
                    for dst, col in ((g1, D), (sh1, 0)):
                        for b in range(DEC_B):
                            sp.dma_start(dst[b * DEC_T:(b + 1) * DEC_T, :],
                                         d["modrows"][1 + b:2 + b, col:col + D].partition_broadcast(DEC_T).rearrange("p a n -> p (a n)")
                                         ).then_inc(rows_loaded, 16)
                if rows3:
                    load_x(i + 3, rows3)
                load_tables(i + 1, rows1)
            steps(sp, step)
            sp.wait_ge(roped, NT)
            sp.dma_start(d["win_k_p"], qk[:, NH * HD:QKW]).then_inc(kv_stored, 16)
            sp.wait_ge(v_placed, NT)
            sp.dma_start(d["win_v_p"], vband[:, 1, :]).then_inc(kv_stored, 16)
            sp.wait_ge(kv_stored, 32)

        @block.scalar
        def _(act):
            act.wait_ge(consts, 3)

            def square_x(i, rows):
                act.wait_ge(x_loaded, 16 * (i + 1))
                if later(i):
                    act.wait_ge(psT_full, use_h(i - 1))
                nc.scalar.activation(h[0:rows, :], x[0:rows, :], ACT.Square, accum_out=ss[0:rows, :]).then_inc(x_squared, 1)

            def move_T(dst, src, use):
                act.wait_ge(psT_full, use)
                nc.scalar.activation(dst, src, ACT.Copy).then_inc(psT_free, 1)

            def move_h(i, rows):
                if later(i):
                    act.wait_ge(qkv_mult, 3 * i)
                    act.wait_ge(hT_copied, i)
                move_T(hTc[:, :, 0:rows], psT[:, :, 0:rows], use_h(i))

            def move_qkv(i, c, rows):
                act.wait_ge(qkv_mult, 3 * i + c + 1)
                if c == 0 and later(i):
                    act.wait_ge(qkv_read, i)
                    act.wait_ge(v_kept, i)
                nc.scalar.activation(qkv[0:rows, c * 512:(c + 1) * 512], psQ[c % 2][0:rows, :], ACT.Copy).then_inc(qkv_moved, 1)

            def square_qk(i, rows):
                act.wait_ge(qkv_moved, 3 * (i + 1))
                if later(i):
                    act.wait_ge(roped, i)
                nc.scalar.activation(sq[0:rows, :], qkv[0:rows, 0:QKW], ACT.Square).then_inc(qk_squared, 1)

            def exp_group(i, g):
                act.wait_ge(max_ready, NKV * i + g + 1)
                for j in range(GRP):
                    hd = g * GRP + j
                    nc.scalar.activation(S[g % 2][:, j, :], S[g % 2][:, j, :], ACT.Exp, bias=nm[:, hd:hd + 1],
                                         accum_out=rsum[:, hd:hd + 1]).then_inc(exps, 1)
                nc.scalar.activation(es[:, g * GRP:(g + 1) * GRP], ds_[:, g * GRP:(g + 1) * GRP], ACT.Exp).then_inc(exps, 1)

            for i in range(2):
                square_x(i, P)
                move_h(i, P)
                for c in range(3):
                    move_qkv(i, c, P)
                square_qk(i, P)
            square_x(2, P)

            def step(i, rows1, rows2, rows3):
                u = use_q(i)
                if rows2:
                    move_h(i + 2, rows2)
                if later(i):
                    act.wait_ge(scores, NKV * i)
                move_T(qT[:, 0:8, :], psT[0:HD, :, :], u + 1)
                move_T(qT[:, 8:16, :], psT[0:HD, :, :], u + 2)
                if later(i):
                    act.wait_ge(band_shifted, 2 * i)
                move_T(kband[:, :, 1, :], psT[0:HD, 0:NKV, :], u + 3)
                if rows2:
                    move_qkv(i + 2, 0, rows2)
                if rows3:
                    square_x(i + 3, rows3)
                for g in range(NKV):
                    exp_group(i, g)
                    if g or later(i):
                        act.wait_ge(pv_done, NKV * i + g)
                    move_T(PT[:], psT[:, :, :].rearrange("p (j b) q -> p j b q", b=2), use_probs(i, g))
                    if g in (0, 2) and rows2:
                        move_qkv(i + 2, 1 + g // 2, rows2)
                move_T(attnT[:, :, tile_cols(i)], psT[:, :, :], use_probs(i, NKV))
                if rows2:
                    square_qk(i + 2, rows2)
            steps(act, step)

        @block.gpsimd
        def _(pool):
            nc.gpsimd.memset(half[:], -0.5).then_inc(consts, 1)
            nc.gpsimd.memset(kband[:], 0.0).then_inc(consts, 1)
            nc.gpsimd.memset(vband[:], 0.0).then_inc(consts, 1)
            hold(pool, consts, 3)

            def rms(i, rows):
                hold(pool, x_squared, i + 1)
                if later(i):
                    hold(pool, h_ready, i)
                nc.gpsimd.tensor_scalar(rs[0:rows, :], ss[0:rows, :], 1.0 / D, EPS, ALU.mult, ALU.add).then_inc(rms_step, 1)
                hold(pool, rms_step, i + 1)
                nc.gpsimd.tensor_tensor(rs[0:rows, :], rs[0:rows, :], half[0:rows, 0:1], ALU.pow).then_inc(rms_ready, 1)

            def copy_hT(i, rows):
                hold(pool, psT_free, use_h(i))
                cols = slice(SEQ, T) if rows == NS else tile_cols(i)
                nc.gpsimd.tensor_copy(hT[:, :, cols], hTc[:, :, 0:rows]).then_inc(hT_copied, 1)

            def head_rms_of(i, rows):
                hold(pool, qk_summed, i + 1)
                nc.gpsimd.tensor_scalar(rsh[0:rows, :], ssh[0:rows, :], 1.0 / HD, EPS, ALU.mult, ALU.add).then_inc(head_rms_step, 1)
                hold(pool, head_rms_step, i + 1)
                nc.gpsimd.tensor_tensor(rsh[0:rows, :], rsh[0:rows, :], half[0:rows, :], ALU.pow).then_inc(head_rms, 1)

            def keep_v(i, rows):
                hold(pool, qkv_moved, 3 * (i + 1))
                if later(i):
                    hold(pool, v_placed, i)
                nc.gpsimd.tensor_copy(v_next[0:rows, :] if rows == P else v_s[:], qkv[0:rows, QKW:QKVW]).then_inc(v_kept, 1)

            def place_v(i):
                hold(pool, v_kept, i + 1)
                nc.gpsimd.tensor_copy(vband[:, 1, :], v_next[:]).then_inc(v_placed, 1)

            def shift_band(i):
                hold(pool, scores, NKV * (i + 1))
                nc.gpsimd.tensor_copy(kband[:, :, 0, :], kband[:, :, 1, :]).then_inc(band_shifted, 1)
                hold(pool, pv_done, NKV * (i + 1))
                nc.gpsimd.tensor_copy(vband[:, 0, :], vband[:, 1, :]).then_inc(band_shifted, 1)
                hold(pool, band_shifted, 2 * (i + 1))

            rms(0, P)
            copy_hT(0, P)
            keep_v(0, P)
            place_v(0)
            head_rms_of(0, P)
            rms(1, P)
            copy_hT(1, P)
            keep_v(1, P)
            rms(2, P)

            def step(i, rows1, rows2, rows3):
                head_rms_of(i + 1, rows1)
                if rows2:
                    copy_hT(i + 2, rows2)
                if rows3:
                    rms(i + 3, rows3)
                shift_band(i)
                if rows1 == P:
                    place_v(i + 1)
                    keep_v(i + 2, rows2)
            steps(pool, step)

        @block.vector
        def _(dve):
            dve.wait_ge(rows_loaded, 80)
            dve.wait_ge(consts, 3)
            heads = lambda t, r: t[r, 0:QKW].rearrange("p (n e) -> p n e", e=HD)

            def make_h(i, rows):
                if rows == NS:
                    dve.wait_ge(rows_loaded, 80 + 32 * DEC_B)
                dve.wait_ge(rms_ready, i + 1)
                nc.vector.scalar_tensor_tensor(h[0:rows, :], x[0:rows, :], rs[0:rows, :], g1[0:rows, :], ALU.mult, ALU.mult).then_inc(h_step, 1)
                dve.wait_ge(h_step, i + 1)
                nc.vector.tensor_tensor(h[0:rows, :], h[0:rows, :], sh1[0:rows, :], ALU.add).then_inc(h_ready, 1)

            def sum_squares(i, rows):
                r = slice(0, rows)
                dve.wait_ge(qk_squared, i + 1)
                if later(i):
                    dve.wait_ge(head_rms, i)
                nc.vector.tensor_reduce(ssh[r, :], heads(sq, r), AX, ALU.add).then_inc(qk_summed, 1)

            def norm_heads(i, rows):
                r = slice(0, rows)
                dve.wait_ge(head_rms, i + 1)
                dve.wait_ge(qk_summed, i + 1)
                nc.vector.tensor_tensor(heads(sq, r), heads(qkv, r), bc(rsh[r, :].unsqueeze(2), [rows, NQK, HD]), ALU.mult).then_inc(qkv_read, 1)
                dve.wait_ge(qkv_read, i + 1)
                nc.vector.tensor_tensor(sq[r, :], sq[r, :], gain[r, :], ALU.mult).then_inc(gained, 1)

            def rope(i, rows, out):
                r = slice(0, rows)
                st = Steps(dve, rope_step, base=3 * i)
                dve.wait_ge(rope_loaded, 32 * (i + 1))
                dve.wait_ge(gained, i + 1)
                tab = lambda t: bc(t.unsqueeze(1), [rows, NQK, t.shape[1]])
                H2 = HD // 2
                st.did(nc.vector.tensor_tensor(heads(rot, r)[:, :, 0:H2], heads(sq, r)[:, :, H2:HD], tab(sin[r, 0:H2]), ALU.mult))
                st.did(nc.vector.tensor_tensor(heads(rot, r)[:, :, H2:HD], heads(sq, r)[:, :, 0:H2], tab(sin[r, H2:HD]), ALU.mult))
                st.wait()
                st.did(nc.vector.tensor_tensor(heads(sq, r), heads(sq, r), tab(cos[r, :]), ALU.mult))
                st.wait()
                if later(i):
                    dve.wait_ge(psT_full, 2 + UT * (i - 1) + 4)
                nc.vector.tensor_tensor(out[r, :], sq[r, :], rot[r, :], ALU.add).then_inc(roped, 1)

            def soft_group(i, g):
                st = Steps(dve, soft_step, base=(NKV * i + g) * 3)
                hs = slice(g * GRP, (g + 1) * GRP)
                which = 1 if later(i) else 0
                dve.wait_ge(scores, NKV * i + g + 1)
                if g >= 2 or later(i):
                    dve.wait_ge(psT_full, use_probs(i, g - 2) if g >= 2 else 2 + UT * (i - 1) + 4 + (g + 2) + 1)
                nc.vector.scalar_tensor_tensor(S[g % 2][:], psS[:], SCALE, bc(mask[:, which, :].unsqueeze(1), [P, GRP, 2 * P]),
                                               ALU.mult, ALU.add).then_inc(scores_moved, 1)
                dve.wait_ge(scores_moved, NKV * i + g + 1)
                if g == 0 and later(i):
                    dve.wait_ge(attn_ready, i)
                st.did(nc.vector.tensor_reduce(mx[:, hs], S[g % 2][:], AX, ALU.max))
                st.wait()
                st.did(nc.vector.tensor_tensor(mx[:, hs], mx[:, hs], sinks[:, hs], ALU.max))
                st.wait()
                st.did(nc.vector.tensor_scalar(nm[:, hs], mx[:, hs], -1.0, None, ALU.mult))
                st.wait()
                nc.vector.tensor_tensor(ds_[:, hs], sinks[:, hs], mx[:, hs], ALU.subtract).then_inc(max_ready, 1)

            def normalise(i):
                dve.wait_ge(exps, NKV * (GRP + 1) * (i + 1))
                nc.vector.tensor_tensor(den[:], rsum[:], es[:], ALU.add).then_inc(den_ready, 1)
                dve.wait_ge(den_ready, 2 * i + 1)
                nc.vector.reciprocal(rden[:], den[:]).then_inc(den_ready, 1)
                dve.wait_ge(den_ready, 2 * i + 2)
                dve.wait_ge(pv_done, NKV * (i + 1))
                nc.vector.tensor_tensor(attn[:, :].rearrange("p (n e) -> p n e", e=HD), psO[:],
                                        bc(rden[:].unsqueeze(2), [P, NH, HD]), ALU.mult).then_inc(attn_ready, 1)

            make_h(0, P)
            sum_squares(0, P)
            norm_heads(0, P)
            make_h(1, P)
            rope(0, P, qk)
            make_h(2, P)

            def step(i, rows1, rows2, rows3):
                sum_squares(i + 1, rows1)
                norm_heads(i + 1, rows1)
                soft_group(i, 0)
                soft_group(i, 1)
                soft_group(i, 2)
                if rows3:
                    make_h(i + 3, rows3)
                soft_group(i, 3)
                rope(i + 1, rows1, qk if rows1 == P else qk_s)
                normalise(i)
            steps(dve, step)

        @block.tensor
        def _(pe):
            pe.wait_ge(d["ident_loaded"], 16)
            pe.wait_ge(qkv_loaded, 16)
            pe.wait_ge(consts, 3)

            def turn(srcs, use, width=P, rows=P):
                if not (isinstance(use, int) and use == 1):
                    hold(pe, psT_free, use - 1)
                for j, src in enumerate(srcs):
                    mm = nc.tensor.transpose(psT[0:width, j, 0:rows], src, ident[0:rows, 0:rows])
                mm.then_inc(psT_full, 1)

            def turn_h(i, rows):
                pe.wait_ge(h_ready, i + 1)
                turn([h[0:rows, k * P:(k + 1) * P] for k in range(DK)], use_h(i), P, rows)

            def project(i, q, rows):
                c, at = q // 4, 2 * (q % 4)
                if at == 0:
                    pe.wait_ge(psT_free, use_h(i))
                    if c == 0 and later(i):
                        pe.wait_ge(qkv_moved, 3 * i)
                    if c == 2:
                        pe.wait_ge(qkv_moved, 3 * i + 1)
                for k in (at, at + 1):
                    mm = nc.tensor.matmul(psQ[c % 2][0:rows, :], hTc[:, k, 0:rows], w_qkv[:, k, c * 512:(c + 1) * 512],
                                          start=(k == 0), stop=(k == DK - 1))
                if at + 2 == DK:
                    mm.then_inc(qkv_mult, 1)

            def score(i, g):
                if g or later(i):
                    pe.wait_ge(scores_moved, NKV * i + g)
                pe.wait_ge(psT_free, use_q(i) + 3)
                for j in range(GRP):
                    mm = nc.tensor.matmul(psS[:, j, :], qT[:, g * GRP + j, :], kband[:, g, :, :].rearrange("p b n -> p (b n)"), start=True, stop=True)
                mm.then_inc(scores, 1)

            def turn_probs(i, g):
                pe.wait_ge(exps, (GRP + 1) * (NKV * i + g + 1))
                turn([S[g % 2][:, j, b * P:(b + 1) * P] for j in range(GRP) for b in range(2)], use_probs(i, g))

            def weigh(i, g):
                pe.wait_ge(psT_free, use_probs(i, g))
                pe.wait_ge(v_placed, i + 1)
                if later(i):
                    pe.wait_ge(attn_ready, i)
                    pe.wait_ge(band_shifted, 2 * i)
                for j in range(GRP):
                    for b in range(2):
                        mm = nc.tensor.matmul(psO[:, g * GRP + j, :], PT[:, j, b, :], vband[:, b, g * HD:(g + 1) * HD],
                                              start=(b == 0), stop=(b == 1))
                mm.then_inc(pv_done, 1)

            for i in range(2):
                turn_h(i, P)
                for q in range(12):
                    project(i, q, P)

            def step(i, rows1, rows2, rows3):
                u = use_q(i)
                parts = iter(range(12))

                def fill(n):
                    for _ in range(n if rows2 else 0):
                        project(i + 2, next(parts), rows2)

                if rows2:
                    turn_h(i + 2, rows2)
                pe.wait_ge(roped, i + 1)
                turn([qk[:, n * HD:(n + 1) * HD] for n in range(0, 8)], u + 1, HD)
                fill(1)
                turn([qk[:, n * HD:(n + 1) * HD] for n in range(8, 16)], u + 2, HD)
                fill(1)
                turn([qk[:, n * HD:(n + 1) * HD] for n in range(16, 20)], u + 3, HD)
                fill(2)
                score(i, 0)
                fill(2)
                score(i, 1)
                fill(1)
                turn_probs(i, 0)
                fill(1)
                weigh(i, 0)
                score(i, 2)
                fill(1)
                turn_probs(i, 1)
                fill(1)
                weigh(i, 1)
                score(i, 3)
                fill(1)
                turn_probs(i, 2)
                fill(1)
                weigh(i, 2)
                turn_probs(i, 3)
                weigh(i, 3)
                pe.wait_ge(attn_ready, i + 1)
                turn([attn[:, k * P:(k + 1) * P] for k in range(DK)], use_probs(i, NKV))
            steps(pe, step)


def sample_stage(nc, d, ident, qk_s, v_s, attnT, w_bcx):
    R = GRP * DEC_T
    KN = WIN + DEC_T
    with ExitStack() as ctx:
        m = Memory(nc, ctx)
        kc = m.sb("k_cache", [P, DEC_B, KVW])
        vc = m.sb("v_cache", [P, DEC_B, KVW])
        vn = m.sb("v_new", [DEC_T, DEC_B, KVW])
        mask = m.sb("mask_s", [R, KN])
        sinks = m.sb("sinks_s", [R, NKV])
        qT = m.sb("qT_s", [HD, DEC_B, NKV, GRP, DEC_T])
        kn = m.sb("k_new_T", [HD, NKV, NS])
        kT = [m.sb(f"k_cache_T{b}", [HD, NKV, WIN]) for b in range(2)]
        S = m.sb("S_s", [R, DEC_B, NKV, KN])
        mx, ds_, es, den, rden = (m.sb(n, [R, DEC_B, NKV]) for n in ("mx_s", "ds_s", "es_s", "den_s", "rden_s"))
        PT = [m.sb(f"PT_s{b}", [P, NKV, R]) for b in range(2)]
        PN = [m.sb(f"PN_s{b}", [DEC_T, NKV, R]) for b in range(2)]
        psA = m.ps("psA", [P, NH, NS])
        psK = m.ps("psK", [P, NKV, WIN])
        psS = m.ps("psS_s", [P, NKV, 256])
        psP = m.ps("psP", [P, NKV, R])
        psN = m.ps("psN", [P, NKV, R])
        psO = m.ps("psO_s", [P, NKV, R])
        s = m.sem
        new_stored, cache_loaded, v_new_loaded = s("new_stored"), s("cache_loaded"), s("v_new_loaded")
        q_turned, q_moved, kn_turned = s("q_turned"), s("q_moved"), s("kn_turned")
        k_turned, k_moved, scores, scores_moved = s("k_turned"), s("k_moved"), s("scores_sm"), s("scores_sm_moved")
        soft, shifted, exped, probs = s("soft_s"), s("shifted_s"), s("exped_s"), s("probs_s")
        p_turned, p_moved, weighed, out_moved = s("p_turned"), s("p_moved"), s("weighed"), s("out_moved")
        block = ctx.enter_context(nc.Block())

        @block.sync
        def _(sp):
            sp.dma_start(kc[:], d["cache_k"].rearrange("b j n -> j b n")).then_inc(cache_loaded, 16)
            sp.dma_start(vc[:], d["cache_v"].rearrange("b j n -> j b n")).then_inc(cache_loaded, 16)
            sp.dma_start(mask[:], d["mask_s"]).then_inc(cache_loaded, 16)
            sp.dma_start(sinks[:], d["sinks_s"]).then_inc(cache_loaded, 16)
            for b in range(2):
                sp.dma_start(w_bcx[b], d["w_bcx"][b]).then_inc(d["w_bcx_loaded"][b], 16)
            for b in range(DEC_B):
                rows = slice(b * DEC_T, (b + 1) * DEC_T)
                sp.dma_start(d["win_v_s"][b, WIN - DEC_T:WIN, :], v_s[rows, :]).then_inc(new_stored, 16)
                sp.dma_start(d["win_k_s"][b, WIN - DEC_T:WIN, :], qk_s[rows, NH * HD:QKW]).then_inc(new_stored, 16)
            for out, cache in (("win_v_s", "cache_v"), ("win_k_s", "cache_k")):
                sp.dma_start(d[out][:, 0:WIN - DEC_T, :], d[cache][:, DEC_T:WIN, :]).then_inc(new_stored, 16)
            sp.wait_ge(new_stored, 16 * (2 * DEC_B + 2))
            sp.dma_start(vn[:], d["win_v_s"][:, WIN - DEC_T:WIN, :].rearrange("b t n -> t b n")).then_inc(v_new_loaded, 16)

        @block.scalar
        def _(act):
            act.wait_ge(q_turned, 1)
            for g in range(NKV):
                nc.scalar.activation(qT[:, :, g, :, :].rearrange("p b h t -> p h b t"),
                                     psA[0:HD, g * GRP:(g + 1) * GRP, :].rearrange("p h (b t) -> p h b t", t=DEC_T), ACT.Copy).then_inc(q_moved, 1)
            act.wait_ge(kn_turned, 1)
            nc.scalar.activation(kn[:], psK[0:HD, :, 0:NS], ACT.Copy).then_inc(k_moved, 1)
            for b in range(DEC_B):
                act.wait_ge(k_turned, b + 1)
                if b >= 2:
                    act.wait_ge(scores, b - 1)
                nc.scalar.activation(kT[b % 2][:], psK[0:HD, :, :], ACT.Copy).then_inc(k_moved, 1)
            act.wait_ge(shifted, 2)
            nc.scalar.activation(S[:], S[:], ACT.Exp).then_inc(exped, 1)
            nc.scalar.activation(es[:], ds_[:], ACT.Exp).then_inc(exped, 1)
            for b in range(DEC_B):
                act.wait_ge(p_turned, b + 1)
                if b >= 2:
                    act.wait_ge(weighed, b - 1)
                nc.scalar.activation(PT[b % 2][:], psP[:], ACT.Copy).then_inc(p_moved, 1)
                nc.scalar.activation(PN[b % 2][:], psN[0:DEC_T], ACT.Copy).then_inc(p_moved, 1)

        @block.vector
        def _(dve):
            dve.wait_ge(cache_loaded, 64)
            for b in range(DEC_B):
                dve.wait_ge(scores, b + 1)
                nc.vector.scalar_tensor_tensor(S[:, b], psS[0:R, :, 0:KN], SCALE, bc(mask[:].unsqueeze(1), [R, NKV, KN]), ALU.mult, ALU.add).then_inc(scores_moved, 1)
            dve.wait_ge(scores_moved, DEC_B)
            flat = lambda t: t[:].rearrange("p b g -> p (b g)")
            rows = S[:].rearrange("p b g n -> p (b g) n")
            st = Steps(dve, soft)
            st.did(nc.vector.tensor_reduce(flat(mx), rows, AX, ALU.max))
            st.wait()
            sink = bc(sinks[:].unsqueeze(1), [R, DEC_B, NKV])
            st.did(nc.vector.tensor_tensor(mx[:], mx[:], sink, ALU.max))
            st.wait()
            spread = lambda t: bc(flat(t).unsqueeze(2), [R, DEC_B * NKV, KN])
            nc.vector.tensor_tensor(rows, rows, spread(mx), ALU.subtract).then_inc(shifted, 1)
            nc.vector.tensor_tensor(ds_[:], sink, mx[:], ALU.subtract).then_inc(shifted, 1)
            dve.wait_ge(exped, 2)
            st.did(nc.vector.tensor_reduce(flat(den), rows, AX, ALU.add))
            st.wait()
            st.did(nc.vector.tensor_tensor(den[:], den[:], es[:], ALU.add))
            st.wait()
            st.did(nc.vector.reciprocal(rden[:], den[:]))
            st.wait()
            nc.vector.tensor_tensor(rows, rows, spread(rden), ALU.mult).then_inc(probs, 1)
            for b in range(DEC_B):
                dve.wait_ge(weighed, b + 1)
                for par in range(2):
                    src = psO[0:HD].rearrange("p g (k e t) -> p g k e t", e=2, t=DEC_T)[:, :, :, par, :]
                    dst = attnT[par * HD:(par + 1) * HD, :, SEQ + b * DEC_T:SEQ + (b + 1) * DEC_T].rearrange("p (g k) t -> p g k t", k=GRP // 2)
                    nc.vector.tensor_copy(dst, src).then_inc(out_moved, 1)

        @block.tensor
        def _(pe):
            for n in range(NH):
                mm = nc.tensor.transpose(psA[0:HD, n, :], qk_s[:, n * HD:(n + 1) * HD], ident[0:NS, 0:NS])
            mm.then_inc(q_turned, 1)
            for n in range(NKV):
                mm = nc.tensor.transpose(psK[0:HD, n, 0:NS], qk_s[:, (NH + n) * HD:(NH + n + 1) * HD], ident[0:NS, 0:NS])
            mm.then_inc(kn_turned, 1)
            pe.wait_ge(cache_loaded, 64)
            pe.wait_ge(q_moved, NKV)
            for b in range(DEC_B):
                pe.wait_ge(k_moved, b + 1)
                for g in range(NKV):
                    mm = nc.tensor.transpose(psK[0:HD, g, :], kc[:, b, g * HD:(g + 1) * HD], ident[:, :])
                mm.then_inc(k_turned, 1)
                pe.wait_ge(k_moved, b + 2)
                if b:
                    pe.wait_ge(scores_moved, b)
                for g in range(NKV):
                    q = qT[:, b, g].rearrange("p h t -> p (h t)")
                    nc.tensor.matmul(psS[0:R, g, 0:WIN], q, kT[b % 2][:, g, :], start=True, stop=True)
                    mm = nc.tensor.matmul(psS[0:R, g, WIN:KN], q, kn[:, g, b * DEC_T:(b + 1) * DEC_T], start=True, stop=True)
                mm.then_inc(scores, 1)
            pe.wait_ge(probs, 1)
            pe.wait_ge(v_new_loaded, 16)
            for b in range(DEC_B):
                if b:
                    pe.wait_ge(p_moved, 2 * b)
                for g in range(NKV):
                    nc.tensor.transpose(psP[:, g, :], S[:, b, g, 0:WIN], ident[0:R, 0:R])
                    mm = nc.tensor.transpose(psN[0:DEC_T, g, :], S[:, b, g, WIN:KN], ident[0:R, 0:R])
                mm.then_inc(p_turned, 1)
                pe.wait_ge(p_moved, 2 * b + 2)
                if b:
                    pe.wait_ge(out_moved, 2 * b)
                for g in range(NKV):
                    nc.tensor.matmul(psO[0:HD, g, :], vc[:, b, g * HD:(g + 1) * HD], PT[b % 2][:, g, :], start=True, stop=False)
                    mm = nc.tensor.matmul(psO[0:HD, g, :], vn[:, b, g * HD:(g + 1) * HD], PN[b % 2][:, g, :], start=False, stop=True)
                mm.then_inc(weighed, 1)


def conv_stage(nc, d, hT, yT, w, w_merge):
    with ExitStack() as ctx:
        m = Memory(nc, ctx)
        csb = [m.sb(f"c_gate{b}", [P, CB]) for b in range(2)]
        u = [m.sb(f"u{b}", [P, 2 + SEQ]) for b in range(2)]
        us = [m.sb(f"u_s{b}", [P, DEC_B, 2 + DEC_T]) for b in range(2)]
        y = m.sb("y", [P, SEQ])
        ys = m.sb("y_s", [P, DEC_B, DEC_T])
        cw = m.sb("conv_w", [P, DK, 3])
        state = m.sb("state", [P, DK, DEC_B, 2])
        new = m.sb("conv_new", [P, DK, 2 + 2 * DEC_B])
        psB = [m.ps(f"psB{j}", [P, 512]) for j in range(3)]
        psC = m.ps("psC", [P, 512])
        psX = [m.ps(f"psX{b}", [P, 512]) for b in range(2)]
        s = m.sem
        w_loaded = d["w_bcx_loaded"]
        small_loaded, zeroed = s("small_loaded"), s("zeroed")
        c_mult, c_moved, x_mult, u_ready, b_mult = s("c_mult"), s("c_moved"), s("x_mult"), s("u_ready"), s("b_mult")
        conv_step, y_ready, state_placed, tail_saved, tail_stored = s("conv_step"), s("y_ready"), s("state_placed"), s("tail_saved"), s("tail_stored")
        block = ctx.enter_context(nc.Block())
        PAIRS = DK // 2
        TAIL = SEQ - 2 * CB

        @block.sync
        def _(sp):
            for dst, name in ((cw, "conv_wT"), (state, "stateT")):
                sp.dma_start(dst[:], d[name]).then_inc(small_loaded, 16)
            with sp.Fori(1, PAIRS) as i:
                for b in range(2):
                    sp.wait_ge(b_mult, 3 * (2 * i + b - 1))
                    sp.dma_start(w[b], d["w_bcx"][2 * i + b]).then_inc(w_loaded[b], 16)
            for b in range(2):
                sp.wait_ge(b_mult, 3 * (DK - 1 + b))
                sp.dma_start(w_merge[b], d["w_merge"][b]).then_inc(d["w_merge_loaded"][b], 16)
            sp.wait_ge(tail_saved, 2 * DK)
            sp.dma_start(d["conv_new"], new[:]).then_inc(tail_stored, 16)
            sp.wait_ge(tail_stored, 16)

        def pairs(eng, body):
            for b in range(2):
                body(b, b, 0)
            with eng.Fori(1, PAIRS) as i:
                for b in range(2):
                    body(2 * i + b, b, i)

        @block.tensor
        def _(pe):
            def chunk(c, b, i):
                pe.wait_ge(w_loaded[b], 16 * (i + 1))
                for j in range(3):
                    cols = slice(j * CB, (j + 1) * CB)
                    n = 3 * c + j
                    for part, ps, sem in ((1, psC, c_mult), (2, psX[(3 * b + j) % 2], x_mult), (0, psB[j], b_mult)):
                        if part == 1 and not (isinstance(n, int) and n == 0):
                            pe.wait_ge(c_moved, n)
                        if part == 2 and not (isinstance(n, int) and n < 2):
                            pe.wait_ge(u_ready, n - 1)
                        if part == 0 and not (isinstance(c, int) and c == 0):
                            pe.wait_ge(y_ready, 4 * c)
                        for k in range(DK):
                            mm = nc.tensor.matmul(ps[:, 0:CB], w[b][:, part, k, :], hT[:, k, cols], start=(k == 0), stop=(k == DK - 1))
                        mm.then_inc(sem, 1)
            pairs(pe, chunk)

        @block.scalar
        def _(act):
            def chunk(c, b, i):
                for j in range(3):
                    n = 3 * c + j
                    act.wait_ge(c_mult, n + 1)
                    if not (isinstance(n, int) and n < 2):
                        act.wait_ge(u_ready, n - 1)
                    nc.scalar.activation(csb[(3 * b + j) % 2][:], psC[:, 0:CB], ACT.Copy).then_inc(c_moved, 1)
            pairs(act, chunk)

        @block.gpsimd
        def _(pool):
            for b in range(2):
                nc.gpsimd.memset(u[b][:, 0:2], 0.0).then_inc(zeroed, 1)
            hold(pool, small_loaded, 32)

            def chunk(c, b, i):
                if not (isinstance(c, int) and c < 2):
                    hold(pool, y_ready, 4 * (c - 1))
                nc.gpsimd.tensor_copy(us[b][:, :, 0:2], state[:, bass.ds(c, 1) if not isinstance(c, int) else slice(c, c + 1), :, :].rearrange("p a b j -> p (a b) j")).then_inc(state_placed, 1)
                hold(pool, u_ready, 3 * (c + 1))
                one = bass.ds(c, 1) if not isinstance(c, int) else slice(c, c + 1)
                nc.gpsimd.tensor_copy(new[:, one, 0:2].rearrange("p a j -> p (a j)"), u[b][:, SEQ:SEQ + 2]).then_inc(tail_saved, 1)
                nc.gpsimd.tensor_copy(new[:, one, 2:2 + 2 * DEC_B].rearrange("p a (b j) -> p (a b) j", j=2), us[b][:, :, DEC_T:DEC_T + 2]).then_inc(tail_saved, 1)
            pairs(pool, chunk)

        @block.vector
        def _(dve):
            dve.wait_ge(small_loaded, 32)
            dve.wait_ge(zeroed, 2)

            def chunk(c, b, i):
                first = isinstance(c, int) and c == 0
                st = Steps(dve, conv_step, base=7 * c)
                if not (isinstance(c, int) and c < 2):
                    dve.wait_ge(tail_saved, 2 * (c - 1))
                for j in range(3):
                    n = 3 * c + j
                    dve.wait_ge(c_moved, n + 1)
                    dve.wait_ge(x_mult, n + 1)
                    cg, xp = csb[(3 * b + j) % 2], psX[(3 * b + j) % 2]
                    width = CB if j < 2 else TAIL
                    ins = nc.vector.tensor_tensor(u[b][:, 2 + j * CB:2 + j * CB + width], xp[:, 0:width], cg[:, 0:width], ALU.mult)
                    if j == 2:
                        st.did(ins)
                        ins = nc.vector.tensor_tensor(us[b][:, :, 2:2 + DEC_T], xp[:, TAIL:CB].rearrange("p (b t) -> p b t", t=DEC_T),
                                                      cg[:, TAIL:CB].rearrange("p (b t) -> p b t", t=DEC_T), ALU.mult)
                    ins.then_inc(u_ready, 1)
                dve.wait_ge(u_ready, 3 * (c + 1))
                st.wait()
                dve.wait_ge(state_placed, c + 1)
                if not first:
                    dve.wait_ge(y_ready, 4 * c)
                one = bass.ds(c, 1) if not isinstance(c, int) else slice(c, c + 1)
                tap = lambda j: cw[:, one, j:j + 1].rearrange("p a j -> p (a j)")
                for o, ext, width in ((y[:], lambda j: u[b][:, j:j + SEQ], 0), (ys[:], lambda j: us[b][:, :, j:j + DEC_T], 0)):
                    st.did(nc.vector.tensor_scalar(o, ext(0), tap(0), None, ALU.mult))
                    for j in (1, 2):
                        st.wait()
                        st.did(nc.vector.scalar_tensor_tensor(o, ext(j), tap(j), o, ALU.mult, ALU.add))
                st.wait()
                dve.wait_ge(b_mult, 3 * (c + 1))
                for j in range(3):
                    width = CB if j < 2 else TAIL
                    nc.vector.tensor_tensor(yT[:, one, j * CB:j * CB + width].rearrange("p a n -> p (a n)"), y[:, j * CB:j * CB + width], psB[j][:, 0:width], ALU.mult).then_inc(y_ready, 1)
                nc.vector.tensor_tensor(yT[:, one, SEQ:T].rearrange("p a n -> p (a n)"), ys[:].rearrange("p b t -> p (b t)"), psB[2][:, TAIL:CB], ALU.mult).then_inc(y_ready, 1)
            pairs(dve, chunk)


def merge_stage(nc, d, hT, attnT, yT, w, w_out, mergedT):
    with ExitStack() as ctx:
        m = Memory(nc, ctx)
        th = [[m.sb(f"th{g}{b}", [P, CB]) for b in range(2)] for g in range(2)]
        tmp = m.sb("tmp", [P, CB])
        ps = [[m.ps(f"psm{n}{b}", [P, 512]) for b in range(2)] for n in range(4)]
        s = m.sem
        w_loaded = d["w_merge_loaded"]
        gate_mult, proj_mult, gate_tanh, part_step, merged = s("gate_mult"), s("proj_mult"), s("gate_tanh"), s("part_step"), s("merged")
        block = ctx.enter_context(nc.Block())
        PAIRS = DK // 2

        def pairs(eng, body):
            for b in range(2):
                body(b, b, 0)
            with eng.Fori(1, PAIRS) as i:
                for b in range(2):
                    body(2 * i + b, b, i)

        @block.sync
        def _(sp):
            with sp.Fori(0, PAIRS - 1) as i:
                for b in range(2):
                    sp.wait_ge(merged, 3 * (2 * i + b + 1))
                    sp.dma_start(w[b], d["w_merge"][2 * i + b + 2]).then_inc(w_loaded[b], 16)
            for b in range(2):
                sp.wait_ge(merged, 3 * (DK - 1 + b))
                sp.dma_start(w_out[b], d["w_out"][:, b * DK // 2:(b + 1) * DK // 2, :]).then_inc(d["w_out_loaded"], 16)

        @block.tensor
        def _(pe):
            def chunk(c, b, i):
                pe.wait_ge(w_loaded[b], 16 * (i + 1))
                for j in range(3):
                    cols = slice(j * CB, (j + 1) * CB)
                    n = 3 * c + j
                    if not (isinstance(n, int) and n < 2):
                        pe.wait_ge(merged, n - 1)
                    for part, src in ((0, hT), (2, hT), (1, attnT), (3, yT)):
                        for k in range(DK):
                            mm = nc.tensor.matmul(ps[part][(3 * b + j) % 2][:, 0:CB], w[b][:, part, k, :], src[:, k, cols], start=(k == 0), stop=(k == DK - 1))
                        mm.then_inc(gate_mult if src is hT else proj_mult, 1)
            pairs(pe, chunk)

        @block.scalar
        def _(act):
            def chunk(c, b, i):
                for j in range(3):
                    n = 3 * c + j
                    if not (isinstance(n, int) and n < 2):
                        act.wait_ge(merged, n - 1)
                    for g in range(2):
                        act.wait_ge(gate_mult, 2 * n + g + 1)
                        nc.scalar.activation(th[g][(3 * b + j) % 2][:], ps[2 * g][(3 * b + j) % 2][:, 0:CB], ACT.Tanh, scale=0.5).then_inc(gate_tanh, 1)
            pairs(act, chunk)

        @block.vector
        def _(dve):
            def chunk(c, b, i):
                for j in range(3):
                    n = 3 * c + j
                    q = (3 * b + j) % 2
                    st = Steps(dve, part_step, base=2 * n)
                    cols = slice(j * CB, (j + 1) * CB)
                    if not (isinstance(n, int) and n == 0):
                        dve.wait_ge(merged, n)
                    dve.wait_ge(gate_tanh, 2 * n + 2)
                    dve.wait_ge(proj_mult, 2 * n + 1)
                    st.did(nc.vector.scalar_tensor_tensor(tmp[:], th[0][q][:], 1.0, ps[1][q][:, 0:CB], ALU.add, ALU.mult))
                    dve.wait_ge(proj_mult, 2 * n + 2)
                    st.did(nc.vector.scalar_tensor_tensor(th[1][q][:], th[1][q][:], 1.0, ps[3][q][:, 0:CB], ALU.add, ALU.mult))
                    st.wait()
                    one = slice(c, c + 1) if isinstance(c, int) else bass.ds(c, 1)
                    nc.vector.tensor_tensor(mergedT[:, one, cols].rearrange("p a n -> p (a n)"), tmp[:], th[1][q][:], ALU.add).then_inc(merged, 1)
            pairs(dve, chunk)


def residual_stage(nc, d, ident, mergedT, w, w_pq):
    with ExitStack() as ctx:
        m = Memory(nc, ctx)
        rows_of = {n: m.sb(n, [P, D]) for n in ("gt1", "g2", "sh2")}
        mT = [m.sb(f"mT{b}", [P, DK, P]) for b in range(2)]
        x = [m.sb(f"xr{b}", [P, D]) for b in range(2)]
        x1 = [m.sb(f"x1{b}", [P, D]) for b in range(2)]
        h2 = [m.sb(f"h2{b}", [P, D]) for b in range(2)]
        h2T = [m.sb(f"h2T{b}", [P, DK, P]) for b in range(2)]
        ss = m.sb("ss2", [P, 1])
        rs = m.sb("rs2", [P, 1])
        half = m.sb("neg_half2", [P, 1])
        psY = [m.ps(f"psY{b}", [P, D]) for b in range(2)]
        psT = m.ps("psT2", [P, DK, P])
        s = m.sem
        rows_loaded, mT_ready = s("rows2_loaded"), s("mT_ready")
        in_loaded = [s(f"in_loaded{b}") for b in range(2)]
        half_set, y_mult, x1_step, x1_ready, x1_squared = s("half_set"), s("y_mult"), s("x1_step"), s("x1_ready"), s("x1_squared")
        rms_step, rms, h2_step, h2_ready, turned, h2T_ready = s("rms2_step"), s("rms2"), s("h2_step"), s("h2_ready"), s("turned"), s("h2T_ready")
        out_stored = [s(f"out_stored{b}") for b in range(2)]
        block = ctx.enter_context(nc.Block())

        def tiles(eng, body):
            for b in range(2):
                body(b, b, P, 0)
            with eng.Fori(1, NT // 2) as k:
                for b in range(2):
                    body(2 * k + b, b, P, k)
            body(NT, 0, NS, NT // 2)

        early = lambda i, n: isinstance(i, int) and i < n

        @block.sync
        def _(sp):

            def load(i, b, rows):
                if not early(i, 2):
                    sp.wait_ge(h2T_ready, i - 1)
                sp.dma_start(x[b][0:rows, :], d["x"][tile_rows(i, rows), :]).then_inc(in_loaded[b], 16)

            def store(i, b, rows):
                sp.wait_ge(h2T_ready, i + 1)
                sp.dma_start(d["x1"][tile_rows(i, rows), :], x1[b][0:rows, :]).then_inc(out_stored[b], 16)
                sp.dma_start(d["h2"][tile_rows(i, rows), :], h2[b][0:rows, :]).then_inc(out_stored[b], 16)
                one = slice(i, i + 1) if isinstance(i, int) else bass.ds(i, 1)
                dst = d["h2T"][one, :, :].rearrange("a p (k n) -> p (a k) n", n=P)
                sp.dma_start(dst[:, :, 0:rows], h2T[b][:, :, 0:rows]).then_inc(out_stored[b], 16)

            load(0, 0, P)
            load(1, 1, P)
            for n, col in (("gt1", 2), ("g2", 4), ("sh2", 3)):
                sp.dma_start(rows_of[n][:], d["modrows"][0:1, col * D:(col + 1) * D].partition_broadcast(P).rearrange("p a n -> p (a n)")).then_inc(rows_loaded, 16)
            sp.dma_start(w_pq, d["w_pq"]).then_inc(d["w_peer_loaded"], 16)
            with sp.Fori(0, NT // 2 - 1) as k:
                for b in range(2):
                    store(2 * k + b, b, P)
                    load(2 * k + b + 2, b, P)
            store(NT - 2, 0, P)
            load(NT, 0, NS)
            store(NT - 1, 1, P)
            for n, col in (("gt1", 2), ("g2", 4), ("sh2", 3)):
                for q in range(DEC_B):
                    sp.dma_start(rows_of[n][q * DEC_T:(q + 1) * DEC_T, :],
                                 d["modrows"][1 + q:2 + q, col * D:(col + 1) * D].partition_broadcast(DEC_T).rearrange("p a n -> p (a n)")).then_inc(rows_loaded, 16)
            store(NT, 0, NS)
            sp.wait_ge(out_stored[0], 48 * (NT // 2 + 1))
            sp.wait_ge(out_stored[1], 48 * (NT // 2))

        @block.tensor
        def _(pe):
            pe.wait_ge(d["w_out_loaded"], 32)
            pe.wait_ge(half_set, 1)

            def mult(i, b, rows, k):
                pe.wait_ge(mT_ready, i + 1)
                if not early(i, 2):
                    pe.wait_ge(x1_ready, i - 1)
                for c in range(2):
                    for kk in range(DK):
                        mm = nc.tensor.matmul(psY[b][0:rows, c * 512:(c + 1) * 512], mT[b][:, kk, 0:rows], w[2 * kk // DK][:, kk % (DK // 2), c * 512:(c + 1) * 512],
                                              start=(kk == 0), stop=(kk == DK - 1))
                mm.then_inc(y_mult, 1)

            def turn(i, b, rows):
                pe.wait_ge(h2_ready, i + 1)
                if not early(i, 1):
                    pe.wait_ge(h2T_ready, i)
                for kk in range(DK):
                    mm = nc.tensor.transpose(psT[:, kk, 0:rows], h2[b][0:rows, kk * P:(kk + 1) * P], ident[0:rows, 0:rows])
                mm.then_inc(turned, 1)

            def pair(k, last):
                mult(2 * k + 1, 1, P, k)
                turn(2 * k, 0, P)
                mult(2 * k + 2, 0, NS if last else P, k + 1)
                turn(2 * k + 1, 1, P)

            mult(0, 0, P, 0)
            pair(0, False)
            with pe.Fori(1, NT // 2 - 1) as k:
                pair(k, False)
            pair(NT // 2 - 1, True)
            turn(NT, 0, NS)

        @block.scalar
        def _(act):
            def place(i, b, rows):
                if not early(i, 2):
                    act.wait_ge(y_mult, i - 1)
                cols = slice(SEQ, T) if rows == NS else tile_cols(i)
                nc.scalar.activation(mT[b][:, :, 0:rows], mergedT[:, :, cols], ACT.Copy).then_inc(mT_ready, 1)

            place(0, 0, P)
            place(1, 1, P)

            def body(i, b, rows, k):
                act.wait_ge(x1_ready, i + 1)
                if not (isinstance(i, int) and i >= NT - 1):
                    place(i + 2, b, NS if isinstance(i, int) and i == NT - 2 else P)
                nc.scalar.activation(h2[b][0:rows, :], x1[b][0:rows, :], ACT.Square, accum_out=ss[0:rows, :]).then_inc(x1_squared, 1)
                act.wait_ge(turned, i + 1)
                nc.scalar.activation(h2T[b][:, :, 0:rows], psT[:, :, 0:rows], ACT.Copy).then_inc(h2T_ready, 1)
            for b in range(2):
                body(b, b, P, 0)
            with act.Fori(1, NT // 2 - 1) as k:
                for b in range(2):
                    body(2 * k + b, b, P, k)
            for b in range(2):
                body(NT - 2 + b, b, P, NT // 2 - 1)
            body(NT, 0, NS, NT // 2)

        @block.gpsimd
        def _(pool):
            nc.gpsimd.memset(half[:], -0.5).then_inc(half_set, 1)
            hold(pool, half_set, 1)

            def body(i, b, rows, k):
                hold(pool, x1_squared, i + 1)
                if not early(i, 1):
                    hold(pool, h2_ready, i)
                nc.gpsimd.tensor_scalar(rs[0:rows, :], ss[0:rows, :], 1.0 / D, EPS, ALU.mult, ALU.add).then_inc(rms_step, 1)
                hold(pool, rms_step, i + 1)
                nc.gpsimd.tensor_tensor(rs[0:rows, :], rs[0:rows, :], half[0:rows, :], ALU.pow).then_inc(rms, 1)
            tiles(pool, body)

        @block.vector
        def _(dve):
            dve.wait_ge(rows_loaded, 48)

            def body(i, b, rows, k):
                r = slice(0, rows)
                dve.wait_ge(y_mult, i + 1)
                dve.wait_ge(in_loaded[b], 16 * (k + 1))
                if rows == NS:
                    dve.wait_ge(rows_loaded, 48 * (1 + DEC_B))
                if not early(i, 2):
                    dve.wait_ge(out_stored[b], 48 * k)
                nc.vector.scalar_tensor_tensor(x1[b][r, :], psY[b][r, :], 0.5, rows_of["gt1"][r, :], ALU.mult, ALU.mult).then_inc(x1_step, 1)
                dve.wait_ge(x1_step, i + 1)
                nc.vector.tensor_tensor(x1[b][r, :], x1[b][r, :], x[b][r, :], ALU.add).then_inc(x1_ready, 1)
                dve.wait_ge(rms, i + 1)
                nc.vector.scalar_tensor_tensor(h2[b][r, :], x1[b][r, :], rs[r, :], rows_of["g2"][r, :], ALU.mult, ALU.mult).then_inc(h2_step, 1)
                dve.wait_ge(h2_step, i + 1)
                nc.vector.tensor_tensor(h2[b][r, :], h2[b][r, :], rows_of["sh2"][r, :], ALU.add).then_inc(h2_ready, 1)
            tiles(dve, body)


def peer_stage(nc, d, ident, w):
    with ExitStack() as ctx:
        m = Memory(nc, ctx)
        BF16 = mybir.dt.bfloat16
        keys = m.sb("sub_keys", [P, 2 * PH, NKEYS])
        ring = [m.sb(f"rows{r}", [P, 2 * D]) for r in range(RING)]
        diag = [m.sb(f"diag{r}", [P, P]) for r in range(RING)]
        idx = [m.sb(f"idx{b}", [P, TOPK], U32) for b in range(2)]
        ids = m.sb("expert_ids", [P, PH, TOPK], U32)
        gates = m.sb("half_gates", [P, PH, TOPK])
        gcur = [m.sb(f"gates_now{b}", [P, TOPK]) for b in range(2)]
        gt2, x1, y, h2n, h2c = (m.sb(n, [P, D]) for n in ("gt2", "x1_now", "y_out", "h2_next", "h2_now"))
        h2T = m.sb("h2T_now", [P, DK, P])
        q_sb = m.sb("q_sb", [P, 2 * PHALF])
        qT = m.sb("qT_p", [P, 2, P])
        sc = m.sb("key_scores", [P, 2, NKEYS])
        sc2 = m.sb("key_scores_rest", [P, 2, NKEYS])
        top = m.sb("top_scores", [P, 2, TOPK])
        topi = m.sb("top_keys", [P, 2, TOPK], U32)
        topf = m.sb("top_keys_f", [P, 2, TOPK])
        cand = m.sb("pair_scores", [P, TOPK, TOPK])
        cand2 = m.sb("pair_scores_rest", [P, TOPK * TOPK])
        cs = m.sb("best_scores", [P, TOPK])
        ci = m.sb("best_pairs", [P, TOPK], U32)
        pair = m.sb("pair_halves", [P, 2, TOPK], U32)
        iota = m.sb("iota16", [P, TOPK])
        pick = m.sb("pick", [P, 2, TOPK, TOPK])
        picked = m.sb("picked", [P, 2, TOPK])
        nmax, esum, rsum = m.sb("neg_best", [P, 1]), m.sb("exp_sum", [P, 1]), m.sb("exp_rsum", [P, 1])
        ex = m.sb("exp_best", [P, TOPK])
        a, g1, th, co = ([m.sb(f"{n}{b}", [P, BATCH]) for b in range(2)] for n in ("dots", "poly", "tanh", "coef"))
        zeros = m.sb("zeros", [P, 512], BF16)
        ids_s, gates_s = m.sb("expert_ids_s", [P, 2, TOPK], U32), m.sb("half_gates_s", [P, 2, TOPK])
        fold = m.sb("fold", [P, NS])
        acc = m.ps("acc_peer", [P, D])
        psq, psT, pss = m.ps("ps_q", [P, 2 * PHALF]), m.ps("ps_qT", [P, 2, P]), m.ps("ps_scores", [P, 2, NKEYS])
        s = m.sem
        w_loaded = d["w_peer_loaded"]
        small_loaded, h2T_loaded, h2_loaded, x1_loaded, y_stored = s("small3_loaded"), s("h2T_loaded"), s("h2_loaded"), s("x1_loaded"), s("y_stored")
        zero_set = s("zero_set")
        q_mult, q_moved, q_turned, qT_moved, key_mult, keys_moved = s("q_mult"), s("q_moved3"), s("q_turned3"), s("qT_moved"), s("key_mult"), s("keys_moved")
        top_step, pick_step, softmax_in, exp_done, ids_ready, gates_ready = s("top_step"), s("pick_step"), s("softmax_in"), s("exp_done"), s("ids_ready"), s("gates_ready")
        staged, slot_free, dotted, gelu_step, gelu_in, tanh_done, coef_ready, diag_ready = s("staged"), s("slot_free"), s("dotted"), s("gelu_step"), s("gelu_in"), s("tanh_done"), s("coef_ready"), s("diag_ready")
        gathered = [s(f"gathered{r}") for r in range(RING)]
        folded = s("folded")
        h2_taken, y_step, y_ready = s("h2_taken"), s("y_step"), s("y_ready")
        block = ctx.enter_context(nc.Block())
        NB = TOPK // BATCH

        FOLDS = P // NS

        def schedule(eng, unit, begin=None, end=None):
            def tile(t, rows, next_rows):
                if begin and rows:
                    begin(t, rows)
                with eng.Fori(0, PH // 2) as hp:
                    for b in range(2):
                        unit(PH * t + 2 * hp + b, 2 * hp + b, b, rows, next_rows, False)
                if end and rows:
                    end(t, rows)
            tile(-1, None, P)
            with eng.Fori(0, NT - 1) as t:
                tile(t, P, P)
            tile(NT - 1, P, NS)
            if begin:
                begin(NT, P)
            for b in range(2):
                unit(PH * NT + b, b, b, P, None, True)
            if end:
                end(NT, NS)

        @block.sync
        def _(sp):
            sp.dma_start(h2T[:], d["h2T"][0].rearrange("p (k n) -> p k n", n=P)).then_inc(h2T_loaded, 16)
            sp.dma_start(keys[:], d["subkT"]).then_inc(small_loaded, 16)
            sp.dma_start(iota[:], d["iota"].partition_broadcast(P)).then_inc(small_loaded, 16)
            sp.dma_start(h2n[:], d["h2"][0:P, :]).then_inc(h2_loaded, 16)
            sp.dma_start(x1[:], d["x1"][0:P, :]).then_inc(x1_loaded, 16)
            sp.dma_start(gt2[:], d["modrows"][0:1, 5 * D:6 * D].partition_broadcast(P).rearrange("p a n -> p (a n)")).then_inc(small_loaded, 16)
            sp.dma_start(fold[:], d["fold"]).then_inc(small_loaded, 16)
            sp.wait_ge(q_mult, PH)
            sp.dma_start(h2T[:], d["h2T"][1].rearrange("p (k n) -> p k n", n=P)).then_inc(h2T_loaded, 16)

            def tile(t, next_rows, rows_after):
                sp.wait_ge(h2_taken, t + 1)
                for f in range(1 if next_rows == P else FOLDS):
                    sp.dma_start(h2n[f * NS:f * NS + next_rows, :], d["h2"][tile_rows(t + 1, next_rows), :]).then_inc(h2_loaded, 16)
                if rows_after:
                    sp.wait_ge(q_mult, PH * (t + 2))
                    one = slice(t + 2, t + 3) if isinstance(t, int) else bass.ds(t + 2, 1)
                    src = d["h2T"][one, :, :].rearrange("a p (k n) -> p (a k) n", n=P)
                    sp.dma_start(h2T[:, :, 0:rows_after], src[:, :, 0:rows_after]).then_inc(h2T_loaded, 16)
                if next_rows == NS:
                    sp.wait_ge(ids_ready, PH * (NT + 1))
                    sp.wait_ge(gates_ready, PH * (NT + 1))
                    for f in range(FOLDS):
                        for dst, src in ((ids_s, ids), (gates_s, gates)):
                            sp.dma_start(dst[f * NS:(f + 1) * NS, :, :], src[0:NS, 2 * f:2 * f + 2, :]).then_inc(folded, 16)
                sp.wait_ge(y_ready, t + 1)
                sp.dma_start(d["y"][tile_rows(t, P), :], y[:]).then_inc(y_stored, 16)
                sp.dma_start(x1[0:next_rows, :], d["x1"][tile_rows(t + 1, next_rows), :]).then_inc(x1_loaded, 16)

            with sp.Fori(0, NT - 2) as t:
                tile(t, P, P)
            tile(NT - 2, P, NS)
            tile(NT - 1, NS, None)
            for q in range(DEC_B):
                sp.dma_start(gt2[q * DEC_T:(q + 1) * DEC_T, :],
                             d["modrows"][1 + q:2 + q, 5 * D:6 * D].partition_broadcast(DEC_T).rearrange("p a n -> p (a n)")).then_inc(small_loaded, 16)
            sp.wait_ge(y_ready, NT + 1)
            sp.dma_start(d["y"][SEQ:T, :], y[0:NS, :]).then_inc(y_stored, 16)
            sp.wait_ge(y_stored, 16 * (NT + 2))

        @block.gpsimd
        def _(pool):
            nc.gpsimd.memset(zeros[:], 0.0).then_inc(zero_set, 1)

            def unit(n, h, b, last):
                if last:
                    hold(pool, folded, 32 * FOLDS)
                else:
                    hold(pool, ids_ready, n + 1)
                hold(pool, dotted, TOPK * (n + 1))
                src = ids_s[:, h:h + 1, :] if last else ids[:, bass.ds(h, 1), :]
                nc.gpsimd.tensor_copy(idx[b][:], src.rearrange("p a k -> p (a k)")).then_inc(staged, 1)
                hold(pool, staged, n + 1)
                for j in range(TOPK):
                    hold(pool, slot_free, TOPK * n + j + 1)
                    nc.gpsimd.indirect_dma_start(ring[j % RING][:], None, d["uv"],
                                                 bass.IndirectOffsetOnAxis(ap=idx[b][:, j:j + 1], axis=0)).then_inc(gathered[j % RING], 16)

            with pool.Fori(0, NT) as t:
                with pool.Fori(0, PH // 2) as hp:
                    for b in range(2):
                        unit(PH * t + 2 * hp + b, 2 * hp + b, b, False)
            for b in range(2):
                unit(PH * NT + b, b, b, True)

        @block.scalar
        def _(act):
            act.wait_ge(small_loaded, 64)
            act.sem_inc(y_stored, 16)
            act.sem_inc(slot_free, RING)
            act.sem_inc(dotted, 2 * TOPK)

            def weigh(n, q, last):
                bq = q % 2
                act.wait_ge(gelu_in, NB * n + q + 1)
                nc.scalar.activation(th[bq][:], g1[bq][:], ACT.Tanh, scale=GELU_A).then_inc(tanh_done, 1)
                act.wait_ge(coef_ready, NB * n + q + 1)
                for k in range(BATCH):
                    r = (q * BATCH + k) % RING
                    nc.scalar.activation(diag[r][:, 0:NS] if last else diag[r][:], fold[:] if last else ident[:], ACT.Copy, scale=co[bq][:, k:k + 1]).then_inc(diag_ready, 1)

            def unit(n, h, b, rows, next_rows, last):
                m_ = n + PH

                def move(dst, src, full, sem):
                    act.wait_ge(full, m_ + 1)
                    nc.scalar.activation(dst, src, ACT.Copy).then_inc(sem, 1)
                for q in range(NB):
                    if rows:
                        weigh(n, q, last)
                    if next_rows:
                        r = slice(0, next_rows)
                        if q == 0:
                            move(q_sb[r, :], psq[r, :], q_mult, q_moved)
                        elif q == 1:
                            move(qT[:, :, r], psT[:, :, r], q_turned, qT_moved)
                        elif q == 2:
                            move(sc[r], pss[r], key_mult, keys_moved)
                        else:
                            act.wait_ge(softmax_in, m_ + 1)
                            nc.scalar.activation(ex[r, :], cs[r, :], ACT.Exp, bias=nmax[r, :], accum_out=esum[r, :]).then_inc(exp_done, 1)
            schedule(act, unit)

        @block.tensor
        def _(pe):
            pe.wait_ge(w_loaded, 16)
            pe.wait_ge(small_loaded, 64)
            pe.wait_ge(zero_set, 1)

            def begin(t, rows):
                pe.wait_ge(y_step, t + 1)
                for c in range(2):
                    nc.tensor.matmul(acc[:, c * 512:(c + 1) * 512], zeros[:, 0:P], zeros[:], start=True, stop=False, skip_group_check=True)

            def unit(n, h, b, rows, next_rows, last):
                m_ = n + PH
                cols = bass.ds(h * 2 * PHALF, 2 * PHALF)
                for q in range(NB):
                    if next_rows:
                        r = slice(0, next_rows)
                        if q == 0:
                            for k in range(DK):
                                mm = nc.tensor.matmul(psq[r, :], h2T[:, k, r], w[:, k, cols], start=(k == 0), stop=(k == DK - 1))
                            mm.then_inc(q_mult, 1)
                        elif q == 1:
                            hold(pe, q_moved, m_ + 1)
                            for p in range(2):
                                mm = nc.tensor.transpose(psT[:, p, r], q_sb[r, p * P:(p + 1) * P], ident[r, r])
                            mm.then_inc(q_turned, 1)
                        elif q == 2:
                            pe.wait_ge(qT_moved, m_ + 1)
                            for p in range(2):
                                one = bass.ds(2 * h + p, 1)
                                mm = nc.tensor.matmul(pss[r, p, :], qT[:, p, r], keys[:, one, :].rearrange("p a n -> p (a n)"), start=True, stop=True)
                            mm.then_inc(key_mult, 1)
                    if rows:
                        for k in range(BATCH):
                            j = q * BATCH + k
                            hold(pe, diag_ready, TOPK * n + j + 1)
                            for c in range(2):
                                out = slice(0, NS if last else P)
                                mm = nc.tensor.matmul(acc[out, c * 512:(c + 1) * 512], diag[j % RING][:, out],
                                                      ring[j % RING][:, D + c * 512:D + (c + 1) * 512], start=False, stop=False, skip_group_check=True)
                            mm.then_inc(slot_free, 1)

            def tile(t, rows, next_rows):
                if next_rows:
                    pe.wait_ge(h2T_loaded, 16 * (t + 2))
                if rows:
                    begin(t, rows)
                with pe.Fori(0, PH // 2) as hp:
                    for b in range(2):
                        unit(PH * t + 2 * hp + b, 2 * hp + b, b, rows, next_rows, False)

            tile(-1, None, P)
            with pe.Fori(0, NT - 1) as t:
                tile(t, P, P)
            tile(NT - 1, P, NS)
            begin(NT, P)
            for b in range(2):
                unit(PH * NT + b, b, b, P, None, True)

        @block.vector
        def _(dve):
            dve.wait_ge(small_loaded, 64)
            dve.sem_inc(y_step, 1)
            SMALL = 3
            TOP = 19

            def begin(t, rows):
                dve.wait_ge(h2_loaded, 16 * (NT + FOLDS) if isinstance(t, int) and t == NT else 16 * (t + 1))
                dve.wait_ge(dotted, 2 * TOPK + SLOTS * t)
                nc.vector.tensor_copy(h2c[0:rows, :], h2n[0:rows, :]).then_inc(h2_taken, 1)
                hold(dve, h2_taken, t + 1)

            def end(t, rows):
                r = slice(0, rows)
                if rows == NS:
                    dve.wait_ge(small_loaded, 64 + 16 * DEC_B)
                dve.wait_ge(slot_free, RING + (SLOTS * NT + 2 * TOPK if rows == NS else SLOTS * (t + 1)))
                dve.wait_ge(y_stored, 16 * (t + 1))
                dve.wait_ge(x1_loaded, 16 * (t + 1))
                nc.vector.tensor_tensor(y[r, :], acc[r, :], gt2[r, :], ALU.mult).then_inc(y_step, 1)
                dve.wait_ge(y_step, t + 2)
                nc.vector.tensor_tensor(y[r, :], y[r, :], x1[r, :], ALU.add).then_inc(y_ready, 1)

            def dots(n, b, q, rows):
                r, bq = slice(0, rows), q % 2
                st = Steps(dve, gelu_step, base=(SMALL * NB + 1) * n + 1 + SMALL * q)
                for k in range(BATCH):
                    j = q * BATCH + k
                    u = ring[j % RING][r, 0:D]
                    dve.wait_ge(gathered[j % RING], 16 * ((TOPK // RING) * n + j // RING + 1))
                    nc.vector.tensor_tensor_reduce(u, u, h2c[r, :], 1.0, 0.0, ALU.mult, ALU.add, a[bq][r, k:k + 1]).then_inc(dotted, 1)
                dve.wait_ge(dotted, 2 * TOPK + TOPK * n + (q + 1) * BATCH)
                st.did(nc.vector.tensor_tensor(g1[bq][r, :], a[bq][r, :], a[bq][r, :], ALU.mult))
                st.wait()
                st.did(nc.vector.tensor_scalar(g1[bq][r, :], g1[bq][r, :], GELU_B, 1.0, ALU.mult, ALU.add))
                st.wait()
                nc.vector.tensor_tensor(g1[bq][r, :], g1[bq][r, :], a[bq][r, :], ALU.mult).then_inc(gelu_in, 1)
                dve.wait_ge(tanh_done, NB * n + q + 1)
                st.did(nc.vector.scalar_tensor_tensor(co[bq][r, :], th[bq][r, :], 1.0, a[bq][r, :], ALU.add, ALU.mult))
                st.wait()
                nc.vector.tensor_tensor(co[bq][r, :], co[bq][r, :], gcur[b][r, q * BATCH:(q + 1) * BATCH], ALU.mult).then_inc(coef_ready, 1)

            def choose(m_, h, rows):
                r = slice(0, rows)
                one = bass.ds(h, 1)
                st = Steps(dve, top_step, base=TOP * m_, own=True)
                E8 = slice(0, 8), slice(8, 16)
                hold(dve, keys_moved, m_ + 1)
                for p in range(2):
                    st.did(nc.vector.max(top[r, p, E8[0]], sc[r, p, :]))
                st.wait()
                for p in range(2):
                    st.did(nc.vector.max_index(topi[r, p, E8[0]], top[r, p, E8[0]], sc[r, p, :]))
                    nc_ins = nc.vector.match_replace(sc2[r, p, :], top[r, p, E8[0]], sc[r, p, :], -3.0e38)
                    st.did(nc_ins)
                st.wait()
                for p in range(2):
                    st.did(nc.vector.max(top[r, p, E8[1]], sc2[r, p, :]))
                st.wait()
                for p in range(2):
                    st.did(nc.vector.max_index(topi[r, p, E8[1]], top[r, p, E8[1]], sc2[r, p, :]))
                st.did(nc.vector.tensor_tensor(cand[r], bc(top[r, 0, :].unsqueeze(2), [rows, TOPK, TOPK]),
                                               bc(top[r, 1, :].unsqueeze(1), [rows, TOPK, TOPK]), ALU.add))
                st.wait()
                flat = cand[r].rearrange("p a b -> p (a b)")
                st.did(nc.vector.tensor_copy(topf[r], topi[r]))
                st.did(nc.vector.max(cs[r, E8[0]], flat))
                st.wait()
                st.did(nc.vector.max_index(ci[r, E8[0]], cs[r, E8[0]], flat))
                st.did(nc.vector.match_replace(cand2[r, :], cs[r, E8[0]], flat, -3.0e38))
                st.wait()
                st.did(nc.vector.max(cs[r, E8[1]], cand2[r, :]))
                st.wait()
                nc.vector.tensor_scalar(nmax[r, :], cs[r, 0:1], -1.0, None, ALU.mult).then_inc(softmax_in, 1)
                st.did(nc.vector.max_index(ci[r, E8[1]], cs[r, E8[1]], cand2[r, :]))
                st.wait()
                st.did(nc.vector.tensor_scalar(pair[r, 0, :], ci[r, :], 4, None, ALU.logical_shift_right))
                st.did(nc.vector.tensor_scalar(pair[r, 1, :], ci[r, :], TOPK - 1, None, ALU.bitwise_and))
                assert st.n == TOP, st.n
                return st

            def choose_ids(m_, h, rows, staged_before):
                r = slice(0, rows)
                one = bass.ds(h, 1)
                st = Steps(dve, pick_step, base=4 * m_)
                dve.wait_ge(top_step, TOP * (m_ + 1))
                halves = pair[r].rearrange("p a k -> p (a k)")
                st.did(nc.vector.tensor_tensor(pick[r].rearrange("p a k j -> p (a k) j"), bc(halves.unsqueeze(2), [rows, 2 * TOPK, TOPK]),
                                               bc(iota[r, :].unsqueeze(1), [rows, 2 * TOPK, TOPK]), ALU.is_equal))
                st.wait()
                st.did(nc.vector.tensor_tensor(pick[r], pick[r], bc(topf[r].unsqueeze(2), [rows, 2, TOPK, TOPK]), ALU.mult))
                st.wait()
                st.did(nc.vector.tensor_reduce(picked[r].rearrange("p a k -> p (a k)"), pick[r].rearrange("p a k j -> p (a k) j"), AX, ALU.add))
                st.wait()
                if staged_before:
                    dve.wait_ge(staged, m_ - PH + 1)
                nc.vector.scalar_tensor_tensor(ids[r, one, :].rearrange("p a k -> p (a k)"), picked[r, 0, :], float(NKEYS), picked[r, 1, :],
                                               ALU.mult, ALU.add).then_inc(ids_ready, 1)
                dve.wait_ge(exp_done, m_ + 1)
                st.did(nc.vector.reciprocal(rsum[r, :], esum[r, :]))
                st.wait()
                nc.vector.tensor_scalar(gates[r, one, :].rearrange("p a k -> p (a k)"), ex[r, :], rsum[r, :], 0.5, ALU.mult, ALU.mult).then_inc(gates_ready, 1)

            def unit(n, h, b, rows, next_rows, last):
                m_ = n + PH
                if rows:
                    if last:
                        dve.wait_ge(folded, 32 * FOLDS)
                    else:
                        dve.wait_ge(gates_ready, n + 1)
                    src = gates_s[:, h:h + 1, :] if last else gates[:, bass.ds(h, 1), :]
                    g = Steps(dve, gelu_step, base=(SMALL * NB + 1) * n)
                    g.did(nc.vector.tensor_copy(gcur[b][:], src.rearrange("p a k -> p (a k)")))
                    g.wait()
                    for q in range(NB):
                        dots(n, b, q, rows)
                if next_rows:
                    choose(m_, h, next_rows)
                    choose_ids(m_, h, next_rows, rows is not None)
            schedule(dve, unit, begin, end)


def build(nc, ins, outs):
    d = dict(ins)
    d.update(outs)

    def scratch(name, shape):
        return nc.dram_tensor(name, shape, F32, kind="Internal").ap()

    d["modrows"] = scratch("modrows", (1 + DEC_B, NMOD * 512))
    d["x1"] = scratch("x1_d", (T, D))
    d["h2"] = scratch("h2_d", (T, D))
    d["h2T"] = scratch("h2T_d", (NT + 1, P, DK * P))
    with ExitStack() as whole:
        def sb(ctx, name, shape):
            return ctx.enter_context(nc.sbuf_tensor(name, shape, F32))

        def sem(name):
            return whole.enter_context(nc.semaphore(name))

        ident = sb(whole, "ident", [P, P])
        wide = sb(whole, "wide", [P, 2, DK * T])
        hT, attnT = (wide[:, n, :].rearrange("p (k n) -> p k n", k=DK) for n in range(2))
        w_pq = wide[:].rearrange("p a n -> p (a n)")[:, 0:DK * PH * 2 * PHALF].rearrange("p (k n) -> p k n", k=DK)
        for name in ("ident_loaded", "qkv_loaded", "w_out_loaded", "w_peer_loaded"):
            d[name] = sem(name)
        for name in ("w_bcx_loaded", "w_merge_loaded"):
            d[name] = [sem(f"{name}{b}") for b in range(2)]
        with ExitStack() as c2:
            qk_s, v_s = sb(c2, "qk_s", [NS, QKW]), sb(c2, "v_s", [NS, KVW])
            with ExitStack() as c3:
                w_qkv = sb(c3, "w_qkv", [P, DK, QKVW])
                mods_stage(nc, d, ident, w_qkv, hT, attnT)
                qkv_attn_stage(nc, d, ident, w_qkv, d["qkv_loaded"], hT, attnT, qk_s, v_s)
            wbuf = [sb(c2, f"w_chunk{b}", [P, 4 * DK * P]) for b in range(2)]
            w_bcx = [w[:, 0:3 * DK * P].rearrange("p (a k n) -> p a k n", a=3, k=DK) for w in wbuf]
            w_merge = [w[:].rearrange("p (a k n) -> p a k n", a=4, k=DK) for w in wbuf]
            w_out = [w[:].rearrange("p (k n) -> p k n", n=D) for w in wbuf]
            sample_stage(nc, d, ident, qk_s, v_s, attnT, w_bcx)
            with ExitStack() as c3:
                mergedT = sb(c3, "mergedT", [P, DK, T])
                with ExitStack() as c4:
                    yT = sb(c4, "yT", [P, DK, T])
                    conv_stage(nc, d, hT, yT, w_bcx, w_merge)
                    merge_stage(nc, d, hT, attnT, yT, w_merge, w_out, mergedT)
                residual_stage(nc, d, ident, mergedT, w_out, w_pq)
        peer_stage(nc, d, ident, w_pq)


def _constants():
    half = HD // 2
    inv = (10000.0 ** (-np.arange(half, dtype=np.float32) / np.float32(half)).astype(np.float64)).astype(np.float32)
    pos = np.concatenate([np.arange(SEQ), np.tile(PAST + np.arange(DEC_T), DEC_B)]).astype(np.float32)
    ang = (pos[:, None] * inv[None, :]).astype(np.float64)
    cos, sin = np.cos(ang).astype(np.float32), np.sin(ang).astype(np.float32)
    q, k = np.arange(P)[:, None], np.arange(2 * P)[None, :]
    band = (k >= q) & (k <= q + WIN)
    masks = np.stack([np.where(band & (k >= P), 0.0, NEG), np.where(band, 0.0, NEG)], axis=1).astype(np.float32)
    tok, j = np.tile(np.arange(DEC_T), GRP)[:, None], np.arange(WIN + DEC_T)[None, :]
    mask_s = np.where((j >= tok) & (j <= tok + WIN), 0.0, NEG).astype(np.float32)
    return dict(ident=np.eye(P, dtype=np.float32), cos=np.concatenate([cos, cos], 1), sin=np.concatenate([-sin, sin], 1),
                mask=masks, mask_s=mask_s, fold=np.tile(np.eye(NS, dtype=np.float32), (P // NS, 1)), iota=np.arange(TOPK, dtype=np.float32))


def _chunks(w):
    return w.reshape(DK, P, -1).transpose(1, 0, 2)


def _by_columns(w):
    return w.reshape(DK, P, DK, P).transpose(2, 1, 0, 3)


def _layout(a):
    w_in = a["w_in"][0]
    at = np.cumsum([0, NH * HD, KVW, KVW, D, D, D, D, D])
    part = lambda n: w_in[:, at[n]:at[n + 1]]
    c_all = np.concatenate([a["c_prompt"], a["c_sample"]])
    stack = lambda *ws: np.stack([_by_columns(w) for w in ws], axis=2)
    return dict(
        x=np.concatenate([a["x_prompt"].reshape(SEQ, D), a["x_sample"].reshape(NS, D)]),
        cT=c_all.T.reshape(DK, P, -1).transpose(1, 0, 2),
        w_ada=a["w_ada"][0].reshape(DK, P, NMOD, 512).transpose(2, 1, 0, 3),
        b_ada=a["b_ada"][0],
        norms=np.stack([a["norm1"][0], a["norm2"][0]]),
        w_qkv=_chunks(w_in[:, :QKVW]),
        gain=np.concatenate([np.tile(a["q_norm"][0], NH), np.tile(a["k_norm"][0], NKV)]),
        sinks=a["attn_sinks"][0],
        sinks_s=np.repeat(a["attn_sinks"][0].reshape(NKV, GRP).T, DEC_T, axis=0),
        cache_k=a["cache_win_k"][0].reshape(DEC_B, WIN, KVW),
        cache_v=a["cache_win_v"][0].reshape(DEC_B, WIN, KVW),
        w_bcx=stack(part(3), part(4), part(5)),
        conv_wT=a["conv_w"][0].T.reshape(DK, P, 3).transpose(1, 0, 2),
        stateT=a["state_conv"][0].reshape(DEC_B, 2, DK, P).transpose(3, 2, 0, 1),
        w_merge=stack(part(6), a["w_attn_o"][0], part(7), a["w_conv_o"][0]),
        w_out=_chunks(a["w_out"][0]),
        w_pq=_chunks(a["w_peer_q"][0]),
        subkT=a["peer_sub_keys"][0].reshape(2 * PH, NKEYS, PHALF).transpose(2, 0, 1),
        uv=np.concatenate([a["peer_u"][0], a["peer_v"][0]], axis=1),
    )


_OUTS = dict(y=(T, D), win_k_p=(P, KVW), win_v_p=(P, KVW), win_k_s=(DEC_B, WIN, KVW), win_v_s=(DEC_B, WIN, KVW),
             conv_new=(P, DK, 2 + 2 * DEC_B))


def kernel(**inputs):
    import concourse.bacc as _bacc
    from concourse.bass_utils import run_bass_kernel_spmd as _run

    nc = _bacc.Bacc("TRN2", target_bir_lowering=False, num_devices=1)
    arrays = {n: np.ascontiguousarray(v) for n, v in _layout({k: np.asarray(v) for k, v in inputs.items()}).items()}
    arrays.update({n: np.ascontiguousarray(v) for n, v in _constants().items()})
    ins = {n: nc.dram_tensor(f"in_{n}", v.shape, F32, kind="ExternalInput").ap() for n, v in arrays.items()}
    outs = {n: nc.dram_tensor(f"out_{n}", shape, F32, kind="ExternalOutput").ap() for n, shape in _OUTS.items()}
    build(nc, ins, outs)
    r = _run(nc, [{f"in_{n}": v for n, v in arrays.items()}], core_ids=[0]).results[0]
    y = r["out_y"]
    new = r["out_conv_new"]
    window = (1, 1, WIN, NKV, HD)
    windows = (1, DEC_B, WIN, NKV, HD)
    conv_p = new[:, :, 0:2].transpose(2, 1, 0).reshape(1, 1, 2, D)
    conv_s = new[:, :, 2:].reshape(P, DK, DEC_B, 2).transpose(2, 3, 1, 0).reshape(1, DEC_B, 2, D)
    return (y[:SEQ].reshape(1, SEQ, D), y[SEQ:].reshape(DEC_B, DEC_T, D),
            r["out_win_k_p"].reshape(window), r["out_win_v_p"].reshape(window), np.ascontiguousarray(conv_p),
            r["out_win_k_s"].reshape(windows), r["out_win_v_s"].reshape(windows), np.ascontiguousarray(conv_s))
```

```python
from contextlib import ExitStack

import numpy as np

import concourse.bass as bass
from concourse import mybir

ALU = mybir.AluOpType
ACT = mybir.ActivationFunctionType
F32 = mybir.dt.float32
F32R = mybir.dt.float32r
U32 = mybir.dt.uint32
AX = mybir.AxisListType.X

P = 128
D = 1024
DK = D // P
SEQ = 1024
DEC_B, DEC_T = 8, 4
NS = DEC_B * DEC_T
T = SEQ + NS
NT = SEQ // P
PAST = 4096
NH, NKV, HD = 16, 4, 64
GRP = NH // NKV
NQK = NH + NKV
WIN = 128
KVW = NKV * HD
QKVW = NH * HD + 2 * KVW
QKW = NQK * HD
CB = T // 3
PH, TOPK, NKEYS, PHALF = 8, 16, 128, 128
EPS = 1e-6
SCALE = HD ** -0.5
NEG = -1e30
GELU_A, GELU_B = 0.7978845608028654, 0.044715
NMOD = 12
RING = 8
BATCH = 4
SLOTS = PH * TOPK


def hold(eng, sem, value):
    eng.wait_ge(sem, value)
    if not isinstance(value, int):
        eng.nop(nofuse=True)


class Steps:

    def __init__(self, eng, sem, base=0, own=False):
        self.eng, self.sem, self.base, self.n, self.own = eng, sem, base, 0, own

    def did(self, ins):
        self.n += 1
        return ins.then_inc(self.sem, 1)

    def wait(self):
        if self.own:
            hold(self.eng, self.sem, self.base + self.n)
        else:
            self.eng.wait_ge(self.sem, self.base + self.n)


def bc(ap, shape):
    return ap.to_broadcast(shape)


def tile_cols(i):
    return bass.ds(i * P, P) if not isinstance(i, int) else slice(i * P, i * P + P)


def tile_rows(i, rows):
    if isinstance(i, int):
        return slice(i * P, i * P + rows)
    return bass.ds(i * P, rows)


class Memory:

    def __init__(self, nc, ctx):
        self.nc, self.ctx = nc, ctx

    def sb(self, name, shape, dt=F32):
        return self.ctx.enter_context(self.nc.sbuf_tensor(name, shape, dt))

    def ps(self, name, shape):
        return self.ctx.enter_context(self.nc.psum_tensor(name, shape, F32))

    def sem(self, name):
        return self.ctx.enter_context(self.nc.semaphore(name))


def mods_stage(nc, d, ident, hT, attnT):
    with ExitStack() as ctx:
        m = Memory(nc, ctx)
        NR = 1 + DEC_B
        cT = m.sb("cT", [P, DK, NR])
        cth = m.sb("cth", [P, DK, NR])
        csil = m.sb("csil", [P, DK, NR])
        early, late = hT.rearrange("p k n -> p (k n)"), attnT.rearrange("p k n -> p (k n)")
        w = [early[:, b * DK * 512:(b + 1) * DK * 512].rearrange("p (k n) -> p k n", k=DK) for b in range(2)]
        bias = m.sb("bias", [NR, NMOD * 512])
        mod = late[0:NR, 0:NMOD * 512]
        norms = late[0:NR, NMOD * 512:NMOD * 512 + 2 * D].rearrange("p (a n) -> p a n", a=2)
        acc = [m.ps(f"acc{b}", [P, 512]) for b in range(2)]
        c_loaded, rows_loaded, c_tanh, silu_ready = m.sem("c_loaded"), m.sem("rows_loaded"), m.sem("c_tanh"), m.sem("silu_ready")
        w_loaded = [m.sem(f"w_ada_loaded{b}") for b in range(2)]
        acc_ready, acc_free, mods_ready, mods_stored = m.sem("acc_ready"), m.sem("acc_free"), m.sem("mods_ready"), m.sem("mods_stored")
        silu_step = m.sem("silu_step")
        block = ctx.enter_context(nc.Block())

        @block.sync
        def _(sp):
            sp.dma_start(cT[:], d["cT"]).then_inc(c_loaded, 16)
            for n in range(2):
                sp.dma_start(w[n], d["w_ada"][n]).then_inc(w_loaded[n], 16)
            sp.dma_start(bias[:], d["b_ada"].partition_broadcast(NR)).then_inc(rows_loaded, 16)
            sp.dma_start(norms, d["norms"].partition_broadcast(NR)).then_inc(rows_loaded, 16)
            with sp.Fori(1, NMOD // 2) as i:
                for b in range(2):
                    sp.wait_ge(acc_ready, 2 * i + b - 1)
                    sp.dma_start(w[b], d["w_ada"][2 * i + b]).then_inc(w_loaded[b], 16)
            sp.dma_start(ident[:], d["ident"]).then_inc(d["ident_loaded"], 16)
            sp.wait_ge(mods_ready, 2)
            sp.dma_start(d["modrows"], mod).then_inc(mods_stored, 16)
            sp.wait_ge(mods_stored, 16)

        @block.scalar
        def _(act):
            act.wait_ge(c_loaded, 16)
            nc.scalar.activation(cth[:], cT[:], ACT.Tanh, scale=0.5).then_inc(c_tanh, 1)

        @block.vector
        def _(dve):
            dve.wait_ge(c_tanh, 1)
            nc.vector.scalar_tensor_tensor(csil[:], cth[:], 1.0, cT[:], ALU.add, ALU.mult).then_inc(silu_step, 1)
            dve.wait_ge(silu_step, 1)
            nc.vector.tensor_scalar(csil[:], csil[:], 0.5, None, ALU.mult).then_inc(silu_ready, 1)
            dve.wait_ge(rows_loaded, 32)
            with dve.Fori(0, NMOD // 2) as i:
                for b in range(2):
                    dve.wait_ge(acc_ready, 2 * i + b + 1)
                    cols = bass.ds((2 * i + b) * 512, 512)
                    nc.vector.tensor_tensor(mod[:, cols], acc[b][0:NR, :], bias[:, cols], ALU.add).then_inc(acc_free, 1)
            dve.wait_ge(acc_free, NMOD)
            for s, first in ((0, D), (1, 4 * D)):
                part = mod[:, first:first + D]
                nc.vector.scalar_tensor_tensor(part, part, 1.0, norms[:, s, :], ALU.add, ALU.mult).then_inc(mods_ready, 1)

        @block.tensor
        def _(pe):
            pe.wait_ge(silu_ready, 1)

            def chunk_pair(i):
                for b in range(2):
                    pe.wait_ge(w_loaded[b], 16 * (i + 1))
                    if not isinstance(i, int):
                        pe.wait_ge(acc_free, 2 * i + b - 1)
                    for k in range(DK):
                        mm = nc.tensor.matmul(acc[b][0:NR, :], csil[:, k, :], w[b][:, k, :], start=(k == 0), stop=(k == DK - 1))
                    mm.then_inc(acc_ready, 1)

            chunk_pair(0)
            with pe.Fori(1, NMOD // 2) as i:
                chunk_pair(i)


def qkv_attn_stage(nc, d, ident, w_qkv, hT, attnT, qk_s, v_s):
    with ExitStack() as ctx:
        m = Memory(nc, ctx)
        x = m.sb("x", [P, D])
        h = m.sb("h", [P, D])
        hTc = m.sb("hTc", [P, DK, P])
        g1 = m.sb("g1", [P, D])
        sh1 = m.sb("sh1", [P, D])
        gain = m.sb("gain", [P, QKW])
        cos = m.sb("cos", [P, HD])
        sin = m.sb("sin", [P, HD])
        mask = m.sb("mask", [P, 2, 2 * P])
        sinks = m.sb("sinks", [P, NH])
        half = m.sb("neg_half", [P, NQK])
        ss = m.sb("ss", [P, 1])
        rs = m.sb("rs", [P, 1])
        qkv = m.sb("qkv", [P, QKVW])
        sq = m.sb("sq", [P, QKW])
        rot = m.sb("rot", [P, QKW])
        qk = m.sb("qk", [P, QKW])
        ssh = m.sb("ssh", [P, NQK])
        rsh = m.sb("rsh", [P, NQK])
        qT = m.sb("qT", [HD, NH, P])
        kband = m.sb("kband", [HD, NKV, 2, P])
        vband = m.sb("vband", [P, 2, KVW])
        S = [m.sb(f"S{b}", [P, GRP, 2 * P]) for b in range(2)]
        PT = m.sb("PT", [P, GRP, 2, P])
        mx = m.sb("mx", [P, NH])
        nm = m.sb("nm", [P, NH])
        ds_ = m.sb("sink_minus_max", [P, NH])
        es = m.sb("exp_sink", [P, NH])
        rsum = m.sb("rsum", [P, NH])
        den = m.sb("den", [P, NH])
        rden = m.sb("rden", [P, NH])
        attn = m.sb("attn", [P, D])
        v_next = m.sb("v_next", [P, KVW])
        psT = m.ps("psT", [P, 8, P])
        psQ = [m.ps(f"psQ{b}", [P, 512]) for b in range(2)]
        psS = m.ps("psS", [P, GRP, 2 * P])
        psO = m.ps("psO", [P, NH, HD])

        s = m.sem
        rows_loaded, rope_loaded, x_loaded = s("bc_rows_loaded"), s("rope_loaded"), s("x_loaded")
        consts, gained = s("consts_set"), s("gained")
        x_squared, rms_step, rms_ready, h_step, h_ready = s("x_squared"), s("rms_step"), s("rms_ready"), s("h_step"), s("h_ready")
        psT_full, psT_free = s("psT_full"), s("psT_free")
        hT_copied = s("hT_copied")
        qkv_mult, qkv_moved = s("qkv_mult"), s("qkv_moved")
        qk_squared, qk_summed, head_rms_step, head_rms = s("qk_squared"), s("qk_summed"), s("head_rms_step"), s("head_rms")
        rope_step, roped, v_placed, band_shifted = s("rope_step"), s("roped"), s("v_placed"), s("band_shifted")
        scores, scores_moved, soft_step, max_ready, exps = s("scores"), s("scores_moved"), s("soft_step"), s("max_ready"), s("exps")
        pv_done, attn_ready, den_ready = s("pv_done"), s("attn_ready"), s("den_ready")
        kv_stored = s("kv_stored")

        qkv_loaded = [s(f"w_qkv_loaded{c}") for c in range(3)]
        qkv_read, v_kept = s("qkv_read"), s("v_kept")

        UT = 9
        LAST = NT - 1

        def later(i, n=1):
            return not isinstance(i, int) or i >= n

        def use_h(i):
            return i + 1 if isinstance(i, int) and i < 2 else 2 + UT * (i - 2) + 1

        def use_q(i):
            return 2 + UT * i + (0 if isinstance(i, int) and i == LAST else 1)

        def use_probs(i, g):
            return use_q(i) + 3 + g + 1

        def steps(eng, step):
            step(0, P, P, P)
            with eng.Fori(1, NT - 3) as i:
                step(i, P, P, P)
            step(NT - 3, P, P, NS)
            step(NT - 2, P, NS, None)
            step(LAST, NS, None, None)

        block = ctx.enter_context(nc.Block())

        def xrows(i, rows):
            return d["x"][tile_rows(i, rows), :]

        @block.sync
        def _(sp):
            sp.dma_start(x[:], xrows(0, P)).then_inc(x_loaded, 16)
            sp.dma_start(g1[:], d["modrows"][0:1, D:2 * D].partition_broadcast(P).rearrange("p a n -> p (a n)")).then_inc(rows_loaded, 16)
            sp.dma_start(sh1[:], d["modrows"][0:1, 0:D].partition_broadcast(P).rearrange("p a n -> p (a n)")).then_inc(rows_loaded, 16)
            sp.dma_start(gain[:], d["gain"].partition_broadcast(P)).then_inc(rows_loaded, 16)
            sp.dma_start(sinks[:], d["sinks"].partition_broadcast(P)).then_inc(rows_loaded, 16)
            sp.dma_start(mask[:], d["mask"]).then_inc(rows_loaded, 16)

            def load_tables(i, rows):
                if later(i):
                    sp.wait_ge(roped, i)
                sp.dma_start(cos[0:rows, :], d["cos"][tile_rows(i, rows), :]).then_inc(rope_loaded, 16)
                sp.dma_start(sin[0:rows, :], d["sin"][tile_rows(i, rows), :]).then_inc(rope_loaded, 16)

            def load_x(i, rows):
                sp.wait_ge(h_ready, i)
                sp.dma_start(x[0:rows, :], xrows(i, rows)).then_inc(x_loaded, 16)

            for c in range(3):
                cols = slice(c * 512, (c + 1) * 512)
                sp.dma_start(w_qkv[:, :, cols], d["w_qkv"][:, :, cols]).then_inc(qkv_loaded[c], 16)
            load_tables(0, P)
            load_x(1, P)
            load_x(2, P)

            def step(i, rows1, rows2, rows3):
                if rows3 == NS:
                    sp.wait_ge(h_ready, NT)
                    for dst, col in ((g1, D), (sh1, 0)):
                        for b in range(DEC_B):
                            sp.dma_start(dst[b * DEC_T:(b + 1) * DEC_T, :],
                                         d["modrows"][1 + b:2 + b, col:col + D].partition_broadcast(DEC_T).rearrange("p a n -> p (a n)")
                                         ).then_inc(rows_loaded, 16)
                if rows3:
                    load_x(i + 3, rows3)
                load_tables(i + 1, rows1)
            steps(sp, step)
            sp.wait_ge(roped, NT)
            sp.dma_start(d["win_k_p"], qk[:, NH * HD:QKW]).then_inc(kv_stored, 16)
            sp.wait_ge(v_placed, NT)
            sp.dma_start(d["win_v_p"], vband[:, 1, :]).then_inc(kv_stored, 16)
            sp.wait_ge(kv_stored, 32)

        @block.scalar
        def _(act):
            act.wait_ge(consts, 3)

            def square_x(i, rows):
                act.wait_ge(x_loaded, 16 * (i + 1))
                if later(i):
                    act.wait_ge(psT_full, use_h(i - 1))
                nc.scalar.activation(h[0:rows, :], x[0:rows, :], ACT.Square, accum_out=ss[0:rows, :]).then_inc(x_squared, 1)

            def move_T(dst, src, use):
                act.wait_ge(psT_full, use)
                nc.scalar.activation(dst, src, ACT.Copy).then_inc(psT_free, 1)

            def move_h(i, rows):
                if later(i):
                    act.wait_ge(qkv_mult, 3 * i)
                    act.wait_ge(hT_copied, i)
                move_T(hTc[:, :, 0:rows], psT[:, :, 0:rows], use_h(i))

            def move_qkv(i, c, rows):
                act.wait_ge(qkv_mult, 3 * i + c + 1)
                if c == 0 and later(i):
                    act.wait_ge(qkv_read, i)
                    act.wait_ge(v_kept, i)
                nc.scalar.activation(qkv[0:rows, c * 512:(c + 1) * 512], psQ[c % 2][0:rows, :], ACT.Copy).then_inc(qkv_moved, 1)

            def square_qk(i, rows):
                act.wait_ge(qkv_moved, 3 * (i + 1))
                if later(i):
                    act.wait_ge(roped, i)
                nc.scalar.activation(sq[0:rows, :], qkv[0:rows, 0:QKW], ACT.Square).then_inc(qk_squared, 1)

            def exp_group(i, g):
                act.wait_ge(max_ready, NKV * i + g + 1)
                for j in range(GRP):
                    hd = g * GRP + j
                    nc.scalar.activation(S[g % 2][:, j, :], S[g % 2][:, j, :], ACT.Exp, bias=nm[:, hd:hd + 1],
                                         accum_out=rsum[:, hd:hd + 1]).then_inc(exps, 1)
                nc.scalar.activation(es[:, g * GRP:(g + 1) * GRP], ds_[:, g * GRP:(g + 1) * GRP], ACT.Exp).then_inc(exps, 1)

            for i in range(2):
                square_x(i, P)
                move_h(i, P)
                for c in range(3):
                    move_qkv(i, c, P)
                square_qk(i, P)
            square_x(2, P)

            def step(i, rows1, rows2, rows3):
                u = use_q(i)
                if rows2:
                    move_h(i + 2, rows2)
                if later(i):
                    act.wait_ge(scores, NKV * i)
                move_T(qT[:, 0:8, :], psT[0:HD, :, :], u + 1)
                move_T(qT[:, 8:16, :], psT[0:HD, :, :], u + 2)
                if later(i):
                    act.wait_ge(band_shifted, 2 * i)
                move_T(kband[:, :, 1, :], psT[0:HD, 0:NKV, :], u + 3)
                if rows2:
                    move_qkv(i + 2, 0, rows2)
                if rows3:
                    square_x(i + 3, rows3)
                for g in range(NKV):
                    exp_group(i, g)
                    if g or later(i):
                        act.wait_ge(pv_done, NKV * i + g)
                    move_T(PT[:], psT[:, :, :].rearrange("p (j b) q -> p j b q", b=2), use_probs(i, g))
                    if g in (0, 2) and rows2:
                        move_qkv(i + 2, 1 + g // 2, rows2)
                move_T(attnT[:, :, tile_cols(i)], psT[:, :, :], use_probs(i, NKV))
                if rows2:
                    square_qk(i + 2, rows2)
            steps(act, step)

        @block.gpsimd
        def _(pool):
            nc.gpsimd.memset(half[:], -0.5).then_inc(consts, 1)
            nc.gpsimd.memset(kband[:], 0.0).then_inc(consts, 1)
            nc.gpsimd.memset(vband[:], 0.0).then_inc(consts, 1)
            hold(pool, consts, 3)

            def rms(i, rows):
                hold(pool, x_squared, i + 1)
                if later(i):
                    hold(pool, h_ready, i)
                nc.gpsimd.tensor_scalar(rs[0:rows, :], ss[0:rows, :], 1.0 / D, EPS, ALU.mult, ALU.add).then_inc(rms_step, 1)
                hold(pool, rms_step, i + 1)
                nc.gpsimd.tensor_tensor(rs[0:rows, :], rs[0:rows, :], half[0:rows, 0:1], ALU.pow).then_inc(rms_ready, 1)

            def copy_hT(i, rows):
                hold(pool, psT_free, use_h(i))
                cols = slice(SEQ, T) if rows == NS else tile_cols(i)
                nc.gpsimd.tensor_copy(hT[:, :, cols], hTc[:, :, 0:rows]).then_inc(hT_copied, 1)

            def head_rms_of(i, rows):
                hold(pool, qk_summed, i + 1)
                nc.gpsimd.tensor_scalar(rsh[0:rows, :], ssh[0:rows, :], 1.0 / HD, EPS, ALU.mult, ALU.add).then_inc(head_rms_step, 1)
                hold(pool, head_rms_step, i + 1)
                nc.gpsimd.tensor_tensor(rsh[0:rows, :], rsh[0:rows, :], half[0:rows, :], ALU.pow).then_inc(head_rms, 1)

            def keep_v(i, rows):
                hold(pool, qkv_moved, 3 * (i + 1))
                if later(i):
                    hold(pool, v_placed, i)
                nc.gpsimd.tensor_copy(v_next[0:rows, :] if rows == P else v_s[:], qkv[0:rows, QKW:QKVW]).then_inc(v_kept, 1)

            def place_v(i):
                hold(pool, v_kept, i + 1)
                nc.gpsimd.tensor_copy(vband[:, 1, :], v_next[:]).then_inc(v_placed, 1)

            def shift_band(i):
                hold(pool, scores, NKV * (i + 1))
                nc.gpsimd.tensor_copy(kband[:, :, 0, :], kband[:, :, 1, :]).then_inc(band_shifted, 1)
                hold(pool, pv_done, NKV * (i + 1))
                nc.gpsimd.tensor_copy(vband[:, 0, :], vband[:, 1, :]).then_inc(band_shifted, 1)
                hold(pool, band_shifted, 2 * (i + 1))

            rms(0, P)
            copy_hT(0, P)
            keep_v(0, P)
            place_v(0)
            head_rms_of(0, P)
            rms(1, P)
            copy_hT(1, P)
            keep_v(1, P)
            rms(2, P)

            def step(i, rows1, rows2, rows3):
                head_rms_of(i + 1, rows1)
                if rows2:
                    copy_hT(i + 2, rows2)
                if rows3:
                    rms(i + 3, rows3)
                shift_band(i)
                if rows1 == P:
                    place_v(i + 1)
                    keep_v(i + 2, rows2)
            steps(pool, step)

        @block.vector
        def _(dve):
            dve.wait_ge(rows_loaded, 80)
            dve.wait_ge(consts, 3)
            heads = lambda t, r: t[r, 0:QKW].rearrange("p (n e) -> p n e", e=HD)

            def make_h(i, rows):
                if rows == NS:
                    dve.wait_ge(rows_loaded, 80 + 32 * DEC_B)
                dve.wait_ge(rms_ready, i + 1)
                nc.vector.scalar_tensor_tensor(h[0:rows, :], x[0:rows, :], rs[0:rows, :], g1[0:rows, :], ALU.mult, ALU.mult).then_inc(h_step, 1)
                dve.wait_ge(h_step, i + 1)
                nc.vector.tensor_tensor(h[0:rows, :], h[0:rows, :], sh1[0:rows, :], ALU.add).then_inc(h_ready, 1)

            def sum_squares(i, rows):
                r = slice(0, rows)
                dve.wait_ge(qk_squared, i + 1)
                if later(i):
                    dve.wait_ge(head_rms, i)
                nc.vector.tensor_reduce(ssh[r, :], heads(sq, r), AX, ALU.add).then_inc(qk_summed, 1)

            def norm_heads(i, rows):
                r = slice(0, rows)
                dve.wait_ge(head_rms, i + 1)
                dve.wait_ge(qk_summed, i + 1)
                nc.vector.tensor_tensor(heads(sq, r), heads(qkv, r), bc(rsh[r, :].unsqueeze(2), [rows, NQK, HD]), ALU.mult).then_inc(qkv_read, 1)
                dve.wait_ge(qkv_read, i + 1)
                nc.vector.tensor_tensor(sq[r, :], sq[r, :], gain[r, :], ALU.mult).then_inc(gained, 1)

            def rope(i, rows, out):
                r = slice(0, rows)
                st = Steps(dve, rope_step, base=3 * i)
                dve.wait_ge(rope_loaded, 32 * (i + 1))
                dve.wait_ge(gained, i + 1)
                tab = lambda t: bc(t.unsqueeze(1), [rows, NQK, t.shape[1]])
                H2 = HD // 2
                st.did(nc.vector.tensor_tensor(heads(rot, r)[:, :, 0:H2], heads(sq, r)[:, :, H2:HD], tab(sin[r, 0:H2]), ALU.mult))
                st.did(nc.vector.tensor_tensor(heads(rot, r)[:, :, H2:HD], heads(sq, r)[:, :, 0:H2], tab(sin[r, H2:HD]), ALU.mult))
                st.wait()
                st.did(nc.vector.tensor_tensor(heads(sq, r), heads(sq, r), tab(cos[r, :]), ALU.mult))
                st.wait()
                if later(i):
                    dve.wait_ge(psT_full, 2 + UT * (i - 1) + 4)
                nc.vector.tensor_tensor(out[r, :], sq[r, :], rot[r, :], ALU.add).then_inc(roped, 1)

            def soft_group(i, g):
                st = Steps(dve, soft_step, base=(NKV * i + g) * 3)
                hs = slice(g * GRP, (g + 1) * GRP)
                which = 1 if later(i) else 0
                dve.wait_ge(scores, NKV * i + g + 1)
                if g >= 2 or later(i):
                    dve.wait_ge(psT_full, use_probs(i, g - 2) if g >= 2 else 2 + UT * (i - 1) + 4 + (g + 2) + 1)
                nc.vector.scalar_tensor_tensor(S[g % 2][:], psS[:], SCALE, bc(mask[:, which, :].unsqueeze(1), [P, GRP, 2 * P]),
                                               ALU.mult, ALU.add).then_inc(scores_moved, 1)
                dve.wait_ge(scores_moved, NKV * i + g + 1)
                if g == 0 and later(i):
                    dve.wait_ge(attn_ready, i)
                st.did(nc.vector.tensor_reduce(mx[:, hs], S[g % 2][:], AX, ALU.max))
                st.wait()
                st.did(nc.vector.tensor_tensor(mx[:, hs], mx[:, hs], sinks[:, hs], ALU.max))
                st.wait()
                st.did(nc.vector.tensor_scalar(nm[:, hs], mx[:, hs], -1.0, None, ALU.mult))
                st.wait()
                nc.vector.tensor_tensor(ds_[:, hs], sinks[:, hs], mx[:, hs], ALU.subtract).then_inc(max_ready, 1)

            def normalise(i):
                dve.wait_ge(exps, NKV * (GRP + 1) * (i + 1))
                nc.vector.tensor_tensor(den[:], rsum[:], es[:], ALU.add).then_inc(den_ready, 1)
                dve.wait_ge(den_ready, 2 * i + 1)
                nc.vector.reciprocal(rden[:], den[:]).then_inc(den_ready, 1)
                dve.wait_ge(den_ready, 2 * i + 2)
                dve.wait_ge(pv_done, NKV * (i + 1))
                nc.vector.tensor_tensor(attn[:, :].rearrange("p (n e) -> p n e", e=HD), psO[:],
                                        bc(rden[:].unsqueeze(2), [P, NH, HD]), ALU.mult).then_inc(attn_ready, 1)

            make_h(0, P)
            sum_squares(0, P)
            norm_heads(0, P)
            make_h(1, P)
            rope(0, P, qk)
            make_h(2, P)

            def step(i, rows1, rows2, rows3):
                sum_squares(i + 1, rows1)
                norm_heads(i + 1, rows1)
                soft_group(i, 0)
                soft_group(i, 1)
                soft_group(i, 2)
                if rows3:
                    make_h(i + 3, rows3)
                soft_group(i, 3)
                rope(i + 1, rows1, qk if rows1 == P else qk_s)
                normalise(i)
            steps(dve, step)

        @block.tensor
        def _(pe):
            pe.wait_ge(d["ident_loaded"], 16)
            pe.wait_ge(consts, 3)

            def turn(srcs, use, width=P, rows=P):
                if not (isinstance(use, int) and use == 1):
                    hold(pe, psT_free, use - 1)
                for j, src in enumerate(srcs):
                    mm = nc.tensor.transpose(psT[0:width, j, 0:rows], src, ident[0:rows, 0:rows])
                mm.then_inc(psT_full, 1)

            def turn_h(i, rows):
                pe.wait_ge(h_ready, i + 1)
                turn([h[0:rows, k * P:(k + 1) * P] for k in range(DK)], use_h(i), P, rows)

            def project(i, q, rows):
                c, at = q // 4, 2 * (q % 4)
                if at == 0:
                    if not later(i):
                        pe.wait_ge(qkv_loaded[c], 16)
                    pe.wait_ge(psT_free, use_h(i))
                    if c == 0 and later(i):
                        pe.wait_ge(qkv_moved, 3 * i)
                    if c == 2:
                        pe.wait_ge(qkv_moved, 3 * i + 1)
                for k in (at, at + 1):
                    mm = nc.tensor.matmul(psQ[c % 2][0:rows, :], hTc[:, k, 0:rows], w_qkv[:, k, c * 512:(c + 1) * 512],
                                          start=(k == 0), stop=(k == DK - 1))
                if at + 2 == DK:
                    mm.then_inc(qkv_mult, 1)

            def score(i, g):
                if g or later(i):
                    pe.wait_ge(scores_moved, NKV * i + g)
                pe.wait_ge(psT_free, use_q(i) + 3)
                for j in range(GRP):
                    mm = nc.tensor.matmul(psS[:, j, :], qT[:, g * GRP + j, :], kband[:, g, :, :].rearrange("p b n -> p (b n)"), start=True, stop=True)
                mm.then_inc(scores, 1)

            def turn_probs(i, g):
                pe.wait_ge(exps, (GRP + 1) * (NKV * i + g + 1))
                turn([S[g % 2][:, j, b * P:(b + 1) * P] for j in range(GRP) for b in range(2)], use_probs(i, g))

            def weigh(i, g):
                pe.wait_ge(psT_free, use_probs(i, g))
                pe.wait_ge(v_placed, i + 1)
                if later(i):
                    pe.wait_ge(attn_ready, i)
                    pe.wait_ge(band_shifted, 2 * i)
                for j in range(GRP):
                    for b in range(2):
                        mm = nc.tensor.matmul(psO[:, g * GRP + j, :], PT[:, j, b, :], vband[:, b, g * HD:(g + 1) * HD],
                                              start=(b == 0), stop=(b == 1))
                mm.then_inc(pv_done, 1)

            for i in range(2):
                turn_h(i, P)
                for q in range(12):
                    project(i, q, P)

            def step(i, rows1, rows2, rows3):
                u = use_q(i)
                parts = iter(range(12))

                def fill(n):
                    for _ in range(n if rows2 else 0):
                        project(i + 2, next(parts), rows2)

                if rows2:
                    turn_h(i + 2, rows2)
                pe.wait_ge(roped, i + 1)
                turn([qk[:, n * HD:(n + 1) * HD] for n in range(0, 8)], u + 1, HD)
                fill(1)
                turn([qk[:, n * HD:(n + 1) * HD] for n in range(8, 16)], u + 2, HD)
                fill(1)
                turn([qk[:, n * HD:(n + 1) * HD] for n in range(16, 20)], u + 3, HD)
                fill(2)
                score(i, 0)
                fill(2)
                score(i, 1)
                fill(1)
                turn_probs(i, 0)
                fill(1)
                weigh(i, 0)
                score(i, 2)
                fill(1)
                turn_probs(i, 1)
                fill(1)
                weigh(i, 1)
                score(i, 3)
                fill(1)
                turn_probs(i, 2)
                fill(1)
                weigh(i, 2)
                turn_probs(i, 3)
                weigh(i, 3)
                pe.wait_ge(attn_ready, i + 1)
                turn([attn[:, k * P:(k + 1) * P] for k in range(DK)], use_probs(i, NKV))
            steps(pe, step)


def sample_stage(nc, d, ident, qk_s, v_s, attnT, w, hT, h_hi, h_lo):
    R = GRP * DEC_T
    KN = WIN + DEC_T
    with ExitStack() as ctx:
        m = Memory(nc, ctx)
        kc = m.sb("k_cache", [P, DEC_B, KVW])
        vc = m.sb("v_cache", [P, DEC_B, KVW])
        vn = m.sb("v_new", [DEC_T, DEC_B, KVW])
        mask = m.sb("mask_s", [R, KN])
        sinks = m.sb("sinks_s", [R, NKV])
        qT = m.sb("qT_s", [HD, DEC_B, NKV, GRP, DEC_T])
        kn = m.sb("k_new_T", [HD, NKV, NS])
        kT = [m.sb(f"k_cache_T{b}", [HD, NKV, WIN]) for b in range(2)]
        S = m.sb("S_s", [R, DEC_B, NKV, KN])
        mx, ds_, es, den, rden = (m.sb(n, [R, DEC_B, NKV]) for n in ("mx_s", "ds_s", "es_s", "den_s", "rden_s"))
        PT = [m.sb(f"PT_s{b}", [P, NKV, R]) for b in range(2)]
        PN = [m.sb(f"PN_s{b}", [DEC_T, NKV, R]) for b in range(2)]
        psA = m.ps("psA", [P, NH, NS])
        psK = m.ps("psK", [P, NKV, WIN])
        psS = m.ps("psS_s", [P, NKV, 256])
        psP = m.ps("psP", [P, NKV, R])
        psN = m.ps("psN", [P, NKV, R])
        psO = m.ps("psO_s", [P, NKV, R])
        s = m.sem
        new_stored, cache_loaded, v_new_loaded = s("new_stored"), s("cache_loaded"), s("v_new_loaded")
        q_turned, q_moved, kn_turned = s("q_turned"), s("q_moved"), s("kn_turned")
        k_turned, k_moved, scores, scores_moved = s("k_turned"), s("k_moved"), s("scores_sm"), s("scores_sm_moved")
        soft, shifted, exped, probs = s("soft_s"), s("shifted_s"), s("exped_s"), s("probs_s")
        p_turned, p_moved, weighed, out_moved = s("p_turned"), s("p_moved"), s("weighed"), s("out_moved")
        block = ctx.enter_context(nc.Block())

        @block.sync
        def _(sp):
            sp.dma_start(kc[:], d["cache_k"].rearrange("b j n -> j b n")).then_inc(cache_loaded, 16)
            sp.dma_start(vc[:], d["cache_v"].rearrange("b j n -> j b n")).then_inc(cache_loaded, 16)
            sp.dma_start(mask[:], d["mask_s"]).then_inc(cache_loaded, 16)
            sp.dma_start(sinks[:], d["sinks_s"]).then_inc(cache_loaded, 16)
            for n in range(2):
                w.load(sp, n, n)
            for b in range(DEC_B):
                rows = slice(b * DEC_T, (b + 1) * DEC_T)
                sp.dma_start(d["win_v_s"][b, WIN - DEC_T:WIN, :], v_s[rows, :]).then_inc(new_stored, 16)
                sp.dma_start(d["win_k_s"][b, WIN - DEC_T:WIN, :], qk_s[rows, NH * HD:QKW]).then_inc(new_stored, 16)
            for out, cache in (("win_v_s", "cache_v"), ("win_k_s", "cache_k")):
                sp.dma_start(d[out][:, 0:WIN - DEC_T, :], d[cache][:, DEC_T:WIN, :]).then_inc(new_stored, 16)
            sp.wait_ge(new_stored, 16 * (2 * DEC_B + 2))
            sp.dma_start(vn[:], d["win_v_s"][:, WIN - DEC_T:WIN, :].rearrange("b t n -> t b n")).then_inc(v_new_loaded, 16)

        @block.gpsimd
        def _(pool):
            nc.gpsimd.tensor_copy(h_hi, hT).then_inc(d["h_split"], 1)
            hold(pool, d["h_split"], 1)
            nc.gpsimd.tensor_tensor(h_lo, hT, h_hi.bitcast(F32), ALU.subtract).then_inc(d["h_split"], 1)

        @block.scalar
        def _(act):
            def exps(b):
                act.wait_ge(shifted, 2 * (b + 1))
                nc.scalar.activation(S[:, b], S[:, b], ACT.Exp).then_inc(exped, 1)
                nc.scalar.activation(es[:, b], ds_[:, b], ACT.Exp).then_inc(exped, 1)

            act.wait_ge(q_turned, 1)
            for g in range(NKV):
                nc.scalar.activation(qT[:, :, g, :, :].rearrange("p b h t -> p h b t"),
                                     psA[0:HD, g * GRP:(g + 1) * GRP, :].rearrange("p h (b t) -> p h b t", t=DEC_T), ACT.Copy).then_inc(q_moved, 1)
            act.wait_ge(kn_turned, 1)
            nc.scalar.activation(kn[:], psK[0:HD, :, 0:NS], ACT.Copy).then_inc(k_moved, 1)
            for b in range(DEC_B):
                act.wait_ge(k_turned, b + 1)
                if b >= 2:
                    act.wait_ge(scores, b - 1)
                nc.scalar.activation(kT[b % 2][:], psK[0:HD, :, :], ACT.Copy).then_inc(k_moved, 1)
                if b:
                    exps(b - 1)
            exps(DEC_B - 1)
            for b in range(DEC_B):
                act.wait_ge(p_turned, b + 1)
                if b >= 2:
                    act.wait_ge(weighed, b - 1)
                nc.scalar.activation(PT[b % 2][:], psP[:], ACT.Copy).then_inc(p_moved, 1)
                nc.scalar.activation(PN[b % 2][:], psN[0:DEC_T], ACT.Copy).then_inc(p_moved, 1)

        @block.vector
        def _(dve):
            dve.wait_ge(cache_loaded, 64)
            wide = lambda t, b, n: bc(t[:, b].unsqueeze(2), [R, NKV, n])
            st = Steps(dve, soft)

            def shift(b):
                dve.wait_ge(scores, b + 1)
                nc.vector.scalar_tensor_tensor(S[:, b], psS[0:R, :, 0:KN], SCALE, bc(mask[:].unsqueeze(1), [R, NKV, KN]), ALU.mult, ALU.add).then_inc(scores_moved, 1)
                dve.wait_ge(scores_moved, b + 1)
                st.did(nc.vector.tensor_reduce(mx[:, b], S[:, b], AX, ALU.max))
                st.wait()
                st.did(nc.vector.tensor_tensor(mx[:, b], mx[:, b], sinks[:], ALU.max))
                st.wait()
                nc.vector.tensor_tensor(S[:, b], S[:, b], wide(mx, b, KN), ALU.subtract).then_inc(shifted, 1)
                nc.vector.tensor_tensor(ds_[:, b], sinks[:], mx[:, b], ALU.subtract).then_inc(shifted, 1)

            def normalise(b):
                dve.wait_ge(exped, 2 * (b + 1))
                st.did(nc.vector.tensor_reduce(den[:, b], S[:, b], AX, ALU.add))
                st.wait()
                st.did(nc.vector.tensor_tensor(den[:, b], den[:, b], es[:, b], ALU.add))
                st.wait()
                st.did(nc.vector.reciprocal(rden[:, b], den[:, b]))
                st.wait()
                nc.vector.tensor_tensor(S[:, b], S[:, b], wide(rden, b, KN), ALU.mult).then_inc(probs, 1)

            for b in range(DEC_B):
                shift(b)
                if b:
                    normalise(b - 1)
            normalise(DEC_B - 1)
            for b in range(DEC_B):
                dve.wait_ge(weighed, b + 1)
                for par in range(2):
                    src = psO[0:HD].rearrange("p g (k e t) -> p g k e t", e=2, t=DEC_T)[:, :, :, par, :]
                    dst = attnT[par * HD:(par + 1) * HD, :, SEQ + b * DEC_T:SEQ + (b + 1) * DEC_T].rearrange("p (g k) t -> p g k t", k=GRP // 2)
                    nc.vector.tensor_copy(dst, src).then_inc(out_moved, 1)

        @block.tensor
        def _(pe):
            for n in range(NH):
                mm = nc.tensor.transpose(psA[0:HD, n, :], qk_s[:, n * HD:(n + 1) * HD], ident[0:NS, 0:NS])
            mm.then_inc(q_turned, 1)
            for n in range(NKV):
                mm = nc.tensor.transpose(psK[0:HD, n, 0:NS], qk_s[:, (NH + n) * HD:(NH + n + 1) * HD], ident[0:NS, 0:NS])
            mm.then_inc(kn_turned, 1)
            pe.wait_ge(cache_loaded, 64)
            pe.wait_ge(q_moved, NKV)
            for b in range(DEC_B):
                pe.wait_ge(k_moved, b + 1)
                for g in range(NKV):
                    mm = nc.tensor.transpose(psK[0:HD, g, :], kc[:, b, g * HD:(g + 1) * HD], ident[:, :])
                mm.then_inc(k_turned, 1)
                pe.wait_ge(k_moved, b + 2)
                if b:
                    pe.wait_ge(scores_moved, b)
                for g in range(NKV):
                    q = qT[:, b, g].rearrange("p h t -> p (h t)")
                    nc.tensor.matmul(psS[0:R, g, 0:WIN], q, kT[b % 2][:, g, :], start=True, stop=True)
                    mm = nc.tensor.matmul(psS[0:R, g, WIN:KN], q, kn[:, g, b * DEC_T:(b + 1) * DEC_T], start=True, stop=True)
                mm.then_inc(scores, 1)
            pe.wait_ge(v_new_loaded, 16)
            for b in range(DEC_B):
                pe.wait_ge(probs, b + 1)
                if b:
                    pe.wait_ge(p_moved, 2 * b)
                for g in range(NKV):
                    nc.tensor.transpose(psP[:, g, :], S[:, b, g, 0:WIN], ident[0:R, 0:R])
                    mm = nc.tensor.transpose(psN[0:DEC_T, g, :], S[:, b, g, WIN:KN], ident[0:R, 0:R])
                mm.then_inc(p_turned, 1)
                pe.wait_ge(p_moved, 2 * b + 2)
                if b:
                    pe.wait_ge(out_moved, 2 * b)
                for g in range(NKV):
                    nc.tensor.matmul(psO[0:HD, g, :], vc[:, b, g * HD:(g + 1) * HD], PT[b % 2][:, g, :], start=True, stop=False)
                    mm = nc.tensor.matmul(psO[0:HD, g, :], vn[:, b, g * HD:(g + 1) * HD], PN[b % 2][:, g, :], start=False, stop=True)
                mm.then_inc(weighed, 1)


class Weights:

    def __init__(self, d, sb, sem):
        self.dram = d["w_units"]
        self.raw = [sb(f"w_raw{q}", [P, DK, P], F32) for q in range(2)]
        self.hi = [sb(f"w_hi{q}", [P, DK, P], F32R) for q in range(2)]
        self.lo = [sb(f"w_lo{q}", [P, DK, P], F32R) for q in range(2)]
        self.loaded = [sem(f"w_unit_loaded{q}") for q in range(2)]
        self.hi_ready, self.lo_ready = sem("w_hi_ready"), sem("w_lo_ready")
        self.block_done = sem("block_done")

    def load(self, sp, n, q):
        if not (isinstance(n, int) and n < 2):
            sp.wait_ge(self.lo_ready, n - 1)
        sp.dma_start(self.raw[q][:], self.dram[n]).then_inc(self.loaded[q], 16)

    def split_hi(self, nc, act, n, q, turn):
        act.wait_ge(self.loaded[q], 16 * (turn + 1))
        if not (isinstance(n, int) and n < 2):
            act.wait_ge(self.block_done, 3 * (n - 1))
        nc.scalar.activation(self.hi[q][:], self.raw[q][:], ACT.Copy).then_inc(self.hi_ready, 1)

    def split_lo(self, nc, dve, n, q):
        dve.wait_ge(self.hi_ready, n + 1)
        nc.vector.tensor_tensor(self.lo[q][:], self.raw[q][:], self.hi[q][:].bitcast(F32), ALU.subtract).then_inc(self.lo_ready, 1)

    def multiply(self, nc, out, q, hi, lo, cols):
        passes = [(self.hi[q], hi), (self.hi[q], lo), (self.lo[q], hi)]
        for k in range(DK):
            for n, (w, x) in enumerate(passes):
                mm = nc.tensor.matmul(out, w[:, k, :], x[:, k, cols], start=(k == 0 and n == 0), stop=(k == DK - 1 and n == 2))
        mm.then_inc(self.block_done, 1)


def pairs(eng, body, chunks=DK):
    for b in range(2):
        body(b, b, 0)
    with eng.Fori(1, chunks // 2) as i:
        for b in range(2):
            body(2 * i + b, b, i)


def one_of(c):
    return slice(c, c + 1) if isinstance(c, int) else bass.ds(c, 1)


BLOCK_COLS = [slice(j * CB, (j + 1) * CB) for j in range(3)]
CONV_PARTS = 5
MERGE_PARTS = 2
CONV_UNITS = CONV_PARTS * DK


def conv_stage(nc, d, h_hi, h_lo, yT, w):
    with ExitStack() as ctx:
        m = Memory(nc, ctx)
        csb = m.sb("c_gate", [P, T])
        th = [m.sb(f"gate_tanh{g}", [P, T]) for g in range(2)]
        u = [m.sb(f"u{b}", [P, 2 + SEQ]) for b in range(2)]
        us = [m.sb(f"u_s{b}", [P, DEC_B, 2 + DEC_T]) for b in range(2)]
        ys = m.sb("y_s", [P, DEC_B, DEC_T])
        cw = m.sb("conv_w", [P, DK, 3])
        state = m.sb("state", [P, DK, DEC_B, 2])
        new = m.sb("conv_new", [P, DK, 2 + 2 * DEC_B])
        banks = [m.ps(f"conv_bank{j}", [P, 512]) for j in range(6)]
        s = m.sem
        small_loaded, zeroed = s("small_loaded"), s("zeroed")
        c_moved, u_ready = s("c_moved"), s("u_ready")
        gate_done, gate_stored = s("gate_done"), [s(f"gate_stored{g}") for g in range(2)]
        conv_step, y_ready, state_placed, tail_saved, tail_stored = s("conv_step"), s("y_ready"), s("state_placed"), s("tail_saved"), s("tail_stored")
        block = ctx.enter_context(nc.Block())
        TAIL = SEQ - 2 * CB

        def unit(c, b, p):
            return CONV_PARTS * c + p, (CONV_PARTS * b + p) % 2

        def done(c, p, j):
            return 3 * (CONV_PARTS * c + p) + j + 1

        def bank(b, p, j):
            return banks[(3 * (CONV_PARTS * b + p) + j) % 6]

        @block.sync
        def _(sp):
            for dst, name in ((cw, "conv_wT"), (state, "stateT")):
                sp.dma_start(dst[:], d[name]).then_inc(small_loaded, 16)

            def chunk(c, b, i):
                for p in range(CONV_PARTS):
                    n, q = unit(c, b, p)
                    w.load(sp, n + 2, q)
                    if p >= 3:
                        sp.wait_ge(gate_done, 6 * c + 3 * (p - 2))
                        sp.dma_start(d["gates"][p - 3, one_of(c)].rearrange("a p n -> p (a n)"), th[p - 3][:]).then_inc(gate_stored[p - 3], 16)
            pairs(sp, chunk)
            sp.wait_ge(tail_saved, 2 * DK)
            sp.dma_start(d["conv_new"], new[:]).then_inc(tail_stored, 16)
            sp.wait_ge(tail_stored, 16)
            for g in range(2):
                sp.wait_ge(gate_stored[g], 16 * DK)

        @block.tensor
        def _(pe):
            pe.wait_ge(d["h_split"], 2)

            def chunk(c, b, i):
                first = isinstance(c, int) and c == 0
                for p in range(CONV_PARTS):
                    n, q = unit(c, b, p)
                    pe.wait_ge(w.lo_ready, n + 1)
                    for j in range(3):
                        if p == 0 and not first:
                            pe.wait_ge(gate_done, 6 * (c - 1) + 3 + j + 1)
                        if p == 1 and not first:
                            pe.wait_ge(y_ready, 4 * (c - 1) + j + 1 + (j == 2))
                        if p == 2:
                            pe.wait_ge(c_moved, 3 * c + j + 1)
                        if p == 3:
                            pe.wait_ge(u_ready, 3 * c + j + 1)
                        if p == 4:
                            pe.wait_ge(gate_done, 6 * c + j + 1)
                        w.multiply(nc, bank(b, p, j)[:, 0:CB], q, h_hi, h_lo, BLOCK_COLS[j])
            pairs(pe, chunk)

        @block.scalar
        def _(act):
            w.split_hi(nc, act, 0, 0, 0)

            def chunk(c, b, i):
                first = isinstance(c, int) and c == 0
                for p in range(CONV_PARTS):
                    n, q = unit(c, b, p)
                    w.split_hi(nc, act, n + 1, 1 - q, CONV_PARTS * i + (CONV_PARTS * b + p + 1) // 2)
                    if p in (2, 3) and not first:
                        act.wait_ge(gate_stored[p - 2], 16 * c)
                    for j in range(3):
                        if p == 0:
                            act.wait_ge(w.block_done, done(c, p, j))
                            if not first:
                                act.wait_ge(u_ready, 3 * c)
                            nc.scalar.activation(csb[:, BLOCK_COLS[j]], bank(b, p, j)[:, 0:CB], ACT.Copy).then_inc(c_moved, 1)
                        if p in (2, 3):
                            act.wait_ge(w.block_done, done(c, p, j))
                            nc.scalar.activation(th[p - 2][:, BLOCK_COLS[j]], bank(b, p, j)[:, 0:CB], ACT.Tanh, scale=0.5).then_inc(gate_done, 1)
            pairs(act, chunk)

        @block.gpsimd
        def _(pool):
            for b in range(2):
                nc.gpsimd.memset(u[b][:, 0:2], 0.0).then_inc(zeroed, 1)
            hold(pool, small_loaded, 32)

            def chunk(c, b, i):
                if not (isinstance(c, int) and c < 2):
                    hold(pool, y_ready, 4 * (c - 1))
                nc.gpsimd.tensor_copy(us[b][:, :, 0:2], state[:, one_of(c), :, :].rearrange("p a b j -> p (a b) j")).then_inc(state_placed, 1)
                hold(pool, u_ready, 3 * (c + 1))
                nc.gpsimd.tensor_copy(new[:, one_of(c), 0:2].rearrange("p a j -> p (a j)"), u[b][:, SEQ:SEQ + 2]).then_inc(tail_saved, 1)
                nc.gpsimd.tensor_copy(new[:, one_of(c), 2:2 + 2 * DEC_B].rearrange("p a (b j) -> p (a b) j", j=2), us[b][:, :, DEC_T:DEC_T + 2]).then_inc(tail_saved, 1)
            pairs(pool, chunk)

        @block.vector
        def _(dve):
            w.split_lo(nc, dve, 0, 0)
            dve.wait_ge(small_loaded, 32)
            dve.wait_ge(zeroed, 2)

            def chunk(c, b, i):
                st = Steps(dve, conv_step, base=7 * c)
                one = one_of(c)
                y = lambda lo, hi: yT[:, one, lo:hi].rearrange("p a n -> p (a n)")

                def split(p):
                    n, q = unit(c, b, p)
                    w.split_lo(nc, dve, n + 1, 1 - q)

                split(0)
                split(1)
                if not (isinstance(c, int) and c < 2):
                    dve.wait_ge(tail_saved, 2 * (c - 1))
                for j in range(3):
                    dve.wait_ge(c_moved, 3 * c + j + 1)
                    dve.wait_ge(w.block_done, done(c, 1, j))
                    cg, xp = csb[:, BLOCK_COLS[j]], bank(b, 1, j)
                    width = CB if j < 2 else TAIL
                    ins = nc.vector.tensor_tensor(u[b][:, 2 + j * CB:2 + j * CB + width], xp[:, 0:width], cg[:, 0:width], ALU.mult)
                    if j == 2:
                        st.did(ins)
                        ins = nc.vector.tensor_tensor(us[b][:, :, 2:2 + DEC_T], xp[:, TAIL:CB].rearrange("p (b t) -> p b t", t=DEC_T),
                                                      cg[:, TAIL:CB].rearrange("p (b t) -> p b t", t=DEC_T), ALU.mult)
                    ins.then_inc(u_ready, 1)
                split(2)
                dve.wait_ge(u_ready, 3 * (c + 1))
                st.wait()
                dve.wait_ge(state_placed, c + 1)
                tap = lambda j: cw[:, one, j:j + 1].rearrange("p a j -> p (a j)")
                if not (isinstance(c, int) and c == 0):
                    dve.wait_ge(y_ready, 4 * c)
                for o, ext in ((y(0, SEQ), lambda j: u[b][:, j:j + SEQ]), (ys[:], lambda j: us[b][:, :, j:j + DEC_T])):
                    st.did(nc.vector.tensor_scalar(o, ext(0), tap(0), None, ALU.mult))
                    for j in (1, 2):
                        st.wait()
                        st.did(nc.vector.scalar_tensor_tensor(o, ext(j), tap(j), o, ALU.mult, ALU.add))
                split(3)
                split(4)
                st.wait()
                for j in range(3):
                    dve.wait_ge(w.block_done, done(c, 4, j))
                    width = CB if j < 2 else TAIL
                    cols = (j * CB, j * CB + width)
                    nc.vector.tensor_tensor(y(*cols), y(*cols), bank(b, 4, j)[:, 0:width], ALU.mult).then_inc(y_ready, 1)
                nc.vector.tensor_tensor(y(SEQ, T), ys[:].rearrange("p b t -> p (b t)"), bank(b, 4, 2)[:, TAIL:CB], ALU.mult).then_inc(y_ready, 1)
            pairs(dve, chunk)


def merge_stage(nc, d, full, hi, lo, w, w_out):
    with ExitStack() as ctx:
        m = Memory(nc, ctx)
        th = [m.sb(f"gate{g}", [P, T]) for g in range(2)]
        out = [m.sb(f"merged{b}", [P, T]) for b in range(2)]
        banks = [[m.ps(f"merge_bank{p}{j}", [P, 512]) for j in range(3)] for p in range(2)]
        s = m.sem
        src_hi, src_lo = [s(f"src_hi{p}") for p in range(2)], [s(f"src_lo{p}") for p in range(2)]
        gated = [s(f"gated{p}") for p in range(2)]
        gate_loaded, merged, merged_stored = [s(f"gate_loaded{g}") for g in range(2)], s("merged"), [s(f"merged_stored{b}") for b in range(2)]
        block = ctx.enter_context(nc.Block())

        def done(c, p, j):
            return 3 * (CONV_UNITS + MERGE_PARTS * c + p) + j + 1

        @block.sync
        def _(sp):
            for g in range(2):
                sp.dma_start(th[g][:], d["gates"][g, 0]).then_inc(gate_loaded[g], 16)

            def chunk(c, b, i, last=False):
                for p in range(MERGE_PARTS):
                    if not last:
                        w.load(sp, CONV_UNITS + 2 * c + p + 2, p)
                        sp.wait_ge((gated[0], merged)[p], 3 * (c + 1))
                        nxt = slice(c + 1, c + 2) if isinstance(c, int) else bass.ds(c + 1, 1)
                        sp.dma_start(th[p][:], d["gates"][p, nxt].rearrange("a p n -> p (a n)")).then_inc(gate_loaded[p], 16)
                    elif p == 0:
                        sp.wait_ge(w.block_done, done(DK - 1, 0, 2))
                        sp.dma_start(w_out, d["w_out"]).then_inc(d["w_out_loaded"], 16)
                sp.wait_ge(merged, 3 * (c + 1))
                sp.dma_start(d["mergedT"][:, one_of(c), :].rearrange("p a n -> p (a n)"), out[b][:]).then_inc(merged_stored[b], 16)
            for b in range(2):
                chunk(b, b, 0)
            with sp.Fori(1, DK // 2 - 1) as i:
                for b in range(2):
                    chunk(2 * i + b, b, i)
            chunk(DK - 2, 0, DK // 2 - 1)
            chunk(DK - 1, 1, DK // 2 - 1, last=True)
            for b in range(2):
                sp.wait_ge(merged_stored[b], 16 * DK // 2)

        @block.tensor
        def _(pe):
            def chunk(c, b, i):
                for p in range(MERGE_PARTS):
                    pe.wait_ge(w.lo_ready, CONV_UNITS + 2 * c + p + 1)
                    for j in range(3):
                        if isinstance(c, int) and c == 0:
                            pe.wait_ge(src_lo[p], j + 1)
                        else:
                            pe.wait_ge(gated[p], 3 * (c - 1) + j + 1)
                        w.multiply(nc, banks[p][j][:, 0:CB], p, hi[p], lo[p], BLOCK_COLS[j])
            pairs(pe, chunk)

        @block.scalar
        def _(act):
            def split(p):
                for j in range(3):
                    nc.scalar.activation(hi[p][:, :, BLOCK_COLS[j]], full[p][:, :, BLOCK_COLS[j]], ACT.Copy).then_inc(src_hi[p], 1)

            def split_next(c, p):
                n = CONV_UNITS + 2 * c + p + 1
                w.split_hi(nc, act, n, 1 - p, (CONV_UNITS // 2) + c + p)

            split(0)
            split_next(0, 0)
            split(1)
            split_next(0, 1)
            with act.Fori(1, DK - 1) as c:
                split_next(c, 0)
                split_next(c, 1)
            split_next(DK - 1, 0)

        @block.vector
        def _(dve):
            def split(p):
                for j in range(3):
                    dve.wait_ge(src_hi[p], j + 1)
                    cols = BLOCK_COLS[j]
                    nc.vector.tensor_tensor(lo[p][:, :, cols], full[p][:, :, cols], hi[p][:, :, cols].bitcast(F32), ALU.subtract).then_inc(src_lo[p], 1)

            def chunk(c, b, i, first=False, last=False):
                if first:
                    split(0)
                w.split_lo(nc, dve, CONV_UNITS + 2 * c + 1, 1)
                if first:
                    split(1)
                if not (isinstance(c, int) and c < 2):
                    dve.wait_ge(merged_stored[b], 16 * i)
                dve.wait_ge(gate_loaded[0], 16 * (c + 1))
                for j in range(3):
                    cols = BLOCK_COLS[j]
                    dve.wait_ge(w.block_done, done(c, 0, j))
                    nc.vector.scalar_tensor_tensor(out[b][:, cols], th[0][:, cols], 1.0, banks[0][j][:, 0:CB], ALU.add, ALU.mult).then_inc(gated[0], 1)
                if not last:
                    w.split_lo(nc, dve, CONV_UNITS + 2 * c + 2, 0)
                dve.wait_ge(gate_loaded[1], 16 * (c + 1))
                for j in range(3):
                    cols = BLOCK_COLS[j]
                    dve.wait_ge(w.block_done, done(c, 1, j))
                    nc.vector.scalar_tensor_tensor(th[1][:, cols], th[1][:, cols], 1.0, banks[1][j][:, 0:CB], ALU.add, ALU.mult).then_inc(gated[1], 1)
                    dve.wait_ge(gated[1], 3 * c + j + 1)
                    nc.vector.tensor_tensor(out[b][:, cols], out[b][:, cols], th[1][:, cols], ALU.add).then_inc(merged, 1)

            chunk(0, 0, 0, first=True)
            chunk(1, 1, 0)
            with dve.Fori(1, DK // 2 - 1) as i:
                for b in range(2):
                    chunk(2 * i + b, b, i)
            chunk(DK - 2, 0, DK // 2 - 1)
            chunk(DK - 1, 1, DK // 2 - 1, last=True)


def residual_stage(nc, d, ident, w, w_pq):
    with ExitStack() as ctx:
        m = Memory(nc, ctx)
        rows_of = {n: m.sb(n, [P, D]) for n in ("gt1", "g2", "sh2")}
        sample_rows = {n: m.sb(f"{n}_s", [NS, D]) for n in ("gt1", "g2", "sh2")}
        mT = [m.sb(f"mT{b}", [P, DK, P]) for b in range(2)]
        x = [m.sb(f"xr{b}", [P, D]) for b in range(2)]
        x1 = [m.sb(f"x1{b}", [P, D]) for b in range(2)]
        h2 = [m.sb(f"h2{b}", [P, D]) for b in range(2)]
        h2T = [m.sb(f"h2T{b}", [P, DK, P]) for b in range(2)]
        ss = m.sb("ss2", [P, 1])
        rs = m.sb("rs2", [P, 1])
        half = m.sb("neg_half2", [P, 1])
        psY = [m.ps(f"psY{b}", [P, D]) for b in range(2)]
        psT = m.ps("psT2", [P, DK, P])
        s = m.sem
        rows_loaded, sample_rows_loaded, mT_loaded = s("rows2_loaded"), s("sample_rows_loaded"), [s(f"mT_loaded{b}") for b in range(2)]
        in_loaded = [s(f"in_loaded{b}") for b in range(2)]
        half_set, y_mult, x1_step, x1_ready, x1_squared = s("half_set"), s("y_mult"), s("x1_step"), s("x1_ready"), s("x1_squared")
        rms_step, rms, h2_step, h2_ready, turned, h2T_ready = s("rms2_step"), s("rms2"), s("h2_step"), s("h2_ready"), s("turned"), s("h2T_ready")
        out_stored = [s(f"out_stored{b}") for b in range(2)]
        block = ctx.enter_context(nc.Block())

        def tiles(eng, body):
            for b in range(2):
                body(b, b, P, 0)
            with eng.Fori(1, NT // 2) as k:
                for b in range(2):
                    body(2 * k + b, b, P, k)
            body(NT, 0, NS, NT // 2)

        early = lambda i, n: isinstance(i, int) and i < n

        @block.sync
        def _(sp):

            def load(i, b, rows):
                if not early(i, 2):
                    sp.wait_ge(y_mult, i - 1)
                cols = slice(SEQ, T) if rows == NS else tile_cols(i)
                sp.dma_start(mT[b][:, :, 0:rows], d["mergedT"][:, :, cols]).then_inc(mT_loaded[b], 16)
                if not early(i, 2):
                    sp.wait_ge(x1_ready, i - 1)
                sp.dma_start(x[b][0:rows, :], d["x"][tile_rows(i, rows), :]).then_inc(in_loaded[b], 16)

            def store(i, b, rows):
                sp.wait_ge(h2T_ready, i + 1)
                sp.dma_start(d["x1"][tile_rows(i, rows), :], x1[b][0:rows, :]).then_inc(out_stored[b], 16)
                sp.dma_start(d["h2"][tile_rows(i, rows), :], h2[b][0:rows, :]).then_inc(out_stored[b], 16)
                one = slice(i, i + 1) if isinstance(i, int) else bass.ds(i, 1)
                dst = d["h2T"][one, :, :].rearrange("a p (k n) -> p (a k) n", n=P)
                sp.dma_start(dst[:, :, 0:rows], h2T[b][:, :, 0:rows]).then_inc(out_stored[b], 16)

            load(0, 0, P)
            load(1, 1, P)
            for n, col in (("gt1", 2), ("g2", 4), ("sh2", 3)):
                sp.dma_start(rows_of[n][:], d["modrows"][0:1, col * D:(col + 1) * D].partition_broadcast(P).rearrange("p a n -> p (a n)")).then_inc(rows_loaded, 16)
            sp.dma_start(w_pq, d["w_pq"]).then_inc(d["w_peer_loaded"], 16)
            for n, col in (("gt1", 2), ("g2", 4), ("sh2", 3)):
                for q in range(DEC_B):
                    sp.dma_start(sample_rows[n][q * DEC_T:(q + 1) * DEC_T, :],
                                 d["modrows"][1 + q:2 + q, col * D:(col + 1) * D].partition_broadcast(DEC_T).rearrange("p a n -> p (a n)")).then_inc(sample_rows_loaded, 16)
            with sp.Fori(0, NT // 2 - 1) as k:
                for b in range(2):
                    load(2 * k + b + 2, b, P)
                    store(2 * k + b, b, P)
            load(NT, 0, NS)
            store(NT - 2, 0, P)
            store(NT - 1, 1, P)
            store(NT, 0, NS)
            sp.wait_ge(out_stored[0], 48 * (NT // 2 + 1))
            sp.wait_ge(out_stored[1], 48 * (NT // 2))

        @block.tensor
        def _(pe):
            pe.wait_ge(d["w_out_loaded"], 16)
            pe.wait_ge(half_set, 1)

            def mult(i, b, rows, k):
                pe.wait_ge(mT_loaded[b], 16 * (k + 1))
                if not early(i, 2):
                    pe.wait_ge(x1_ready, i - 1)
                for c in range(2):
                    for kk in range(DK):
                        mm = nc.tensor.matmul(psY[b][0:rows, c * 512:(c + 1) * 512], mT[b][:, kk, 0:rows], w[:, kk, c * 512:(c + 1) * 512],
                                              start=(kk == 0), stop=(kk == DK - 1))
                mm.then_inc(y_mult, 1)

            def turn(i, b, rows):
                pe.wait_ge(h2_ready, i + 1)
                if not early(i, 1):
                    pe.wait_ge(h2T_ready, i)
                for kk in range(DK):
                    mm = nc.tensor.transpose(psT[:, kk, 0:rows], h2[b][0:rows, kk * P:(kk + 1) * P], ident[0:rows, 0:rows])
                mm.then_inc(turned, 1)

            def pair(k, last):
                mult(2 * k + 1, 1, P, k)
                turn(2 * k, 0, P)
                mult(2 * k + 2, 0, NS if last else P, k + 1)
                turn(2 * k + 1, 1, P)

            mult(0, 0, P, 0)
            pair(0, False)
            with pe.Fori(1, NT // 2 - 1) as k:
                pair(k, False)
            pair(NT // 2 - 1, True)
            turn(NT, 0, NS)

        @block.scalar
        def _(act):
            def body(i, b, rows, k):
                act.wait_ge(x1_ready, i + 1)
                nc.scalar.activation(h2[b][0:rows, :], x1[b][0:rows, :], ACT.Square, accum_out=ss[0:rows, :]).then_inc(x1_squared, 1)
                act.wait_ge(turned, i + 1)
                nc.scalar.activation(h2T[b][:, :, 0:rows], psT[:, :, 0:rows], ACT.Copy).then_inc(h2T_ready, 1)
            for b in range(2):
                body(b, b, P, 0)
            with act.Fori(1, NT // 2 - 1) as k:
                for b in range(2):
                    body(2 * k + b, b, P, k)
            for b in range(2):
                body(NT - 2 + b, b, P, NT // 2 - 1)
            body(NT, 0, NS, NT // 2)

        @block.gpsimd
        def _(pool):
            nc.gpsimd.memset(half[:], -0.5).then_inc(half_set, 1)
            hold(pool, half_set, 1)

            def body(i, b, rows, k):
                hold(pool, x1_squared, i + 1)
                if not early(i, 1):
                    hold(pool, h2_ready, i)
                nc.gpsimd.tensor_scalar(rs[0:rows, :], ss[0:rows, :], 1.0 / D, EPS, ALU.mult, ALU.add).then_inc(rms_step, 1)
                hold(pool, rms_step, i + 1)
                nc.gpsimd.tensor_tensor(rs[0:rows, :], rs[0:rows, :], half[0:rows, :], ALU.pow).then_inc(rms, 1)
            tiles(pool, body)

        @block.vector
        def _(dve):
            dve.wait_ge(rows_loaded, 48)

            def body(i, b, rows, k):
                r = slice(0, rows)
                dve.wait_ge(y_mult, i + 1)
                dve.wait_ge(in_loaded[b], 16 * (k + 1))
                row = sample_rows if rows == NS else rows_of
                if rows == NS:
                    dve.wait_ge(sample_rows_loaded, 48 * DEC_B)
                if not early(i, 2):
                    dve.wait_ge(out_stored[b], 48 * k)
                nc.vector.scalar_tensor_tensor(x1[b][r, :], psY[b][r, :], 0.5, row["gt1"][r, :], ALU.mult, ALU.mult).then_inc(x1_step, 1)
                dve.wait_ge(x1_step, i + 1)
                nc.vector.tensor_tensor(x1[b][r, :], x1[b][r, :], x[b][r, :], ALU.add).then_inc(x1_ready, 1)
                dve.wait_ge(rms, i + 1)
                nc.vector.scalar_tensor_tensor(h2[b][r, :], x1[b][r, :], rs[r, :], row["g2"][r, :], ALU.mult, ALU.mult).then_inc(h2_step, 1)
                dve.wait_ge(h2_step, i + 1)
                nc.vector.tensor_tensor(h2[b][r, :], h2[b][r, :], row["sh2"][r, :], ALU.add).then_inc(h2_ready, 1)
            tiles(dve, body)


def peer_stage(nc, d, ident, w):
    with ExitStack() as ctx:
        m = Memory(nc, ctx)
        BF16 = mybir.dt.bfloat16
        keys = m.sb("sub_keys", [P, 2 * PH, NKEYS])
        ring = [m.sb(f"rows{r}", [P, 2 * D]) for r in range(RING)]
        diag = [m.sb(f"diag{r}", [P, P]) for r in range(RING)]
        idx = [m.sb(f"idx{b}", [P, TOPK], U32) for b in range(2)]
        ids = m.sb("expert_ids", [P, PH, TOPK], U32)
        gates = m.sb("half_gates", [P, PH, TOPK])
        gcur = [m.sb(f"gates_now{b}", [P, TOPK]) for b in range(2)]
        gt2, x1, y, h2n, h2c = (m.sb(n, [P, D]) for n in ("gt2", "x1_now", "y_out", "h2_next", "h2_now"))
        h2T = m.sb("h2T_now", [P, DK, P])
        q_sb = m.sb("q_sb", [P, 2 * PHALF])
        qT = m.sb("qT_p", [P, 2, P])
        sc = m.sb("key_scores", [P, 2, NKEYS])
        sc2 = m.sb("key_scores_rest", [P, 2, NKEYS])
        top = m.sb("top_scores", [P, 2, TOPK])
        topi = m.sb("top_keys", [P, 2, TOPK], U32)
        topf = m.sb("top_keys_f", [P, 2, TOPK])
        cand = m.sb("pair_scores", [P, TOPK, TOPK])
        cand2 = m.sb("pair_scores_rest", [P, TOPK * TOPK])
        cs = m.sb("best_scores", [P, TOPK])
        ci = m.sb("best_pairs", [P, TOPK], U32)
        pair = m.sb("pair_halves", [P, 2, TOPK], U32)
        iota = m.sb("iota16", [P, TOPK])
        pick = m.sb("pick", [P, 2, TOPK, TOPK])
        picked = m.sb("picked", [P, 2, TOPK])
        nmax, esum, rsum = m.sb("neg_best", [P, 1]), m.sb("exp_sum", [P, 1]), m.sb("exp_rsum", [P, 1])
        ex = m.sb("exp_best", [P, TOPK])
        a, g1, th, co = ([m.sb(f"{n}{b}", [P, BATCH]) for b in range(2)] for n in ("dots", "poly", "tanh", "coef"))
        zeros = m.sb("zeros", [P, 512], BF16)
        ids_s, gates_s = m.sb("expert_ids_s", [P, 2, TOPK], U32), m.sb("half_gates_s", [P, 2, TOPK])
        fold = m.sb("fold", [P, NS])
        acc = m.ps("acc_peer", [P, D])
        psq, psT, pss = m.ps("ps_q", [P, 2 * PHALF]), m.ps("ps_qT", [P, 2, P]), m.ps("ps_scores", [P, 2, NKEYS])
        s = m.sem
        w_loaded = d["w_peer_loaded"]
        small_loaded, h2T_loaded, h2_loaded, x1_loaded, y_stored = s("small3_loaded"), s("h2T_loaded"), s("h2_loaded"), s("x1_loaded"), s("y_stored")
        zero_set, gt2_loaded = s("zero_set"), s("gt2_loaded")
        q_mult, q_moved, q_turned, qT_moved, key_mult, keys_moved = s("q_mult"), s("q_moved3"), s("q_turned3"), s("qT_moved"), s("key_mult"), s("keys_moved")
        top_step, pick_step, softmax_in, exp_done, ids_ready, gates_ready = s("top_step"), s("pick_step"), s("softmax_in"), s("exp_done"), s("ids_ready"), s("gates_ready")
        staged, slot_free, dotted, gelu_step, gelu_in, tanh_done, coef_ready, diag_ready = s("staged"), s("slot_free"), s("dotted"), s("gelu_step"), s("gelu_in"), s("tanh_done"), s("coef_ready"), s("diag_ready")
        gathered = [s(f"gathered{r}") for r in range(RING)]
        folded = s("folded")
        h2_taken, y_step, y_ready = s("h2_taken"), s("y_step"), s("y_ready")
        block = ctx.enter_context(nc.Block())
        NB = TOPK // BATCH

        FOLDS = P // NS

        def schedule(eng, unit, begin=None, end=None):
            def tile(t, rows, next_rows):
                if begin and rows:
                    begin(t, rows)
                with eng.Fori(0, PH // 2) as hp:
                    for b in range(2):
                        unit(PH * t + 2 * hp + b, 2 * hp + b, b, rows, next_rows, False)
                if end and rows:
                    end(t, rows)
            tile(-1, None, P)
            with eng.Fori(0, NT - 1) as t:
                tile(t, P, P)
            tile(NT - 1, P, NS)
            if begin:
                begin(NT, P)
            for b in range(2):
                unit(PH * NT + b, b, b, P, None, True)
            if end:
                end(NT, NS)

        @block.sync
        def _(sp):
            sp.dma_start(h2T[:], d["h2T"][0].rearrange("p (k n) -> p k n", n=P)).then_inc(h2T_loaded, 16)
            sp.dma_start(fold[:], d["fold"]).then_inc(small_loaded, 16)
            sp.dma_start(iota[:], d["iota"].partition_broadcast(P)).then_inc(small_loaded, 16)
            sp.dma_start(keys[:], d["subkT"]).then_inc(small_loaded, 16)
            sp.dma_start(h2n[:], d["h2"][0:P, :]).then_inc(h2_loaded, 16)
            sp.dma_start(x1[:], d["x1"][0:P, :]).then_inc(x1_loaded, 16)
            sp.dma_start(gt2[:], d["modrows"][0:1, 5 * D:6 * D].partition_broadcast(P).rearrange("p a n -> p (a n)")).then_inc(gt2_loaded, 16)
            sp.wait_ge(q_mult, PH)
            sp.dma_start(h2T[:], d["h2T"][1].rearrange("p (k n) -> p k n", n=P)).then_inc(h2T_loaded, 16)

            def tile(t, next_rows, rows_after):
                sp.wait_ge(h2_taken, t + 1)
                for f in range(1 if next_rows == P else FOLDS):
                    sp.dma_start(h2n[f * NS:f * NS + next_rows, :], d["h2"][tile_rows(t + 1, next_rows), :]).then_inc(h2_loaded, 16)
                if rows_after:
                    sp.wait_ge(q_mult, PH * (t + 2))
                    one = slice(t + 2, t + 3) if isinstance(t, int) else bass.ds(t + 2, 1)
                    src = d["h2T"][one, :, :].rearrange("a p (k n) -> p (a k) n", n=P)
                    sp.dma_start(h2T[:, :, 0:rows_after], src[:, :, 0:rows_after]).then_inc(h2T_loaded, 16)
                if next_rows == NS:
                    sp.wait_ge(ids_ready, PH * (NT + 1))
                    sp.wait_ge(gates_ready, PH * (NT + 1))
                    for f in range(FOLDS):
                        for dst, src in ((ids_s, ids), (gates_s, gates)):
                            sp.dma_start(dst[f * NS:(f + 1) * NS, :, :], src[0:NS, 2 * f:2 * f + 2, :]).then_inc(folded, 16)
                sp.wait_ge(y_ready, t + 1)
                sp.dma_start(d["y"][tile_rows(t, P), :], y[:]).then_inc(y_stored, 16)
                sp.dma_start(x1[0:next_rows, :], d["x1"][tile_rows(t + 1, next_rows), :]).then_inc(x1_loaded, 16)

            with sp.Fori(0, NT - 2) as t:
                tile(t, P, P)
            tile(NT - 2, P, NS)
            tile(NT - 1, NS, None)
            for q in range(DEC_B):
                sp.dma_start(gt2[q * DEC_T:(q + 1) * DEC_T, :],
                             d["modrows"][1 + q:2 + q, 5 * D:6 * D].partition_broadcast(DEC_T).rearrange("p a n -> p (a n)")).then_inc(gt2_loaded, 16)
            sp.wait_ge(y_ready, NT + 1)
            sp.dma_start(d["y"][SEQ:T, :], y[0:NS, :]).then_inc(y_stored, 16)
            sp.wait_ge(y_stored, 16 * (NT + 2))

        @block.gpsimd
        def _(pool):
            nc.gpsimd.memset(zeros[:], 0.0).then_inc(zero_set, 1)

            def unit(n, h, b, last):
                if last:
                    hold(pool, folded, 32 * FOLDS)
                else:
                    hold(pool, ids_ready, n + 1)
                hold(pool, dotted, TOPK * (n + 1))
                src = ids_s[:, h:h + 1, :] if last else ids[:, bass.ds(h, 1), :]
                nc.gpsimd.tensor_copy(idx[b][:], src.rearrange("p a k -> p (a k)")).then_inc(staged, 1)
                hold(pool, staged, n + 1)
                for j in range(TOPK):
                    hold(pool, slot_free, TOPK * n + j + 1)
                    nc.gpsimd.indirect_dma_start(ring[j % RING][:], None, d["uv"],
                                                 bass.IndirectOffsetOnAxis(ap=idx[b][:, j:j + 1], axis=0)).then_inc(gathered[j % RING], 16)

            with pool.Fori(0, NT) as t:
                with pool.Fori(0, PH // 2) as hp:
                    for b in range(2):
                        unit(PH * t + 2 * hp + b, 2 * hp + b, b, False)
            for b in range(2):
                unit(PH * NT + b, b, b, True)

        @block.scalar
        def _(act):
            act.wait_ge(small_loaded, 48)
            act.sem_inc(y_stored, 16)
            act.sem_inc(slot_free, RING)
            act.sem_inc(dotted, 2 * TOPK)

            def weigh(n, q, last):
                bq = q % 2
                act.wait_ge(gelu_in, NB * n + q + 1)
                nc.scalar.activation(th[bq][:], g1[bq][:], ACT.Tanh, scale=GELU_A).then_inc(tanh_done, 1)
                act.wait_ge(coef_ready, NB * n + q + 1)
                for k in range(BATCH):
                    r = (q * BATCH + k) % RING
                    nc.scalar.activation(diag[r][:, 0:NS] if last else diag[r][:], fold[:] if last else ident[:], ACT.Copy, scale=co[bq][:, k:k + 1]).then_inc(diag_ready, 1)

            def unit(n, h, b, rows, next_rows, last):
                m_ = n + PH

                def move(dst, src, full, sem):
                    act.wait_ge(full, m_ + 1)
                    nc.scalar.activation(dst, src, ACT.Copy).then_inc(sem, 1)
                for q in range(NB):
                    if rows:
                        weigh(n, q, last)
                    if next_rows:
                        r = slice(0, next_rows)
                        if q == 0:
                            move(q_sb[r, :], psq[r, :], q_mult, q_moved)
                        elif q == 1:
                            move(qT[:, :, r], psT[:, :, r], q_turned, qT_moved)
                        elif q == 2:
                            move(sc[r], pss[r], key_mult, keys_moved)
                        else:
                            act.wait_ge(softmax_in, m_ + 1)
                            nc.scalar.activation(ex[r, :], cs[r, :], ACT.Exp, bias=nmax[r, :], accum_out=esum[r, :]).then_inc(exp_done, 1)
            schedule(act, unit)

        @block.tensor
        def _(pe):
            pe.wait_ge(w_loaded, 16)
            pe.wait_ge(small_loaded, 48)
            pe.wait_ge(zero_set, 1)

            def begin(t, rows):
                pe.wait_ge(y_step, t + 1)
                for c in range(2):
                    nc.tensor.matmul(acc[:, c * 512:(c + 1) * 512], zeros[:, 0:P], zeros[:], start=True, stop=False, skip_group_check=True)

            def unit(n, h, b, rows, next_rows, last):
                m_ = n + PH
                cols = bass.ds(h * 2 * PHALF, 2 * PHALF)
                for q in range(NB):
                    if next_rows:
                        r = slice(0, next_rows)
                        if q == 0:
                            for k in range(DK):
                                mm = nc.tensor.matmul(psq[r, :], h2T[:, k, r], w[:, k, cols], start=(k == 0), stop=(k == DK - 1))
                            mm.then_inc(q_mult, 1)
                        elif q == 1:
                            hold(pe, q_moved, m_ + 1)
                            for p in range(2):
                                mm = nc.tensor.transpose(psT[:, p, r], q_sb[r, p * P:(p + 1) * P], ident[r, r])
                            mm.then_inc(q_turned, 1)
                        elif q == 2:
                            pe.wait_ge(qT_moved, m_ + 1)
                            for p in range(2):
                                one = bass.ds(2 * h + p, 1)
                                mm = nc.tensor.matmul(pss[r, p, :], qT[:, p, r], keys[:, one, :].rearrange("p a n -> p (a n)"), start=True, stop=True)
                            mm.then_inc(key_mult, 1)
                    if rows:
                        for k in range(BATCH):
                            j = q * BATCH + k
                            hold(pe, diag_ready, TOPK * n + j + 1)
                            for c in range(2):
                                out = slice(0, NS if last else P)
                                mm = nc.tensor.matmul(acc[out, c * 512:(c + 1) * 512], diag[j % RING][:, out],
                                                      ring[j % RING][:, D + c * 512:D + (c + 1) * 512], start=False, stop=False, skip_group_check=True)
                            mm.then_inc(slot_free, 1)

            def tile(t, rows, next_rows):
                if next_rows:
                    pe.wait_ge(h2T_loaded, 16 * (t + 2))
                if rows:
                    begin(t, rows)
                with pe.Fori(0, PH // 2) as hp:
                    for b in range(2):
                        unit(PH * t + 2 * hp + b, 2 * hp + b, b, rows, next_rows, False)

            tile(-1, None, P)
            with pe.Fori(0, NT - 1) as t:
                tile(t, P, P)
            tile(NT - 1, P, NS)
            begin(NT, P)
            for b in range(2):
                unit(PH * NT + b, b, b, P, None, True)

        @block.vector
        def _(dve):
            dve.wait_ge(small_loaded, 48)
            dve.sem_inc(y_step, 1)
            SMALL = 3
            TOP = 19

            def begin(t, rows):
                dve.wait_ge(h2_loaded, 16 * (NT + FOLDS) if isinstance(t, int) and t == NT else 16 * (t + 1))
                dve.wait_ge(dotted, 2 * TOPK + SLOTS * t)
                nc.vector.tensor_copy(h2c[0:rows, :], h2n[0:rows, :]).then_inc(h2_taken, 1)
                hold(dve, h2_taken, t + 1)

            def end(t, rows):
                r = slice(0, rows)
                dve.wait_ge(gt2_loaded, 16 * (1 + DEC_B) if rows == NS else 16)
                dve.wait_ge(slot_free, RING + (SLOTS * NT + 2 * TOPK if rows == NS else SLOTS * (t + 1)))
                dve.wait_ge(y_stored, 16 * (t + 1))
                dve.wait_ge(x1_loaded, 16 * (t + 1))
                nc.vector.tensor_tensor(y[r, :], acc[r, :], gt2[r, :], ALU.mult).then_inc(y_step, 1)
                dve.wait_ge(y_step, t + 2)
                nc.vector.tensor_tensor(y[r, :], y[r, :], x1[r, :], ALU.add).then_inc(y_ready, 1)

            def dots(n, b, q, rows):
                r, bq = slice(0, rows), q % 2
                st = Steps(dve, gelu_step, base=(SMALL * NB + 1) * n + 1 + SMALL * q)
                for k in range(BATCH):
                    j = q * BATCH + k
                    u = ring[j % RING][r, 0:D]
                    dve.wait_ge(gathered[j % RING], 16 * ((TOPK // RING) * n + j // RING + 1))
                    nc.vector.tensor_tensor_reduce(u, u, h2c[r, :], 1.0, 0.0, ALU.mult, ALU.add, a[bq][r, k:k + 1]).then_inc(dotted, 1)
                dve.wait_ge(dotted, 2 * TOPK + TOPK * n + (q + 1) * BATCH)
                st.did(nc.vector.tensor_tensor(g1[bq][r, :], a[bq][r, :], a[bq][r, :], ALU.mult))
                st.wait()
                st.did(nc.vector.tensor_scalar(g1[bq][r, :], g1[bq][r, :], GELU_B, 1.0, ALU.mult, ALU.add))
                st.wait()
                nc.vector.tensor_tensor(g1[bq][r, :], g1[bq][r, :], a[bq][r, :], ALU.mult).then_inc(gelu_in, 1)
                dve.wait_ge(tanh_done, NB * n + q + 1)
                st.did(nc.vector.scalar_tensor_tensor(co[bq][r, :], th[bq][r, :], 1.0, a[bq][r, :], ALU.add, ALU.mult))
                st.wait()
                nc.vector.tensor_tensor(co[bq][r, :], co[bq][r, :], gcur[b][r, q * BATCH:(q + 1) * BATCH], ALU.mult).then_inc(coef_ready, 1)

            def choose(m_, rows):
                r = slice(0, rows)
                st = Steps(dve, top_step, base=TOP * m_, own=True)
                E8 = slice(0, 8), slice(8, 16)
                hold(dve, keys_moved, m_ + 1)
                for p in range(2):
                    st.did(nc.vector.max(top[r, p, E8[0]], sc[r, p, :]))
                st.wait()
                for p in range(2):
                    st.did(nc.vector.max_index(topi[r, p, E8[0]], top[r, p, E8[0]], sc[r, p, :]))
                    st.did(nc.vector.match_replace(sc2[r, p, :], top[r, p, E8[0]], sc[r, p, :], -3.0e38))
                st.wait()
                for p in range(2):
                    st.did(nc.vector.max(top[r, p, E8[1]], sc2[r, p, :]))
                st.wait()
                for p in range(2):
                    st.did(nc.vector.max_index(topi[r, p, E8[1]], top[r, p, E8[1]], sc2[r, p, :]))
                st.did(nc.vector.tensor_tensor(cand[r], bc(top[r, 0, :].unsqueeze(2), [rows, TOPK, TOPK]),
                                               bc(top[r, 1, :].unsqueeze(1), [rows, TOPK, TOPK]), ALU.add))
                st.wait()
                flat = cand[r].rearrange("p a b -> p (a b)")
                st.did(nc.vector.tensor_copy(topf[r], topi[r]))
                st.did(nc.vector.max(cs[r, E8[0]], flat))
                st.wait()
                st.did(nc.vector.max_index(ci[r, E8[0]], cs[r, E8[0]], flat))
                st.did(nc.vector.match_replace(cand2[r, :], cs[r, E8[0]], flat, -3.0e38))
                st.wait()
                st.did(nc.vector.max(cs[r, E8[1]], cand2[r, :]))
                st.wait()
                nc.vector.tensor_scalar(nmax[r, :], cs[r, 0:1], -1.0, None, ALU.mult).then_inc(softmax_in, 1)
                st.did(nc.vector.max_index(ci[r, E8[1]], cs[r, E8[1]], cand2[r, :]))
                st.wait()
                st.did(nc.vector.tensor_scalar(pair[r, 0, :], ci[r, :], 4, None, ALU.logical_shift_right))
                st.did(nc.vector.tensor_scalar(pair[r, 1, :], ci[r, :], TOPK - 1, None, ALU.bitwise_and))
                assert st.n == TOP, st.n

            def choose_ids(m_, h, rows, staged_before):
                r = slice(0, rows)
                one = bass.ds(h, 1)
                st = Steps(dve, pick_step, base=4 * m_)
                dve.wait_ge(top_step, TOP * (m_ + 1))
                halves = pair[r].rearrange("p a k -> p (a k)")
                st.did(nc.vector.tensor_tensor(pick[r].rearrange("p a k j -> p (a k) j"), bc(halves.unsqueeze(2), [rows, 2 * TOPK, TOPK]),
                                               bc(iota[r, :].unsqueeze(1), [rows, 2 * TOPK, TOPK]), ALU.is_equal))
                st.wait()
                st.did(nc.vector.tensor_tensor(pick[r], pick[r], bc(topf[r].unsqueeze(2), [rows, 2, TOPK, TOPK]), ALU.mult))
                st.wait()
                st.did(nc.vector.tensor_reduce(picked[r].rearrange("p a k -> p (a k)"), pick[r].rearrange("p a k j -> p (a k) j"), AX, ALU.add))
                st.wait()
                if staged_before:
                    dve.wait_ge(staged, m_ - PH + 1)
                nc.vector.scalar_tensor_tensor(ids[r, one, :].rearrange("p a k -> p (a k)"), picked[r, 0, :], float(NKEYS), picked[r, 1, :],
                                               ALU.mult, ALU.add).then_inc(ids_ready, 1)
                dve.wait_ge(exp_done, m_ + 1)
                st.did(nc.vector.reciprocal(rsum[r, :], esum[r, :]))
                st.wait()
                nc.vector.tensor_scalar(gates[r, one, :].rearrange("p a k -> p (a k)"), ex[r, :], rsum[r, :], 0.5, ALU.mult, ALU.mult).then_inc(gates_ready, 1)

            def unit(n, h, b, rows, next_rows, last):
                m_ = n + PH
                if rows:
                    if last:
                        dve.wait_ge(folded, 32 * FOLDS)
                    else:
                        dve.wait_ge(gates_ready, n + 1)
                    src = gates_s[:, h:h + 1, :] if last else gates[:, bass.ds(h, 1), :]
                    g = Steps(dve, gelu_step, base=(SMALL * NB + 1) * n)
                    g.did(nc.vector.tensor_copy(gcur[b][:], src.rearrange("p a k -> p (a k)")))
                    g.wait()
                    for q in range(NB):
                        dots(n, b, q, rows)
                if next_rows:
                    choose(m_, next_rows)
                    choose_ids(m_, h, next_rows, rows is not None)
            schedule(dve, unit, begin, end)


def build(nc, ins, outs):
    d = dict(ins)
    d.update(outs)

    def scratch(name, shape):
        return nc.dram_tensor(name, shape, F32, kind="Internal").ap()

    d["modrows"] = scratch("modrows", (1 + DEC_B, NMOD * 512))
    d["x1"] = scratch("x1_d", (T, D))
    d["h2"] = scratch("h2_d", (T, D))
    d["gates"] = scratch("gates_d", (2, DK, P, T))
    d["mergedT"] = scratch("merged_d", (P, DK, T))
    d["h2T"] = scratch("h2T_d", (NT + 1, P, DK * P))
    with ExitStack() as whole:
        def sb(ctx, name, shape):
            return ctx.enter_context(nc.sbuf_tensor(name, shape, F32))

        def sem(name):
            return whole.enter_context(nc.semaphore(name))

        def over(name, offset, shape, dt):
            return nc.alloc_sbuf_tensor_at(name, shape, dt, offset=offset)[:]

        ident = sb(whole, "ident", [P, P])
        wide_at = nc.sbuf_base
        wide = sb(whole, "wide", [P, 2, DK * T])
        hT, attnT = (wide[:, n, :].rearrange("p (k n) -> p k n", k=DK) for n in range(2))
        w_pq = wide[:].rearrange("p a n -> p (a n)")[:, 0:DK * PH * 2 * PHALF].rearrange("p (k n) -> p k n", k=DK)
        for name in ("ident_loaded", "w_out_loaded", "w_peer_loaded", "h_split"):
            d[name] = sem(name)
        with ExitStack() as c2:
            qk_s, v_s = sb(c2, "qk_s", [NS, QKW]), sb(c2, "v_s", [NS, KVW])
            with ExitStack() as c3:
                w_qkv = sb(c3, "w_qkv", [P, DK, QKVW])
                mods_stage(nc, d, ident, hT, attnT)
                qkv_attn_stage(nc, d, ident, w_qkv, hT, attnT, qk_s, v_s)
            with ExitStack() as c3:
                spare_at = nc.sbuf_base
                hi_part = c3.enter_context(nc.sbuf_tensor("hi_part", [P, DK, T], F32R))[:]
                w_out = over("w_out", spare_at, [P, DK, D], F32)
                h_lo = over("h_lo", wide_at, [P, DK, T], F32R)
                attn_lo = over("attn_lo", wide_at + 4 * DK * T, [P, DK, T], F32R)
                with ExitStack() as c4:
                    w = Weights(d, lambda name, shape, dt: c4.enter_context(nc.sbuf_tensor(name, shape, dt)), sem)
                    sample_stage(nc, d, ident, qk_s, v_s, attnT, w, hT, hi_part, h_lo)
                    y_at = nc.sbuf_base
                    yT = sb(c4, "yT", [P, DK, T])[:]
                    y_lo = over("y_lo", y_at, [P, DK, T], F32R)
                    conv_stage(nc, d, hi_part, h_lo, yT, w)
                    merge_stage(nc, d, (attnT, yT), (hi_part, h_lo), (attn_lo, y_lo), w, w_out)
                residual_stage(nc, d, ident, w_out, w_pq)
        peer_stage(nc, d, ident, w_pq)


def _constants():
    half = HD // 2
    inv = (10000.0 ** (-np.arange(half, dtype=np.float32) / np.float32(half)).astype(np.float64)).astype(np.float32)
    pos = np.concatenate([np.arange(SEQ), np.tile(PAST + np.arange(DEC_T), DEC_B)]).astype(np.float32)
    ang = (pos[:, None] * inv[None, :]).astype(np.float64)
    cos, sin = np.cos(ang).astype(np.float32), np.sin(ang).astype(np.float32)
    q, k = np.arange(P)[:, None], np.arange(2 * P)[None, :]
    band = (k >= q) & (k <= q + WIN)
    masks = np.stack([np.where(band & (k >= P), 0.0, NEG), np.where(band, 0.0, NEG)], axis=1).astype(np.float32)
    tok, j = np.tile(np.arange(DEC_T), GRP)[:, None], np.arange(WIN + DEC_T)[None, :]
    mask_s = np.where((j >= tok) & (j <= tok + WIN), 0.0, NEG).astype(np.float32)
    return dict(ident=np.eye(P, dtype=np.float32), cos=np.concatenate([cos, cos], 1), sin=np.concatenate([-sin, sin], 1),
                mask=masks, mask_s=mask_s, fold=np.tile(np.eye(NS, dtype=np.float32), (P // NS, 1)), iota=np.arange(TOPK, dtype=np.float32))


def _chunks(w):
    return w.reshape(DK, P, -1).transpose(1, 0, 2)


def _by_columns(w):
    return w.reshape(DK, P, DK, P).transpose(2, 1, 0, 3)


def _layout(a):
    w_in = a["w_in"][0]
    at = np.cumsum([0, NH * HD, KVW, KVW, D, D, D, D, D])
    part = lambda n: w_in[:, at[n]:at[n + 1]]
    c_all = np.concatenate([a["c_prompt"], a["c_sample"]])
    units = lambda *ws: np.stack([_by_columns(w) for w in ws], axis=1).reshape(-1, P, DK, P)
    return dict(
        x=np.concatenate([a["x_prompt"].reshape(SEQ, D), a["x_sample"].reshape(NS, D)]),
        cT=c_all.T.reshape(DK, P, -1).transpose(1, 0, 2),
        w_ada=a["w_ada"][0].reshape(DK, P, NMOD, 512).transpose(2, 1, 0, 3),
        b_ada=a["b_ada"][0],
        norms=np.stack([a["norm1"][0], a["norm2"][0]]),
        w_qkv=_chunks(w_in[:, :QKVW]),
        gain=np.concatenate([np.tile(a["q_norm"][0], NH), np.tile(a["k_norm"][0], NKV)]),
        sinks=a["attn_sinks"][0],
        sinks_s=np.repeat(a["attn_sinks"][0].reshape(NKV, GRP).T, DEC_T, axis=0),
        cache_k=a["cache_win_k"][0].reshape(DEC_B, WIN, KVW),
        cache_v=a["cache_win_v"][0].reshape(DEC_B, WIN, KVW),
        w_units=np.concatenate([units(part(4), part(5), part(6), part(7), part(3)), units(a["w_attn_o"][0], a["w_conv_o"][0])]),
        conv_wT=a["conv_w"][0].T.reshape(DK, P, 3).transpose(1, 0, 2),
        stateT=a["state_conv"][0].reshape(DEC_B, 2, DK, P).transpose(3, 2, 0, 1),
        w_out=_chunks(a["w_out"][0]),
        w_pq=_chunks(a["w_peer_q"][0]),
        subkT=a["peer_sub_keys"][0].reshape(2 * PH, NKEYS, PHALF).transpose(2, 0, 1),
        uv=np.concatenate([a["peer_u"][0], a["peer_v"][0]], axis=1),
    )


_OUTS = dict(y=(T, D), win_k_p=(P, KVW), win_v_p=(P, KVW), win_k_s=(DEC_B, WIN, KVW), win_v_s=(DEC_B, WIN, KVW),
             conv_new=(P, DK, 2 + 2 * DEC_B))


def kernel(**inputs):
    import concourse.bacc as _bacc
    from concourse.bass_utils import run_bass_kernel_spmd as _run

    nc = _bacc.Bacc("TRN2", target_bir_lowering=False, num_devices=1)
    arrays = {n: np.ascontiguousarray(v) for n, v in _layout({k: np.asarray(v) for k, v in inputs.items()}).items()}
    arrays.update({n: np.ascontiguousarray(v) for n, v in _constants().items()})
    ins = {n: nc.dram_tensor(f"in_{n}", v.shape, F32, kind="ExternalInput").ap() for n, v in arrays.items()}
    outs = {n: nc.dram_tensor(f"out_{n}", shape, F32, kind="ExternalOutput").ap() for n, shape in _OUTS.items()}
    build(nc, ins, outs)
    r = _run(nc, [{f"in_{n}": v for n, v in arrays.items()}], core_ids=[0]).results[0]
    y = r["out_y"]
    new = r["out_conv_new"]
    window = (1, 1, WIN, NKV, HD)
    windows = (1, DEC_B, WIN, NKV, HD)
    conv_p = new[:, :, 0:2].transpose(2, 1, 0).reshape(1, 1, 2, D)
    conv_s = new[:, :, 2:].reshape(P, DK, DEC_B, 2).transpose(2, 3, 1, 0).reshape(1, DEC_B, 2, D)
    return (y[:SEQ].reshape(1, SEQ, D), y[SEQ:].reshape(DEC_B, DEC_T, D),
            r["out_win_k_p"].reshape(window), r["out_win_v_p"].reshape(window), np.ascontiguousarray(conv_p),
            r["out_win_k_s"].reshape(windows), r["out_win_v_s"].reshape(windows), np.ascontiguousarray(conv_s))
```
